# Optimizing a Trainium2 kernel written in Bass

```python
import math
import jax
import jax.numpy as jnp
from jax import lax
import numpy as np
import jax, jax.numpy as jnp

D_MODEL = 1024
BATCH = 1
SEQ = 256
DEPTH = 2

HEAD_DIM = 64
N_Q_HEADS = 8
N_KV_HEADS = 2
GROUP = N_Q_HEADS // N_KV_HEADS
WINDOW = 128
ATTN_BLOCK = WINDOW
Q_WIDTH = N_Q_HEADS * HEAD_DIM
KV_WIDTH = N_KV_HEADS * HEAD_DIM
NUM_BUCKETS = 32
MAX_DISTANCE = 128
CONV_CHANNELS = D_MODEL // 2
CONV_WIDTH = 31
EVEN_IN = Q_WIDTH + 2 * KV_WIDTH + 2 * CONV_CHANNELS
EVEN_CAT = Q_WIDTH + CONV_CHANNELS
LRU_WIDTH = D_MODEL
LRU_HEADS = 8
LRU_BLOCK = LRU_WIDTH // LRU_HEADS
LRU_CONV_WIDTH = 4
RG_LRU_C = 8.0
D_FF = 2816
RMS_EPS = 1e-6
LN_EPS = 1e-5
NEG_INF = -1e30
N_EVEN = (DEPTH + 1) // 2
N_ODD = DEPTH // 2


def _rmsnorm(x, g):
    xf = x.astype(jnp.float32)
    y = xf * lax.rsqrt(jnp.mean(xf * xf, axis=-1, keepdims=True) + RMS_EPS)
    return (y * g.astype(jnp.float32)).astype(x.dtype)

def _layernorm(x, g, b):
    xf = x.astype(jnp.float32)
    mu = jnp.mean(xf, axis=-1, keepdims=True)
    var = jnp.mean(jnp.square(xf - mu), axis=-1, keepdims=True)
    y = (xf - mu) * lax.rsqrt(var + LN_EPS)
    return (y * g.astype(jnp.float32) + b.astype(jnp.float32)).astype(x.dtype)

def _swiglu(x, wg, wu, wd):
    return (jax.nn.silu(x @ wg) * (x @ wu)) @ wd

def _causal_depthwise_conv(x, w, b):
    k_width, chans = w.shape
    y = lax.conv_general_dilated(
        x, w[:, None, :].astype(x.dtype), window_strides=(1,),
        padding=[(k_width - 1, 0)], dimension_numbers=("NWC", "WIO", "NWC"),
        feature_group_count=chans)
    return y + b.astype(x.dtype)

def _t5_bucket(dist):
    n = jnp.maximum(dist, 0)
    max_exact = NUM_BUCKETS // 2
    nf = jnp.maximum(n, max_exact).astype(jnp.float32)
    large = max_exact + (jnp.log(nf / max_exact) / math.log(MAX_DISTANCE / max_exact)
                         * (NUM_BUCKETS - max_exact)).astype(jnp.int32)
    large = jnp.minimum(large, NUM_BUCKETS - 1)
    return jnp.where(n < max_exact, n, large)

def _swa_sink_attention(q, k, v, sinks, rel_bias):
    bsz, seq = q.shape[:2]
    nb = seq // ATTN_BLOCK
    qb = q.reshape(bsz, nb, ATTN_BLOCK, N_KV_HEADS, GROUP, HEAD_DIM)
    kb = k.reshape(bsz, nb, ATTN_BLOCK, N_KV_HEADS, HEAD_DIM)
    vb = v.reshape(bsz, nb, ATTN_BLOCK, N_KV_HEADS, HEAD_DIM)
    kk = jnp.concatenate([jnp.concatenate([jnp.zeros_like(kb[:, :1]), kb[:, :-1]], axis=1), kb], axis=2)
    vv = jnp.concatenate([jnp.concatenate([jnp.zeros_like(vb[:, :1]), vb[:, :-1]], axis=1), vb], axis=2)
    scores = jnp.einsum("bnqhgd,bnshd->bnhgqs", qb, kk,
                        preferred_element_type=jnp.float32) * (1.0 / math.sqrt(HEAD_DIM))
    qi = jnp.arange(ATTN_BLOCK)[:, None]
    sj = jnp.arange(2 * ATTN_BLOCK)[None, :]
    dist = qi + ATTN_BLOCK - sj
    bias = rel_bias.astype(jnp.float32)[_t5_bucket(dist)]
    bias = jnp.transpose(bias, (2, 0, 1)).reshape(N_KV_HEADS, GROUP, ATTN_BLOCK, 2 * ATTN_BLOCK)
    in_window = (dist >= 0) & (dist < WINDOW)
    key_pos = jnp.arange(nb)[:, None, None] * ATTN_BLOCK + sj[None] - ATTN_BLOCK
    mask = in_window[None] & (key_pos >= 0)
    scores = jnp.where(mask[None, :, None, None], scores + bias[None, None], NEG_INF)
    sink = sinks.astype(jnp.float32).reshape(N_KV_HEADS, GROUP)[None, None, :, :, None, None]
    sink = jnp.broadcast_to(sink, scores.shape[:-1] + (1,))
    probs = jax.nn.softmax(jnp.concatenate([scores, sink], axis=-1), axis=-1)[..., :-1]
    out = jnp.einsum("bnhgqs,bnshd->bnqhgd", probs.astype(v.dtype), vv)
    return out.reshape(bsz, seq, Q_WIDTH)

def _attn_conv_mixer(h, w_in, sinks, conv_w, conv_b, ln_g, ln_b, w_out, rel_bias):
    bsz, seq, _ = h.shape
    u = h @ w_in
    o1 = Q_WIDTH
    o2 = o1 + KV_WIDTH
    o3 = o2 + KV_WIDTH
    o4 = o3 + CONV_CHANNELS
    q = u[..., :o1].reshape(bsz, seq, N_Q_HEADS, HEAD_DIM)
    k = u[..., o1:o2].reshape(bsz, seq, N_KV_HEADS, HEAD_DIM)
    v = u[..., o2:o3].reshape(bsz, seq, N_KV_HEADS, HEAD_DIM)
    attn = _swa_sink_attention(q, k, v, sinks, rel_bias)
    glu = u[..., o3:o4] * jax.nn.sigmoid(u[..., o4:])
    c = jax.nn.silu(_layernorm(_causal_depthwise_conv(glu, conv_w, conv_b), ln_g, ln_b))
    return jnp.concatenate([attn, c], axis=-1) @ w_out

def _rg_lru(x, ga_w, ga_b, gx_w, gx_b, lam):
    bsz, seq, width = x.shape
    xh = x.reshape(bsz, seq, LRU_HEADS, LRU_BLOCK)
    r = jax.nn.sigmoid(jnp.einsum("bshi,hij->bshj", xh, ga_w).reshape(bsz, seq, width) + ga_b)
    i = jax.nn.sigmoid(jnp.einsum("bshi,hij->bshj", xh, gx_w).reshape(bsz, seq, width) + gx_b)
    log_a = RG_LRU_C * r.astype(jnp.float32) * jax.nn.log_sigmoid(lam.astype(jnp.float32))
    a = jnp.exp(log_a)
    bx = jnp.sqrt(-jnp.expm1(2.0 * log_a)) * (i * x).astype(jnp.float32)

    def combine(left, right):
        a1, b1 = left
        a2, b2 = right
        return a1 * a2, a2 * b1 + b2

    _, hs = lax.associative_scan(combine, (a, bx), axis=1)
    return hs.astype(x.dtype)

def _recurrent_mixer(h, w_in, conv_w, conv_b, ga_w, ga_b, gx_w, gx_b, lam, w_out):
    u = h @ w_in
    gate = jax.nn.gelu(u[..., :LRU_WIDTH])
    rec = _causal_depthwise_conv(u[..., LRU_WIDTH:], conv_w, conv_b)
    rec = _rg_lru(rec, ga_w, ga_b, gx_w, gx_b, lam)
    return (gate * rec) @ w_out

def first_inputs(seed: int = 0) -> dict:
    key = jax.random.key(seed)
    ks = iter(jax.random.split(key, 40))

    def nrm(shape, scale):
        return jax.random.normal(next(ks), shape, jnp.float32) * scale

    def gain(shape):
        return 1.0 + nrm(shape, 0.02)

    x = nrm((BATCH, SEQ, D_MODEL), 1.0)
    u = jax.random.uniform(next(ks), (N_ODD, LRU_WIDTH), jnp.float32, 0.9, 0.999)
    a0 = u ** (1.0 / RG_LRU_C)
    lru_lambda = jnp.log(a0) - jnp.log1p(-a0)
    return {
        "x": x,
        "norm_ffn1": gain((DEPTH, D_MODEL)),
        "ffn1_wg": nrm((DEPTH, D_MODEL, D_FF), D_MODEL ** -0.5),
        "ffn1_wu": nrm((DEPTH, D_MODEL, D_FF), D_MODEL ** -0.5),
        "ffn1_wd": nrm((DEPTH, D_FF, D_MODEL), D_FF ** -0.5),
        "norm_mix": gain((DEPTH, D_MODEL)),
        "norm_ffn2": gain((DEPTH, D_MODEL)),
        "ffn2_wg": nrm((DEPTH, D_MODEL, D_FF), D_MODEL ** -0.5),
        "ffn2_wu": nrm((DEPTH, D_MODEL, D_FF), D_MODEL ** -0.5),
        "ffn2_wd": nrm((DEPTH, D_FF, D_MODEL), D_FF ** -0.5),
        "rel_bias": nrm((NUM_BUCKETS, N_Q_HEADS), 0.3),
        "even_w_in": nrm((N_EVEN, D_MODEL, EVEN_IN), D_MODEL ** -0.5),
        "attn_sinks": nrm((N_EVEN, N_Q_HEADS), 1.0),
        "conv_b_w": nrm((N_EVEN, CONV_WIDTH, CONV_CHANNELS), CONV_WIDTH ** -0.5),
        "conv_b_b": nrm((N_EVEN, CONV_CHANNELS), 0.02),
        "conv_ln_g": gain((N_EVEN, CONV_CHANNELS)),
        "conv_ln_b": nrm((N_EVEN, CONV_CHANNELS), 0.02),
        "even_w_out": nrm((N_EVEN, EVEN_CAT, D_MODEL), EVEN_CAT ** -0.5),
        "odd_w_in": nrm((N_ODD, D_MODEL, 2 * LRU_WIDTH), D_MODEL ** -0.5),
        "lru_conv_w": nrm((N_ODD, LRU_CONV_WIDTH, LRU_WIDTH), LRU_CONV_WIDTH ** -0.5),
        "lru_conv_b": nrm((N_ODD, LRU_WIDTH), 0.02),
        "gate_a_w": nrm((N_ODD, LRU_HEADS, LRU_BLOCK, LRU_BLOCK), LRU_BLOCK ** -0.5),
        "gate_a_b": nrm((N_ODD, LRU_WIDTH), 0.02),
        "gate_x_w": nrm((N_ODD, LRU_HEADS, LRU_BLOCK, LRU_BLOCK), LRU_BLOCK ** -0.5),
        "gate_x_b": nrm((N_ODD, LRU_WIDTH), 0.02),
        "lru_lambda": lru_lambda,
        "odd_w_out": nrm((N_ODD, LRU_WIDTH, D_MODEL), LRU_WIDTH ** -0.5),
        "norm_final": gain((D_MODEL,)),
    }

def first_block(x, norm_ffn1, ffn1_wg, ffn1_wu, ffn1_wd, norm_mix, norm_ffn2, ffn2_wg, ffn2_wu, ffn2_wd,
              rel_bias, even_w_in, attn_sinks, conv_b_w, conv_b_b, conv_ln_g, conv_ln_b, even_w_out,
              odd_w_in, lru_conv_w, lru_conv_b, gate_a_w, gate_a_b, gate_x_w, gate_x_b, lru_lambda,
              odd_w_out, norm_final):
    h = x
    for layer in range(DEPTH):
        h = h + 0.5 * _swiglu(_rmsnorm(h, norm_ffn1[layer]), ffn1_wg[layer], ffn1_wu[layer], ffn1_wd[layer])
        hn = _rmsnorm(h, norm_mix[layer])
        if layer % 2 == 0:
            e = layer // 2
            h = h + _attn_conv_mixer(hn, even_w_in[e], attn_sinks[e], conv_b_w[e], conv_b_b[e],
                                     conv_ln_g[e], conv_ln_b[e], even_w_out[e], rel_bias)
        else:
            o = layer // 2
            h = h + _recurrent_mixer(hn, odd_w_in[o], lru_conv_w[o], lru_conv_b[o], gate_a_w[o],
                                     gate_a_b[o], gate_x_w[o], gate_x_b[o], lru_lambda[o], odd_w_out[o])
        h = h + 0.5 * _swiglu(_rmsnorm(h, norm_ffn2[layer]), ffn2_wg[layer], ffn2_wu[layer], ffn2_wd[layer])
    return _rmsnorm(h, norm_final)


CHUNK = 64
Q_BLOCK = 128
SB_HEADS = 4
MLA_HEADS = 8
MLA_Q_RANK = 256
MLA_KV_RANK = 128
MLA_NOPE = 64
MLA_ROPE = 32
MLA_V = 64
ROPE_THETA = 10000.0
CK_HEADS = 4
CK_LEFT_CHUNKS = 8
REL_CLIP = 128

D_SB = SB_HEADS * HEAD_DIM
D_MLA = MLA_HEADS * MLA_V
D_CK = CK_HEADS * HEAD_DIM
D_MIX = D_SB + D_MLA + D_CK
IN_SIZES = (D_SB, D_SB, D_SB, MLA_Q_RANK, MLA_KV_RANK, MLA_ROPE, D_CK, D_CK, D_CK)
IN_COLS = sum(IN_SIZES)
IN_SPLITS = tuple(int(v) for v in np.cumsum(IN_SIZES)[:-1])
GROUP_SPLITS = (D_SB, D_SB + D_MLA)

N_EXPERTS = 8
TOP_K = 2
N_DENSE = (DEPTH + 1) // 2
N_MOE = DEPTH // 2
EPS = 1e-6
NEG = -1e30


def _rms_norm(x, g):
    xf = x.astype(jnp.float32)
    y = xf * lax.rsqrt(jnp.mean(xf * xf, axis=-1, keepdims=True) + EPS)
    return (y * g.astype(jnp.float32)).astype(x.dtype)

def _rope(x, cos, sin):
    half = x.shape[-1] // 2
    x1, x2 = x[..., :half], x[..., half:]
    return jnp.concatenate([x1 * cos - x2 * sin, x2 * cos + x1 * sin], axis=-1)

def _stick_breaking(q, k, v):
    S, Dh = q.shape[1], q.shape[-1]
    scale = Dh ** -0.5
    outs = []
    for i in range(S // Q_BLOCK):
        q0, q1 = i * Q_BLOCK, (i + 1) * Q_BLOCK
        z = jnp.einsum('bqhd,bkhd->bhqk', q[:, q0:q1], k[:, :q1]).astype(jnp.float32) * scale
        tq = q0 + jnp.arange(Q_BLOCK)
        tk = jnp.arange(q1)
        strict = tk[None, :] < tq[:, None]
        log_1mb = jnp.where(strict, jax.nn.log_sigmoid(-z), 0.0)
        tail = lax.cumsum(log_1mb, axis=3, reverse=True) - log_1mb
        w = jnp.where(strict, jnp.exp(jax.nn.log_sigmoid(z) + tail), 0.0)
        outs.append(jnp.einsum('bhqk,bkhd->bqhd', w.astype(v.dtype), v[:, :q1]))
    return jnp.concatenate(outs, axis=1)

def _chunk_causal_attention(q, k, v, scale):
    S = q.shape[1]
    outs = []
    for i in range(S // Q_BLOCK):
        q0, q1 = i * Q_BLOCK, (i + 1) * Q_BLOCK
        s = jnp.einsum('bqhd,bkhd->bhqk', q[:, q0:q1], k[:, :q1]).astype(jnp.float32) * scale
        tq = q0 + jnp.arange(Q_BLOCK)
        tk = jnp.arange(q1)
        allowed = (tk[None, :] // CHUNK) <= (tq[:, None] // CHUNK)
        p = jax.nn.softmax(jnp.where(allowed, s, NEG), axis=-1)
        outs.append(jnp.einsum('bhqk,bkhd->bqhd', p.astype(v.dtype), v[:, :q1]))
    return jnp.concatenate(outs, axis=1)

def _chunked_band_attention(q, k, v, rel_bias):
    B, S, H, Dh = q.shape
    NC = S // CHUNK
    W = CK_LEFT_CHUNKS + 1
    qc = q.reshape(B, NC, CHUNK, H, Dh)
    pad = ((0, 0), (CK_LEFT_CHUNKS * CHUNK, 0), (0, 0), (0, 0))
    kp = jnp.pad(k, pad).reshape(B, NC + CK_LEFT_CHUNKS, CHUNK, H, Dh)
    vp = jnp.pad(v, pad).reshape(B, NC + CK_LEFT_CHUNKS, CHUNK, H, Dh)
    band = jnp.arange(NC)[:, None] + jnp.arange(W)[None, :]
    kb = kp[:, band].reshape(B, NC, W * CHUNK, H, Dh)
    vb = vp[:, band].reshape(B, NC, W * CHUNK, H, Dh)
    s = jnp.einsum('bnqhd,bnkhd->bnhqk', qc, kb).astype(jnp.float32) * (Dh ** -0.5)
    q_pos = jnp.arange(CHUNK) + CK_LEFT_CHUNKS * CHUNK
    k_pos = jnp.arange(W * CHUNK)
    rel = jnp.clip(q_pos[:, None] - k_pos[None, :], -REL_CLIP, REL_CLIP) + REL_CLIP
    bias = rel_bias.astype(jnp.float32)[:, rel]
    key_chunk = jnp.arange(NC)[:, None] + (k_pos // CHUNK)[None, :] - CK_LEFT_CHUNKS
    valid = (key_chunk >= 0)[None, :, None, None, :]
    p = jax.nn.softmax(jnp.where(valid, s + bias[None, None], NEG), axis=-1)
    o = jnp.einsum('bnhqk,bnkhd->bnqhd', p.astype(v.dtype), vb)
    return o.reshape(B, S, H, Dh)

def _mixer(h, cos, sin, w_in, mla_q_norm, w_q_up, mla_kv_norm, w_kv_up, mla_q_qknorm,
           mla_k_qknorm, ck_q_qknorm, ck_k_qknorm, ck_rel_bias, group_out_norm, w_out):
    B, S, _ = h.shape
    proj = h @ w_in
    sb_q, sb_k, sb_v, cq, ckv, k_pe, ck_q, ck_k, ck_v = jnp.split(proj, IN_SPLITS, axis=-1)

    hd = lambda t, n: t.reshape(B, S, n, -1)
    o_sb = _stick_breaking(hd(sb_q, SB_HEADS), hd(sb_k, SB_HEADS), hd(sb_v, SB_HEADS))

    q = (_rms_norm(cq, mla_q_norm) @ w_q_up).reshape(B, S, MLA_HEADS, MLA_NOPE + MLA_ROPE)
    q = jnp.concatenate([q[..., :MLA_NOPE], _rope(q[..., MLA_NOPE:], cos, sin)], axis=-1)
    kv = (_rms_norm(ckv, mla_kv_norm) @ w_kv_up).reshape(B, S, MLA_HEADS, MLA_NOPE + MLA_V)
    k_pe = _rope(k_pe[:, :, None, :], cos, sin)
    k = jnp.concatenate([kv[..., :MLA_NOPE],
                         jnp.broadcast_to(k_pe, (B, S, MLA_HEADS, MLA_ROPE))], axis=-1)
    q = _rms_norm(q, mla_q_qknorm)
    k = _rms_norm(k, mla_k_qknorm)
    o_mla = _chunk_causal_attention(q, k, kv[..., MLA_NOPE:], (MLA_NOPE + MLA_ROPE) ** -0.5)

    o_ck = _chunked_band_attention(_rms_norm(hd(ck_q, CK_HEADS), ck_q_qknorm),
                                   _rms_norm(hd(ck_k, CK_HEADS), ck_k_qknorm),
                                   hd(ck_v, CK_HEADS), ck_rel_bias)

    g_sb, g_mla, g_ck = jnp.split(group_out_norm, GROUP_SPLITS)
    merged = jnp.concatenate([_rms_norm(o_sb.reshape(B, S, D_SB), g_sb),
                              _rms_norm(o_mla.reshape(B, S, D_MLA), g_mla),
                              _rms_norm(o_ck.reshape(B, S, D_CK), g_ck)], axis=-1)
    return merged @ w_out

def _swiglu_2(h, w_gate, w_up, w_down):
    return (jax.nn.silu(h @ w_gate) * (h @ w_up)) @ w_down

def _moe(h, w_router, w_gate, w_up, w_down):
    logits = (h @ w_router).astype(jnp.float32)
    top_val, top_idx = lax.top_k(logits, TOP_K)
    top_w = jax.nn.softmax(top_val, axis=-1)
    gates = jnp.sum(jax.nn.one_hot(top_idx, N_EXPERTS, dtype=jnp.float32) * top_w[..., None], axis=-2)
    gates = gates.astype(h.dtype)
    out = jnp.zeros_like(h)
    for e in range(N_EXPERTS):
        out = out + gates[..., e:e + 1] * _swiglu_2(h, w_gate[e], w_up[e], w_down[e])
    return out

def second_inputs(seed: int = 0) -> dict:
    key = jax.random.key(seed)
    ks = iter(jax.random.split(key, 32))
    f32 = jnp.float32

    def w(shape, fan_in, mult=1.0):
        return jax.random.normal(next(ks), shape, f32) * (mult * fan_in ** -0.5)

    def gain(shape):
        return 1.0 + 0.1 * jax.random.normal(next(ks), shape, f32)

    x = jax.random.normal(next(ks), (BATCH, SEQ, D_MODEL), f32)
    c = jax.random.normal(next(ks), (BATCH, D_MODEL), f32)
    offsets = jax.random.randint(next(ks), (BATCH, 1), 0, 4096, dtype=jnp.int32)
    positions = (offsets + jnp.arange(SEQ, dtype=jnp.int32)[None, :]).astype(jnp.int32)
    return {
        "x": x,
        "c": c,
        "positions": positions,
        "ada_w": w((DEPTH, D_MODEL, 6 * D_MODEL), D_MODEL, 0.5),
        "ada_b": 0.02 * jax.random.normal(next(ks), (DEPTH, 6 * D_MODEL), f32),
        "norm_mix": gain((DEPTH, D_MODEL)),
        "norm_ffn": gain((DEPTH, D_MODEL)),
        "w_in": w((DEPTH, D_MODEL, IN_COLS), D_MODEL),
        "mla_q_norm": gain((DEPTH, MLA_Q_RANK)),
        "w_q_up": w((DEPTH, MLA_Q_RANK, MLA_HEADS * (MLA_NOPE + MLA_ROPE)), MLA_Q_RANK),
        "mla_kv_norm": gain((DEPTH, MLA_KV_RANK)),
        "w_kv_up": w((DEPTH, MLA_KV_RANK, MLA_HEADS * (MLA_NOPE + MLA_V)), MLA_KV_RANK),
        "mla_q_qknorm": gain((DEPTH, MLA_NOPE + MLA_ROPE)),
        "mla_k_qknorm": gain((DEPTH, MLA_NOPE + MLA_ROPE)),
        "ck_q_qknorm": gain((DEPTH, HEAD_DIM)),
        "ck_k_qknorm": gain((DEPTH, HEAD_DIM)),
        "ck_rel_bias": 0.5 * jax.random.normal(next(ks), (DEPTH, CK_HEADS, 2 * REL_CLIP + 1), f32),
        "group_out_norm": gain((DEPTH, D_MIX)),
        "w_out": w((DEPTH, D_MIX, D_MODEL), D_MIX),
        "ffn_w_gate": w((N_DENSE, D_MODEL, D_FF), D_MODEL),
        "ffn_w_up": w((N_DENSE, D_MODEL, D_FF), D_MODEL),
        "ffn_w_down": w((N_DENSE, D_FF, D_MODEL), D_FF),
        "moe_router": w((N_MOE, D_MODEL, N_EXPERTS), D_MODEL),
        "moe_w_gate": w((N_MOE, N_EXPERTS, D_MODEL, D_FF), D_MODEL),
        "moe_w_up": w((N_MOE, N_EXPERTS, D_MODEL, D_FF), D_MODEL),
        "moe_w_down": w((N_MOE, N_EXPERTS, D_FF, D_MODEL), D_FF),
    }

def second_block(x, c, positions, ada_w, ada_b, norm_mix, norm_ffn, w_in, mla_q_norm, w_q_up,
              mla_kv_norm, w_kv_up, mla_q_qknorm, mla_k_qknorm, ck_q_qknorm, ck_k_qknorm,
              ck_rel_bias, group_out_norm, w_out, ffn_w_gate, ffn_w_up, ffn_w_down,
              moe_router, moe_w_gate, moe_w_up, moe_w_down):
    inv_freq = ROPE_THETA ** (-jnp.arange(0, MLA_ROPE, 2, dtype=jnp.float32) / MLA_ROPE)
    ang = positions.astype(jnp.float32)[..., None] * inv_freq
    cos = jnp.cos(ang)[:, :, None, :].astype(x.dtype)
    sin = jnp.sin(ang)[:, :, None, :].astype(x.dtype)
    c_act = jax.nn.silu(c)
    for layer in range(DEPTH):
        mod = c_act @ ada_w[layer] + ada_b[layer]
        sh1, sc1, g1, sh2, sc2, g2 = [m[:, None, :] for m in jnp.split(mod, 6, axis=-1)]
        h = _rms_norm(x, norm_mix[layer]) * (1.0 + sc1) + sh1
        x = x + g1 * _mixer(h, cos, sin, w_in[layer], mla_q_norm[layer], w_q_up[layer],
                            mla_kv_norm[layer], w_kv_up[layer], mla_q_qknorm[layer],
                            mla_k_qknorm[layer], ck_q_qknorm[layer], ck_k_qknorm[layer],
                            ck_rel_bias[layer], group_out_norm[layer], w_out[layer])
        h = _rms_norm(x, norm_ffn[layer]) * (1.0 + sc2) + sh2
        i = layer // 2
        if layer % 2 == 0:
            y = _swiglu_2(h, ffn_w_gate[i], ffn_w_up[i], ffn_w_down[i])
        else:
            y = _moe(h, moe_router[i], moe_w_gate[i], moe_w_up[i], moe_w_down[i])
        x = x + g2 * y
    return x


def setup_inputs(seed=0):
    out = dict(first_inputs(seed))
    for name, value in second_inputs(seed + 1).items():
        if name != "x":
            out[name + "_2"] = value
    return out


def reference(
    x, norm_ffn1, ffn1_wg, ffn1_wu, ffn1_wd, norm_mix, norm_ffn2, ffn2_wg, ffn2_wu, ffn2_wd,
    rel_bias, even_w_in, attn_sinks, conv_b_w, conv_b_b, conv_ln_g, conv_ln_b, even_w_out,
    odd_w_in, lru_conv_w, lru_conv_b, gate_a_w, gate_a_b, gate_x_w, gate_x_b, lru_lambda,
    odd_w_out, norm_final, c_2, positions_2, ada_w_2, ada_b_2, norm_mix_2, norm_ffn_2, w_in_2,
    mla_q_norm_2, w_q_up_2, mla_kv_norm_2, w_kv_up_2, mla_q_qknorm_2, mla_k_qknorm_2,
    ck_q_qknorm_2, ck_k_qknorm_2, ck_rel_bias_2, group_out_norm_2, w_out_2, ffn_w_gate_2,
    ffn_w_up_2, ffn_w_down_2, moe_router_2, moe_w_gate_2, moe_w_up_2, moe_w_down_2,
):
    x = first_block(
        x, norm_ffn1, ffn1_wg, ffn1_wu, ffn1_wd, norm_mix, norm_ffn2, ffn2_wg, ffn2_wu, ffn2_wd,
        rel_bias, even_w_in, attn_sinks, conv_b_w, conv_b_b, conv_ln_g, conv_ln_b, even_w_out,
        odd_w_in, lru_conv_w, lru_conv_b, gate_a_w, gate_a_b, gate_x_w, gate_x_b, lru_lambda,
        odd_w_out, norm_final,
    )
    return second_block(
        x, c_2, positions_2, ada_w_2, ada_b_2, norm_mix_2, norm_ffn_2, w_in_2, mla_q_norm_2,
        w_q_up_2, mla_kv_norm_2, w_kv_up_2, mla_q_qknorm_2, mla_k_qknorm_2, ck_q_qknorm_2,
        ck_k_qknorm_2, ck_rel_bias_2, group_out_norm_2, w_out_2, ffn_w_gate_2, ffn_w_up_2,
        ffn_w_down_2, moe_router_2, moe_w_gate_2, moe_w_up_2, moe_w_down_2,
    )


_drawn_inputs = setup_inputs


def setup_inputs(seed=0):
    import zlib

    import numpy as np

    out = dict(_drawn_inputs(seed))
    spreads = {}
    factors = {'norm_ffn1': 2.808,
     'norm_mix': 2.686,
     'norm_ffn2': 3.775,
     'attn_sinks': 5.114,
     'conv_ln_g': 3.293,
     'conv_ln_b': 3.085,
     'gate_a_b': 8.0,
     'gate_x_b': 8.0,
     'mla_q_norm_2': 3.516,
     'mla_q_qknorm_2': 3.322,
     'mla_k_qknorm_2': 3.283,
     'ck_q_qknorm_2': 3.94,
     'ck_k_qknorm_2': 6.697}
    for name, (base, spread) in spreads.items():
        noise = np.random.default_rng([zlib.crc32(name.encode()), seed]).standard_normal(out[name].shape)
        drawn = base * np.exp(spread * noise) if base else spread * noise
        out[name] = jnp.asarray(drawn.astype(out[name].dtype))
    for name, factor in factors.items():
        out[name] = (out[name] * factor).astype(out[name].dtype)
    return out
```

```python
from contextlib import ExitStack, contextmanager

import numpy as np
import concourse.bass as bass
from concourse import mybir

F32 = mybir.dt.float32
F32R = mybir.dt.float32r
I32 = mybir.dt.int32
ALU = mybir.AluOpType
ACT = mybir.ActivationFunctionType
AX = mybir.AxisListType

P = 128
S = 256
NT = S // P
D = 1024
KT = D // P
FF = 2816
FC = 256
STEPS = FF // FC
N_EXPERTS = 8
NEG = -1e30
PIECE = 2048
N_RAW = 3
N_HL = 6
AHEAD = 3
LOOK = 255
TOEP = 384

XN = 4096
SIL, PROD, YACC, GATES = 6144, 6656, 7168, 9216
TMP4 = 6144
MOD, GATE_IN, GAIN_AT, TMP = 8192, 10240, 11264, 12288
ROUTE = 11264
SCORES, PROBT = 11264, 12032
ROWS_AT, REL_AT, ONEHOT_AT, CKROW_AT, REV_AT, CKOUT_AT = 8192, 8576, 8704, 9088, 9472, 9856
INVF_AT, ANG_AT, LAM_AT = 10240, 10304, 10496
E_GP, E_KV, E_SQ, E_STD, E_CONV, E_QT, E_BIAS = 4096, 5240, 6144, 6400, 7168, 8192, 9216
O_REC, O_GATE, O_XC, O_R, TMP2 = 4096, 6168, 8216, 10264, 12312
M_QTOK, M_KTOK, M_VTOK, M_QKT, M_OT, M_BIAS = 0, 1536, 3072, 4096, 8192, 10240
M_SB, M_CK = 0, 1536
STICK = 4096

COLUMN_SIZES = (("norm_ffn1", 16), ("norm_mix", 16), ("norm_ffn2", 16), ("conv_b_b", 4), ("conv_ln_g", 4),
                    ("conv_ln_b", 4), ("lru_conv_b", 8), ("gate_a_b", 8), ("gate_x_b", 8), ("lru_lambda", 8),
                    ("lru_conv_w", 32), ("conv_b_w", 124), ("norm_mix_2", 16), ("norm_ffn_2", 16),
                    ("mla_q_norm_2", 4), ("mla_kv_norm_2", 2), ("group_out_norm_2", 16),
                    ("ck_q_qknorm_2", 2), ("ck_k_qknorm_2", 2), ("c_2", 8))
COLS = {name: sum(n for _, n in COLUMN_SIZES[:i]) for i, (name, _) in enumerate(COLUMN_SIZES)}
N_COLS = sum(n for _, n in COLUMN_SIZES)
ROW_TILES = (("norm_ffn1", "norm_mix", "norm_ffn2", "conv_b_b", "conv_ln_g", "conv_ln_b", "lru_conv_b",
              "gate_a_b", "gate_x_b", "lru_lambda", "lru_conv_w"),
             ("conv_b_w",),
             ("norm_mix_2", "norm_ffn_2", "mla_q_norm_2", "mla_kv_norm_2", "group_out_norm_2",
              "ck_q_qknorm_2", "ck_k_qknorm_2", "c_2"))


class Semaphores:

    def __init__(self, nc, ctx):
        self.nc, self.ctx, self.by_name = nc, ctx, {}

    def __getitem__(self, name):
        if name not in self.by_name:
            self.by_name[name] = self.ctx.enter_context(self.nc.semaphore(name))
        return self.by_name[name]


class Engine:

    def __init__(self, queue, sem, name):
        self.q, self.sem, self.own = queue, sem, "own_" + name
        self.seen = {}
        self.it, self.per = None, {}

    def next(self, name, n=1):
        self.seen[name] = self.seen.get(name, 0) + n
        per = self.per.get(name, 0)
        assert self.it is None or per, name
        return self.at(self.seen[name], per)

    def following(self, name):
        return self.seen.get(name, 0) + 1

    def at(self, value, per):
        assert value > 0
        return value if self.it is None or not per else self.it * per + value

    def link(self, instruction):
        instruction.then_inc(self.sem[self.own], 1)
        self.q.wait_ge(self.sem[self.own], self.next(self.own))

    @contextmanager
    def loop(self, iterations, per):
        before = dict(self.seen)
        with self.q.Fori(0, iterations) as it:
            self.it, self.per = it, per
            yield it
        self.it, self.per = None, {}
        for name, n in per.items():
            assert self.seen.get(name, 0) - before.get(name, 0) == n, name
            self.seen[name] += n * (iterations - 1)


def layout(nc, ctx):
    class M:
        pass
    m = M()

    def sb(name, free, dt=F32):
        t = ctx.enter_context(nc.sbuf_tensor(name, [P, free], dt))
        return t

    m.raw = sb("w_raw", N_RAW * PIECE)
    m.whi = sb("w_hi", N_HL * PIECE, F32R)
    m.wlo = sb("w_lo", N_HL * PIECE, F32R)
    m.x = sb("x_resid", NT * D)[:, :].rearrange("p (t d) -> p t d", t=NT)
    m.hhi = sb("h_hi", KT * S, F32R)[:, :].rearrange("p (k s) -> p k s", k=KT)
    m.hlo = sb("h_lo", KT * S, F32R)[:, :].rearrange("p (k s) -> p k s", k=KT)
    m.ahi = sb("act_hi", 4 * S, F32R)[:, :].rearrange("p (f s) -> p f s", f=4)
    m.alo = sb("act_lo", 4 * S, F32R)[:, :].rearrange("p (f s) -> p f s", f=4)
    m.ident = sb("ident", P)
    m.ones = sb("ones", P)
    m.cols = sb("cols", N_COLS)
    m.strict = sb("strict", P)
    m.blocks = sb("blocks", P)
    m.small = sb("small", 176)
    m.pos = sb("positions", NT, I32)
    m.rope = sb("rope_cs", 2 * NT * 16)[:, :].rearrange("p (c t f) -> p c t f", c=2, t=NT)
    m.qkgain = sb("qk_gain", 2 * 96)[:, :].rearrange("p (c f) -> p c f", c=2)
    m.arena = sb("arena", ARENA)
    m.banks = [ctx.enter_context(nc.psum_tensor(f"bank{i}", [P, 512], F32)) for i in range(8)]
    return m


ARENA = 12800


def take_view(m, at, n, pattern=None, **sizes):
    v = m.arena[:, at:at + n]
    return v if pattern is None else v.rearrange(pattern, **sizes)


def small(m, at, n=1):
    return m.small[:, at:at + n]


SS, STD, RSTD, EPS6, EPS5, CACT, SINK, HALF_PI = 0, 2, 4, 6, 7, 8, 16, 24
NM, DEN, ES, RDEN, MX = 26, 30, 34, 38, 42
SHC, GSC, LRUC = 48, 56, 64
SSQ, RSQ, TRI = 80, 96, 112
POOL_CONSTS = 8
ROWS_LOADS = len(COLUMN_SIZES) + 2



def ffn_order(n):
    out = [("gate", 0), ("up", 0)]
    for s in range(n - 1):
        out += [("gate", s + 1), ("up", s + 1), ("down", s)]
    return out + [("down", n - 1)]


def stream(a):
    pieces = []

    def columns(w, c, n=FC, at=0):
        kt = w.shape[0] // P
        src = w.rearrange("(k p) n -> p k n", p=P)[:, :, c:c + n]
        return lambda raw: raw[:, at:at + kt * n].rearrange("p (k n) -> p k n", k=kt), src

    def rows(w, r):
        src = w[r:r + 2 * P, :].rearrange("(k p) n -> p k n", p=P)
        return lambda raw: raw.rearrange("p (k n) -> p k n", k=2), src

    def head_columns(w, h, j):
        src = w.rearrange("(k p) n -> p k n", p=P)[:, :, 64 * h:64 * h + 64]
        return lambda raw: raw.rearrange("p (k n) -> p k n", k=KT)[:, :, 64 * j:64 * j + 64], src

    def head_rows(w, h, kt, half):
        return lambda raw: raw[64 * half:64 * half + 64, kt * D:(kt + 1) * D], w[64 * h:64 * h + 64, :]

    def gates(w, at):
        return lambda raw: raw[:, at:at + D].rearrange("p (h j) -> p h j", h=8), w.rearrange("h i j -> i h j")

    def ffn(tag, n):
        for kind, s in ffn_order(n):
            pieces.append((tag, kind, s))

    def plain(*loads):
        pieces.append(("plain", list(loads), None))

    ffn("ffn1_0", STEPS)
    w = a["even_w_in"][0]
    for i in range(2):
        plain(columns(w, 768 + FC * i))
        plain(columns(w, 1280 + FC * i))
    plain(columns(w, 512))
    for i in range(2):
        plain(*[head_columns(w, h, j) for j, h in enumerate((2 * i, 2 * i + 4, 2 * i + 1, 2 * i + 5))])
    w = a["even_w_out"][0]
    for i in range(2):
        plain(*[head_rows(w, 2 * i + kt + 4 * half, kt, half) for kt in range(2) for half in range(2)])
    for i in range(2):
        plain(rows(w, 512 + 256 * i))
    ffn("ffn2_0", STEPS)
    ffn("ffn1_1", STEPS)
    w = a["odd_w_in"][0]
    for i in range(4):
        plain(columns(w, D + FC * i))
    for i in range(4):
        plain(columns(w, FC * i))
    plain(gates(a["gate_a_w"][0], 0), gates(a["gate_x_w"][0], D))
    for i in range(4):
        plain(rows(a["odd_w_out"][0], 256 * i))
    ffn("ffn2_1", STEPS)
    for layer in range(2):
        w = a["w_in_2"][layer]
        plain(columns(w, 768))
        plain(columns(w, 1024, 160))
        plain(columns(a["w_q_up_2"][layer], 0, 768))
        plain(columns(a["w_kv_up_2"][layer], 0, D))
        for c in (0, 256, 512, 1184, 1440, 1696):
            plain(columns(w, c))
        for i in range(4):
            plain(rows(a["w_out_2"][layer], 256 * i))
        if layer == 0:
            ffn("dense", STEPS)
        else:
            plain(columns(a["moe_router_2"][0], 0, N_EXPERTS))
            ffn("moe", N_EXPERTS * STEPS)
    return pieces


def arrivals(pieces):
    at, out = [0] * N_RAW, []
    for n, piece in enumerate(pieces):
        at[n % N_RAW] += 16 * (len(piece[1]) if piece[0] == "plain" else 1)
        out.append(at[n % N_RAW])
    return out



class Split:

    def __init__(self, eng, m, arrive):
        self.e, self.m, self.arrive, self.n = eng, m, arrive, 0

    def next_hi(self, nc):
        n, m, e = self.n, self.m, self.e
        if n >= len(self.arrive):
            return
        e.q.wait_ge(e.sem[f"raw_filled{n % N_RAW}"], e.at(self.arrive[n], 16 * (6 // N_RAW)))
        if n >= N_HL:
            e.q.wait_ge(e.sem["piece_used"], e.at(n - N_HL + 1, 6))
        raw = m.raw[:, n % N_RAW * PIECE:(n % N_RAW + 1) * PIECE]
        hi = m.whi[:, n % N_HL * PIECE:(n % N_HL + 1) * PIECE]
        nc.scalar.activation(hi, raw, ACT.Copy).then_inc(e.sem["piece_hi"], 1)
        self.n += 1

    def next_lo(self, nc):
        n, m, e = self.n, self.m, self.e
        if n >= len(self.arrive):
            return
        e.q.wait_ge(e.sem["piece_hi"], e.at(n + 1, 6))
        raw = m.raw[:, n % N_RAW * PIECE:(n % N_RAW + 1) * PIECE]
        hi = m.whi[:, n % N_HL * PIECE:(n % N_HL + 1) * PIECE]
        lo = m.wlo[:, n % N_HL * PIECE:(n % N_HL + 1) * PIECE]
        nc.vector.tensor_tensor(lo, raw, hi.bitcast(F32), ALU.subtract).then_inc(e.sem["piece_lo"], 1)
        self.n += 1


def build(nc, a, out, consts):
    x_in = a["x"][0].rearrange("(t p) d -> p t d", p=P)
    out_v = out[0].rearrange("(t p) d -> p t d", p=P)
    ada_sums = nc.dram_tensor("ada_sums", (12, P, D), F32, kind="Internal").ap()
    toep_rows = nc.dram_tensor("toeplitz_rows", (16, TOEP), F32, kind="Internal").ap()
    toep_copies = nc.dram_tensor("toeplitz_copies", (P, 16 * TOEP), F32, kind="Internal").ap()
    pieces = stream(a)
    arrive = arrivals(pieces)
    ffn_w = {
        "ffn1_0": (a["ffn1_wg"][0], a["ffn1_wu"][0], a["ffn1_wd"][0]),
        "ffn2_0": (a["ffn2_wg"][0], a["ffn2_wu"][0], a["ffn2_wd"][0]),
        "ffn1_1": (a["ffn1_wg"][1], a["ffn1_wu"][1], a["ffn1_wd"][1]),
        "ffn2_1": (a["ffn2_wg"][1], a["ffn2_wu"][1], a["ffn2_wd"][1]),
        "dense": (a["ffn_w_gate_2"][0], a["ffn_w_up_2"][0], a["ffn_w_down_2"][0]),
    }

    ctx = ExitStack()
    with ctx:
        sems = Semaphores(nc, ctx)
        m = layout(nc, ctx)
        block = ctx.enter_context(nc.Block())

        @block.sync
        def _(queue):
            load_program(nc, Engine(queue, sems, "sync"), m, a, x_in, out_v, consts, pieces, ffn_w)

        @block.gpsimd
        def _(queue):
            pool_program(nc, Engine(queue, sems, "gpsimd"), m, a, ada_sums)

        @block.scalar
        def _(queue):
            scalar_program(nc, Scalar(nc, queue, sems, m, arrive), a, consts, ada_sums, toep_rows, toep_copies)

        @block.vector
        def _(queue):
            vector_program(nc, Vector(nc, queue, sems, m, arrive), consts)

        @block.tensor
        def _(queue):
            tensor_program(nc, Tensor(nc, queue, sems, m), m)


def pool_program(nc, e, m, a, ada_sums):
    g = nc.gpsimd
    e.link(g.memset(m.ident[:, :], 0.0))
    g.memset(m.ones[:, :], 1.0).then_inc(e.sem["pool_const"], 1)
    e.link(g.memset(m.strict[:, :], 1.0))
    e.link(g.memset(m.blocks[:, :], 0.0))
    tri = small(m, TRI, 64)
    e.link(g.memset(tri, 1.0))
    g.memset(small(m, EPS6), 1e-6).then_inc(e.sem["pool_const"], 1)
    g.memset(small(m, EPS5), 1e-5).then_inc(e.sem["pool_const"], 1)
    g.affine_select(out=m.ident[:, :], in_=m.ident[:, :], compare_op=ALU.not_equal, fill=1.0, base=0,
                          pattern=[[-1, P]], channel_multiplier=1).then_inc(e.sem["pool_const"], 1)
    g.affine_select(out=m.strict[:, :], in_=m.strict[:, :], compare_op=ALU.is_gt, fill=0.0, base=0,
                          pattern=[[-1, P]], channel_multiplier=1).then_inc(e.sem["pool_const"], 1)
    t3 = tri.rearrange("p (e j) -> p e j", e=8)
    g.affine_select(out=t3, in_=t3, compare_op=ALU.is_gt, fill=0.0, base=0,
                          pattern=[[1, 8], [-1, 8]], channel_multiplier=0).then_inc(e.sem["pool_const"], 1)
    e.q.wait_ge(e.sem["pool_const"], e.next("pool_const", POOL_CONSTS - 2))
    for b in range(2):
        g.memset(m.blocks[64 * b:64 * b + 64, 64 * b:64 * b + 64], 1.0).then_inc(e.sem["pool_const"], 1)
        e.q.wait_ge(e.sem["pool_const"], e.next("pool_const"))

    ring = [take_view(m, b * D, D) for b in range(2)]
    acc, tmp = take_view(m, 2 * D, D), take_view(m, 3 * D, D)
    e.q.wait_ge(e.sem["c_ready"], e.next("c_ready"))
    for layer in range(2):
        w = a["ada_w_2"][layer].rearrange("(k p) n -> p k n", p=P)
        bias = a["ada_b_2"][layer:layer + 1, :]
        for v in range(6):
            for k in range(2):
                g.dma_start(ring[k], w[:, k, v * D:(v + 1) * D]).then_inc(e.sem[f"ada_w_loaded{k}"], 16)
            if layer or v:
                e.q.wait_ge(e.sem["ada_stored"], e.next("ada_stored", 16))
            e.link(g.memset(acc, 0.0))
            g.dma_start(acc[0:1, :], bias[:, v * D:(v + 1) * D]).then_inc(e.sem["ada_b_loaded"], 16)
            e.q.wait_ge(e.sem["ada_b_loaded"], e.next("ada_b_loaded", 16))
            for k in range(KT):
                e.q.wait_ge(e.sem[f"ada_w_loaded{k % 2}"], e.next(f"ada_w_loaded{k % 2}", 16))
                e.link(g.tensor_scalar(tmp, ring[k % 2], small(m, CACT + k), None, ALU.mult))
                if k + 2 < KT:
                    g.dma_start(ring[k % 2], w[:, k + 2, v * D:(v + 1) * D]).then_inc(e.sem[f"ada_w_loaded{k % 2}"], 16)
                e.link(g.tensor_tensor(acc, acc, tmp, ALU.add))
            g.dma_start(ada_sums[layer * 6 + v], acc).then_inc(e.sem["ada_stored"], 16)
    e.q.wait_ge(e.sem["ada_stored"], e.next("ada_stored", 16))



def load_program(nc, e, m, a, x_in, out_v, consts, pieces, ffn_w):
    nc.sync.dma_start(m.x, x_in).then_inc(e.sem["x_loaded"], 16)
    n = 0

    def slot():
        nonlocal n
        if n >= N_RAW:
            e.q.wait_ge(e.sem["piece_lo"], e.at(n - N_RAW + 1, PER[0]))
        raw = m.raw[:, n % N_RAW * PIECE:(n % N_RAW + 1) * PIECE]
        name = f"raw_filled{n % N_RAW}"
        n += 1
        return raw, name

    PER = [0]

    def ffn_columns(w, k0, c):
        raw, name = slot()
        nc.sync.dma_start(raw.rearrange("p (k n) -> p k n", k=KT), w[:, k0, c]).then_inc(e.sem[name], 16)

    def ffn_rows(w, k0):
        raw, name = slot()
        nc.sync.dma_start(raw.rearrange("p (k n) -> p k n", k=2), w[:, k0, :]).then_inc(e.sem[name], 16)

    def ffn(wg, wu, wd):
        nonlocal n
        wg, wu, wd = (w.rearrange("(k p) n -> p k n", p=P) for w in (wg, wu, wd))
        every = slice(0, KT)
        for w in (wg, wu):
            ffn_columns(w, every, slice(0, FC))

        def step(s, at):
            for w in (wg, wu):
                ffn_columns(w, every, bass.ds(s * FC + at * FC + FC, FC))
            ffn_rows(wd, bass.ds(s * 2 + at * 2, 2))
        step(0, 0)
        step(1, 0)
        PER[0] = 6
        with e.loop((STEPS - 3) // 2, {}) as it:
            for i in range(2):
                step(it * 2, 2 + i)
        PER[0] = 0
        n += 6 * ((STEPS - 3) // 2 - 1)
        ffn_rows(wd, slice(2 * STEPS - 2, 2 * STEPS))

    def moe(wg, wu, wd):
        nonlocal n
        wg, wu, wd = (w.rearrange("e (k p) n -> p (e k) n", p=P) for w in (wg, wu, wd))
        for w in (wg, wu):
            ffn_columns(w, slice(0, KT), slice(0, FC))

        def step(pair, s, last=False):
            if not last:
                x, c = divmod(s + 1, STEPS)
                for w in (wg, wu):
                    ffn_columns(w, bass.ds(pair * (2 * KT) + x * KT, KT), slice(c * FC, (c + 1) * FC))
            x, c = divmod(s, STEPS)
            kf = FF // P
            ffn_rows(wd, bass.ds(pair * (2 * kf) + (x * kf + 2 * c), 2))
        pairs = N_EXPERTS // 2
        PER[0] = 3 * 2 * STEPS
        with e.loop(pairs - 1, {}) as it:
            for s in range(2 * STEPS):
                step(it, s)
        PER[0] = 0
        n += 3 * 2 * STEPS * (pairs - 2)
        for s in range(2 * STEPS):
            step(pairs - 1, s, last=s == 2 * STEPS - 1)

    done = set()
    for piece in pieces:
        if piece[0] == "plain":
            raw, name = slot()
            for dst, src in piece[1]:
                nc.sync.dma_start(dst(raw), src).then_inc(e.sem[name], 16)
        elif piece[0] not in done:
            done.add(piece[0])
            if piece[0] == "moe":
                moe(a["moe_w_gate_2"][0], a["moe_w_up_2"][0], a["moe_w_down_2"][0])
            else:
                ffn(*ffn_w[piece[0]])
    e.q.wait_ge(e.sem["x_ready_out"], e.next("x_ready_out"))
    nc.sync.dma_start(out_v, m.x).then_inc(e.sem["out_stored"], 16)
    e.q.wait_ge(e.sem["out_stored"], e.next("out_stored", 16))



class Tensor(Engine):

    def __init__(self, nc, queue, sem, m):
        super().__init__(queue, sem, "tensor")
        self.nc, self.m = nc, m
        self.n = 0
        self.unsaid = 0
        self.j = 0
        self.y = 0
        self.v = 0
        self.head = 0
        self.pair = 0

    def mm(self, out, l, r, start=True, stop=True):
        return self.nc.tensor.matmul(out, l, r, start=start, stop=stop)

    def mm3(self, out, l, r, start, stop):
        first = self.mm(out, l[0], r[0], start, False)
        if self.unsaid:
            first.then_inc(self.sem["piece_used"], 1)
            self.unsaid -= 1
        self.mm(out, l[0], r[1], False, False)
        return self.mm(out, l[1], r[0], False, stop)

    def transpose(self, out, in_):
        rows = in_.shape[0]
        return self.nc.tensor.transpose(out, in_, self.m.ident[0:rows, 0:rows])

    def piece(self):
        n, m = self.n, self.m
        self.q.wait_ge(self.sem["piece_lo"], self.at(n + 1, 6))
        self.n += 1
        at = n % N_HL * PIECE
        return m.whi[:, at:at + PIECE], m.wlo[:, at:at + PIECE]

    def used(self):
        self.unsaid += 1

    def vbank(self):
        if self.v >= 4:
            self.q.wait_ge(self.sem["vbank_free"], self.v - 3)
        self.v += 1
        return self.m.banks[(self.v - 1) % 4]

    def emptied(self):
        self.q.wait_ge(self.sem["vbank_free"], self.v)

    def gate_up(self, first=False):
        m = self.m
        w0, w1 = self.piece(), self.piece()
        for f in range(2):
            if self.j >= 4:
                self.q.wait_ge(self.sem["gu_free"], self.at(self.j - 3, 4))
            bank = m.banks[self.j % 4]
            self.j += 1
            for i, w in enumerate((w0, w1)):
                for k in range(KT):
                    if first and f == 0 and i == 0:
                        self.q.wait_ge(self.sem["hT_ready"], self.next("hT_ready"))
                    at = k * FC + f * P
                    last = self.mm3(bank[:, i * S:(i + 1) * S], tuple(h[:, at:at + P] for h in w),
                                    (m.hhi[:, k, :], m.hlo[:, k, :]), k == 0, k == KT - 1)
                if i == 0 and f == 1:
                    self.used()
            last.then_inc(self.sem["gu_ready"], 1)
        self.used()

    def down(self):
        m = self.m
        w = self.piece()
        step = self.y // 4
        self.q.wait_ge(self.sem["act_ready"], self.next("act_ready", 2))
        for t in range(NT):
            for half in range(2):
                b = self.y % 4
                if self.y >= 4:
                    self.q.wait_ge(self.sem["y_free"], self.at(self.y - 3, 8))
                self.y += 1
                for f in range(2):
                    fa = step % 2 * 2 + f
                    at = f * D + half * 512
                    last = self.mm3(m.banks[4 + b][:, :],
                                    (m.ahi[:, fa, t * P:(t + 1) * P], m.alo[:, fa, t * P:(t + 1) * P]),
                                    tuple(h[:, at:at + 512] for h in w), f == 0, f == 1)
                last.then_inc(self.sem["y_ready"], 1)
        self.used()

    def ffn(self, n, peel=0, first=True):
        self.emptied()
        self.gate_up(first)
        for _ in range(peel):
            self.gate_up()
            self.down()
        turns = (n - 1 - peel) // 2
        n0, j0, y0 = self.n, self.j, self.y
        with self.loop(turns, {"act_ready": 4}):
            for _ in range(2):
                self.gate_up()
                self.down()
        self.n, self.j, self.y = n0 + 6 * turns, j0 + 4 * turns, y0 + 8 * turns
        for _ in range((n - 1 - peel) % 2):
            self.gate_up()
            self.down()
        self.down()

    def norm(self):
        m = self.m
        xn = take_view(m, XN, NT * D, "p (t d) -> p t d", t=NT)
        self.q.wait_ge(self.sem["xn_ready"], self.next("xn_ready", NT))
        for kk in range(KT // 2):
            bank = self.vbank()
            for k in range(2):
                for t in range(NT):
                    at = (2 * k + t) * P
                    last = self.transpose(bank[:, at:at + P], xn[:, t, (2 * kk + k) * P:(2 * kk + k + 1) * P])
            last.then_inc(self.sem["vbank_ready"], 1)

    def features(self, w, tiles, bank, n=FC):
        m = self.m
        for i, (c, width) in enumerate(tiles):
            for k in range(KT):
                last = self.mm3(bank[0:width, i * S:(i + 1) * S], tuple(h[:, k * n + c:k * n + c + width] for h in w),
                                (m.hhi[:, k, :], m.hlo[:, k, :]), k == 0, k == KT - 1)
        return last

    def tokens(self, w, t, c, width, out, n=FC, hT=None, kt=KT):
        m = self.m
        hT = hT or (m.hhi, m.hlo)
        for k in range(kt):
            last = self.mm3(out, tuple(h[:, k, t * P:(t + 1) * P] for h in hT),
                            tuple(h[:, k * n + c:k * n + c + width] for h in w), k == 0, k == kt - 1)
        return last

    def out_projection(self, i, banks):
        m = self.m
        w = self.piece()
        for kt in range(2):
            k = 2 * i + kt
            for t in range(NT):
                for half in range(2):
                    at = kt * D + half * 512
                    last = self.mm3(banks[2 * t + half][:, :],
                                    (m.hhi[:, k, t * P:(t + 1) * P], m.hlo[:, k, t * P:(t + 1) * P]),
                                    tuple(h[:, at:at + 512] for h in w), k == 0, k == KT - 1)
                    if k == KT - 1:
                        last.then_inc(self.sem["vbank_ready"], 1)
        self.used()

    def attention(self, heads):
        m, sem = self.m, self.sem

        def scores(i):
            q, k, _, _ = heads[i]
            h = self.head + i
            if h >= 2:
                self.q.wait_ge(sem["scores_taken"], h - 1)
            bank = m.banks[h % 2]
            self.mm(bank[:, 0:P], q[:, 0:P], k[:, 0:P])
            self.mm(bank[:, P:3 * P], q[:, P:2 * P], k[:, :]).then_inc(sem["scores_ready"], 1)

        scores(0)
        scores(1)
        for i, (_, _, value, half) in enumerate(heads):
            h = self.head + i
            s = take_view(m, SCORES + h % 2 * TOEP, TOEP)
            pt = take_view(m, PROBT + h % 2 * TOEP, TOEP)
            bank = m.banks[2 + h % 2]
            self.q.wait_ge(sem["probs_ready"], self.next("probs_ready"))
            self.transpose(bank[:, 0:P], s[:, 0:P])
            self.transpose(bank[:, P:2 * P], s[:, P:2 * P])
            self.transpose(bank[:, 2 * P:3 * P], s[:, 2 * P:3 * P]).then_inc(sem["probs_turned"], 1)
            if i + 2 < len(heads):
                scores(i + 2)
            out = m.banks[4 + self.pair % 2]
            if half == 0 and self.pair >= 2:
                self.q.wait_ge(sem["outs_taken"], self.pair - 1)
            self.q.wait_ge(sem["probT_ready"], self.next("probT_ready"))
            o = out[64 * half:64 * half + 64, :]
            self.mm(o[:, 0:P], value(0), pt[:, 0:P])
            self.mm(o[:, P:2 * P], value(0), pt[:, P:2 * P], True, False)
            last = self.mm(o[:, P:2 * P], value(1), pt[:, 2 * P:3 * P], False, True)
            if half:
                last.then_inc(sem["outs_ready"], 1)
                self.pair += 1
        self.head += len(heads)

    def sums(self, out, operands):
        for i, op in enumerate(operands):
            last = self.mm(out, self.m.ones[:, :], op, i == 0, i == len(operands) - 1)
        return last

    def ada_columns(self):
        m = self.m
        self.q.wait_ge(self.sem["ada_in"], self.next("ada_in", 32))
        for v in range(2):
            for k in range(KT):
                last = self.mm(m.banks[7][:, v * KT + k:v * KT + k + 1], take_view(m, MOD + v * D + k * P, P),
                               m.ones[:, 0:1])
        last.then_inc(self.sem["mean_ready"], 1)

    def ada_gain(self):
        m = self.m
        self.q.wait_ge(self.sem["ada_gate_in"], self.next("ada_gate_in", 16))
        for half in range(2):
            bank = self.vbank()
            self.mm(bank[:, :], m.ones[:, :], take_view(m, GATE_IN + half * 512, 512)).then_inc(
                self.sem["vbank_ready"], 1)


def tensor_program(nc, e, m):
    sem = e.sem
    e.q.wait_ge(sem["pool_const"], e.next("pool_const", POOL_CONSTS))
    e.q.wait_ge(sem["rows_loaded"], ROWS_LOADS * 16)
    for i, names in enumerate(ROW_TILES):
        rows = sum(n for name, n in COLUMN_SIZES if name in names)
        e.transpose(e.vbank()[:, 0:rows], take_view(m, ROWS_AT + i * P, P)[0:rows, :]).then_inc(sem["vbank_ready"], 1)
    e.q.wait_ge(sem["relbias_ready"], e.next("relbias_ready"))
    e.mm(e.vbank()[0:8, 0:TOEP], take_view(m, REL_AT, 8)[0:33, :],
         take_view(m, ONEHOT_AT, TOEP)[0:33, :]).then_inc(sem["vbank_ready"], 1)

    e.norm()
    e.ffn(STEPS, peel=2)
    e.norm()
    even_tensor(e, m)
    e.norm()
    e.ffn(STEPS)
    e.norm()
    e.ffn(STEPS)
    e.norm()
    odd_tensor(e, m)
    e.norm()
    e.ffn(STEPS)
    for layer in range(2):
        e.ada_columns()
        e.norm()
        mix_tensor(e, m, layer)
        e.ada_columns()
        e.norm()
        if layer == 0:
            e.ffn(STEPS)
        else:
            w, bank = e.piece(), e.vbank()
            e.q.wait_ge(sem["hT_ready"], e.next("hT_ready", KT))
            for t in range(NT):
                last = e.tokens(w, t, 0, N_EXPERTS, bank[:, t * 8:t * 8 + 8], n=N_EXPERTS)
            last.then_inc(sem["vbank_ready"], 1)
            e.used()
            e.ffn(N_EXPERTS * STEPS, first=False)
        e.ada_gain()


def even_tensor(e, m):
    sem = e.sem
    e.emptied()
    e.gate_up(True)
    e.gate_up()
    e.q.wait_ge(sem["gu_free"], e.j)
    w, bank = e.piece(), e.vbank()
    e.features(w, [(0, P)], bank)
    for t in range(NT):
        last = e.tokens(w, t, P, P, bank[:, S + t * P:S + (t + 1) * P])
    last.then_inc(sem["vbank_ready"], 1)
    e.used()
    for _ in range(2):
        e.features(e.piece(), [(0, P), (P, P)], e.vbank()).then_inc(sem["vbank_ready"], 1)
        e.used()
    e.emptied()
    qt = take_view(m, E_QT, 4 * S, "p (i s) -> p i s", i=4)
    kt = take_view(m, E_KV, S)
    v = take_view(m, E_KV + S, S, "p (t d) -> p t d", t=NT)
    heads = []
    for i in range(4):
        for b in range(2):
            rows = slice(64 * b, 64 * b + 64)
            heads.append((qt[rows, i, :], kt[rows, :], lambda t, b=b: v[:, t, 64 * b:64 * b + 64], b))
    e.attention(heads)
    conv = take_view(m, E_CONV, 4 * S, "p (c s) -> p c s", c=4)
    sq = take_view(m, E_SQ, 4 * S, "p (c s) -> p c s", c=4)
    e.q.wait_ge(sem["conv_ready"], e.next("conv_ready"))
    e.sums(m.banks[7][:, 0:S], [conv[:, c, :] for c in range(4)]).then_inc(sem["mean_ready"], 1)
    e.q.wait_ge(sem["squares_ready"], e.next("squares_ready"))
    e.sums(m.banks[6][:, 0:S], [sq[:, c, :] for c in range(4)]).then_inc(sem["var_ready"], 1)
    banks = [e.vbank() for _ in range(4)]
    e.q.wait_ge(sem["outs_taken"], e.pair)
    for i in range(4):
        if i >= 2:
            e.q.wait_ge(sem["cat_ready"], e.next("cat_ready", 2))
        e.out_projection(i, banks)


def odd_tensor(e, m):
    sem = e.sem
    e.q.wait_ge(sem["hT_ready"], e.next("hT_ready", KT))
    for _ in range(4):
        e.features(e.piece(), [(0, P), (P, P)], e.vbank()).then_inc(sem["vbank_ready"], 1)
        e.used()
    for i in range(4):
        w = e.piece()
        if i >= 2:
            e.q.wait_ge(sem["gate_ready"], i - 1)
        e.features(w, [(0, P), (P, P)], m.banks[4 + i % 2]).then_inc(sem["gate_mm_ready"], 1)
        e.used()
    w = e.piece()
    for h in range(KT):
        e.q.wait_ge(sem["xc_ready"], e.next("xc_ready"))
        if h >= 2:
            e.q.wait_ge(sem["ri_ready"], h - 1)
        for i in range(2):
            at = i * D + h * P
            last = e.mm3(m.banks[4 + h % 2][:, i * S:(i + 1) * S], tuple(x[:, at:at + P] for x in w),
                         (m.hhi[:, h, :], m.hlo[:, h, :]), True, True)
        last.then_inc(sem["ri_mm_ready"], 1)
    e.used()
    banks = [e.vbank() for _ in range(4)]
    for i in range(4):
        e.q.wait_ge(sem["cat_ready"], e.next("cat_ready", 2))
        e.out_projection(i, banks)


def mix_tensor(e, m, layer):
    sem = e.sem
    e.q.wait_ge(sem["hT_ready"], e.next("hT_ready", KT))
    e.features(e.piece(), [(0, P), (P, P)], e.vbank()).then_inc(sem["vbank_ready"], 1)
    e.used()
    w, bank = e.piece(), e.vbank()
    e.features(w, [(0, P)], bank, n=160)
    for t in range(NT):
        last = e.tokens(w, t, P, 32, bank[:, S + 32 * t:S + 32 * t + 32], n=160)
    last.then_inc(sem["vbank_ready"], 1)
    e.used()
    sq = take_view(m, M_QKT + 1024, 3 * S, "p (c s) -> p c s", c=3)
    e.q.wait_ge(sem["squares_ready"], e.next("squares_ready"))
    e.sums(m.banks[6][:, 0:S], [sq[:, 0, :], sq[:, 1, :]])
    e.sums(m.banks[6][:, S:2 * S], [sq[:, 2, :]]).then_inc(sem["var_ready"], 1)
    w = e.piece()
    e.q.wait_ge(sem["latents_ready"], e.next("latents_ready"))
    for t in range(NT):
        for half in range(2):
            e.tokens(w, t, 384 * half, 384, e.vbank()[:, 0:384], n=768, hT=(m.ahi[:, 0:2, :], m.alo[:, 0:2, :]),
                     kt=2).then_inc(sem["vbank_ready"], 1)
    e.used()
    w = e.piece()
    for t in range(NT):
        for half in range(2):
            e.tokens(w, t, 512 * half, 512, e.vbank()[:, :], n=D, hT=(m.ahi[:, 2:3, :], m.alo[:, 2:3, :]),
                     kt=1).then_inc(sem["vbank_ready"], 1)
    e.used()
    q_tok = take_view(m, M_QTOK, NT * 768, "p (t h d) -> p t h d", t=NT, h=8)
    k_tok = take_view(m, M_KTOK, NT * 768, "p (t h d) -> p t h d", t=NT, h=8)
    e.q.wait_ge(sem["normed_qk"], e.next("normed_qk"))
    for h in range(8):
        bank = m.banks[4 + h % 2]
        if h >= 2:
            e.q.wait_ge(sem["qkT_ready"], 8 * layer + h - 1)
        for i, tok in enumerate((q_tok, k_tok)):
            for t in range(NT):
                at = i * S + t * P
                last = e.transpose(bank[0:96, at:at + P], tok[:, t, h, :])
        last.then_inc(sem["qk_turned"], 1)
    for i in range(6):
        w, bank = e.piece(), e.vbank()
        if i % 3 < 2:
            last = e.features(w, [(0, P), (P, P)], bank)
        else:
            for t in range(NT):
                last = e.tokens(w, t, 0, FC, bank[:, t * FC:(t + 1) * FC])
        last.then_inc(sem["vbank_ready"], 1)
        e.used()
    sq = take_view(m, M_OT, 4 * S)
    e.q.wait_ge(sem["squares_ready"], e.next("squares_ready"))
    for i in range(2):
        e.mm(m.banks[6 + i][:, :], m.blocks[:, :], sq[:, i * 512:(i + 1) * 512]).then_inc(sem["var_ready"], 1)
    e.emptied()
    e.q.wait_ge(sem["qkT_ready"], e.next("qkT_ready", 8))
    qkt = take_view(m, M_QKT, 8 * 512, "p (h s) -> p h s", h=8)
    v_tok = take_view(m, M_VTOK, NT * 512, "p (t h d) -> p t h d", t=NT, h=8)
    e.attention([(qkt[0:96, h, 0:S], qkt[0:96, h, S:2 * S], lambda t, h=h: v_tok[:, t, h, :], h % 2)
                 for h in range(8)])
    for base in (M_SB, M_CK):
        qt, kt, v = (take_view(m, base + 512 * i, 512, "p (i s) -> p i s", i=2) for i in range(3))
        if base == M_CK:
            e.q.wait_ge(sem["band_ready"], e.next("band_ready"))
        e.attention([(qt[64 * (h % 2):64 * (h % 2) + 64, h // 2, :], kt[64 * (h % 2):64 * (h % 2) + 64, h // 2, :],
                      lambda t, h=h, v=v: v[:, t, 64 * h:64 * h + 64], h % 2) for h in range(4)])
    sq = take_view(m, M_QKT, 8 * S, "p (k s) -> p k s", k=8)
    e.q.wait_ge(sem["squares_ready"], e.next("squares_ready"))
    e.sums(m.banks[6][:, 0:S], [sq[:, k, :] for k in (0, 1)])
    e.sums(m.banks[6][:, S:2 * S], [sq[:, k, :] for k in (6, 7)]).then_inc(sem["var_ready"], 1)
    e.sums(m.banks[7][:, 0:S], [sq[:, k, :] for k in (2, 3, 4, 5)]).then_inc(sem["var_ready"], 1)
    e.ada_gain()
    banks = [e.vbank() for _ in range(4)]
    for i in range(4):
        e.q.wait_ge(sem["cat_ready"], e.next("cat_ready", 2))
        e.out_projection(i, banks)



class Scalar(Engine):
    def __init__(self, nc, queue, sems, m, arrive):
        super().__init__(queue, sems, "scalar")
        self.nc, self.m = nc, m
        self.split = Split(self, m, arrive)
        self.j = 0
        self.head = 0
        self.banked = 0

    def hi(self, n=1):
        for _ in range(n):
            self.split.next_hi(self.nc)

    def act(self, out, in_, f, bias=0.0, scale=1.0, accum=None):
        return self.nc.scalar.activation(out, in_, f, bias=bias, scale=scale, accum_out=accum)

    def load(self, dst, src):
        return self.nc.scalar.dma_start(dst, src)

    def norm(self, first=False):
        m = self.m
        self.q.wait_ge(self.sem["x_loaded"], self.next("x_loaded", 16)) if first else self.q.wait_ge(self.sem["x_ready"], self.next("x_ready"))
        for t in range(NT):
            self.link(self.act(take_view(m, XN + t * D, D), m.x[:, t, :], ACT.Square, accum=small(m, SS + t)))
        self.act(small(m, STD, 2), small(m, SS, 2), ACT.Sqrt, bias=small(m, EPS6), scale=1.0 / D).then_inc(self.sem["std_ready"], 1)

    def gate(self, f, half):
        m = self.m
        self.q.wait_ge(self.sem["gu_ready"], self.next("gu_ready"))
        if self.j >= 2:
            self.q.wait_ge(self.sem["gu_free"], self.at(self.j - 1, 4))
        self.act(take_view(m, SIL + self.j % 2 * S, S), m.banks[self.j % 4][:, half * S:(half + 1) * S], f).then_inc(self.sem["gate_act"], 1)
        self.j += 1

    def step(self):
        self.hi()
        self.gate(ACT.Silu, 0)
        self.hi()
        self.gate(ACT.Silu, 0)
        self.hi()

    def ffn(self, n, peel=0):
        self.hi()
        self.gate(ACT.Silu, 0)
        self.hi()
        self.gate(ACT.Silu, 0)
        for _ in range(peel):
            self.step()
        turns = (n - 1 - peel) // 2
        n0, j0 = self.split.n, self.j
        with self.loop(turns, {"gu_ready": 4}):
            self.step()
            self.step()
        self.split.n, self.j = n0 + 6 * turns, j0 + 4 * turns
        for _ in range((n - 1 - peel) % 2):
            self.step()
        self.hi()

    def attention(self, n, kind):
        m = self.m
        for h in range(self.head, self.head + n):
            s = take_view(m, SCORES + h % 2 * TOEP, TOEP)
            p = h % 2
            if kind == "stick":
                t = take_view(m, STICK, 2 * TOEP)
                self.q.wait_ge(self.sem["z_ready"], self.next("z_ready"))
                self.link(self.act(t[:, 0:TOEP], s, ACT.Abs))
                self.link(self.act(t[:, 0:TOEP], t[:, 0:TOEP], ACT.Exp, scale=-1.0))
                self.act(t[:, TOEP:2 * TOEP], t[:, 0:TOEP], ACT.Ln, bias=1.0).then_inc(self.sem["log1p_ready"], 1)
                self.q.wait_ge(self.sem["logw_ready"], self.next("logw_ready"))
                self.act(s, s, ACT.Exp).then_inc(self.sem["exp_ready"], 1)
            else:
                self.q.wait_ge(self.sem["max_ready"], self.next("max_ready"))
                nm, den = small(m, NM + 2 * p, 2), small(m, DEN + 2 * p, 2)
                if kind == "sink":
                    hd = h % 8 // 2 + 4 * (h % 2)
                    self.link(self.act(small(m, ES + 2 * p, 2), nm, ACT.Exp, bias=small(m, SINK + hd)))
                self.link(self.act(s[:, 0:P], s[:, 0:P], ACT.Exp, bias=nm[:, 0:1], accum=den[:, 0:1]))
                self.act(s[:, P:3 * P], s[:, P:3 * P], ACT.Exp, bias=nm[:, 1:2], accum=den[:, 1:2]).then_inc(self.sem["exp_ready"], 1)
            self.q.wait_ge(self.sem["probs_turned"], self.next("probs_turned"))
            self.act(take_view(m, PROBT + p * TOEP, TOEP), m.banks[2 + p][:, 0:TOEP], ACT.Copy).then_inc(self.sem["probT_ready"], 1)
        self.head += n

    def ada_in(self, layer, v, n, at):
        for i in range(n):
            self.load(take_view(self.m, at + i * D, D), self.sums[layer * 6 + v + i]).then_inc(self.sem["ada_gate_in" if n == 1 else "ada_in"], 16)


def broadcast(ap, n):
    return bass.AP(tensor=ap.tensor, offset=ap.offset, ap=[[0, P], [1, n]])


def scalar_program(nc, e, a, consts, ada_sums, toep, toep_copies):
    m = e.m
    e.sums = ada_sums
    for i, names in enumerate(ROW_TILES):
        at = 0
        for name, n in COLUMN_SIZES:
            if name not in names:
                continue
            dst = take_view(m, ROWS_AT + i * P, P)[at:at + n, :]
            src = a[name]
            if "qknorm" in name:
                e.load(dst[:, 0:64], src).then_inc(e.sem["rows_loaded"], 16)
                e.load(dst[:, 64:128], src).then_inc(e.sem["rows_loaded"], 16)
            else:
                while len(src.shape) > 2:
                    src = src.rearrange("a b c -> (a b) c")
                e.load(dst, src.rearrange("a (k f) -> (a k) f", f=P)).then_inc(e.sem["rows_loaded"], 16)
            at += n
    e.load(take_view(m, REL_AT, 8)[0:32, :], a["rel_bias"]).then_inc(e.sem["rel_loaded"], 16)
    e.load(take_view(m, ONEHOT_AT, TOEP)[0:33, :], consts["bucket_onehot"]).then_inc(e.sem["rel_loaded"], 16)
    e.load(take_view(m, CKROW_AT, 257)[0:8, :], a["ck_rel_bias_2"].rearrange("l h r -> (l h) r")).then_inc(e.sem["ck_loaded"], 16)
    e.load(small(m, SINK, 8), broadcast(a["attn_sinks"], 8)).then_inc(e.sem["misc_loaded"], 16)
    pos = a["positions_2"]
    with nc.allow_non_contiguous_dma(reason="one position for each token"):
        e.load(m.pos[:, :], bass.AP(tensor=pos.tensor, offset=pos.offset, ap=[[1, P], [P, NT]])).then_inc(e.sem["misc_loaded"], 16)
    e.load(take_view(m, INVF_AT, 16), broadcast(consts["inv_freq"], 16)).then_inc(e.sem["misc_loaded"], 16)

    e.hi(AHEAD)
    e.q.wait_ge(e.sem["pool_const"], e.next("pool_const", POOL_CONSTS))
    e.norm(first=True)
    e.q.wait_ge(e.sem["cols_ready"], e.next("cols_ready"))
    e.act(small(m, CACT, 8), m.cols[:, COLS["c_2"]:COLS["c_2"] + 8], ACT.Silu).then_inc(e.sem["c_ready"], 1)
    t = take_view(m, LAM_AT, 8)
    e.link(e.act(t, m.cols[:, COLS["lru_lambda"]:COLS["lru_lambda"] + 8], ACT.Abs))
    e.act(t, t, ACT.Exp, scale=-1.0).then_inc(e.sem["lam_exp"], 1)
    e.q.wait_ge(e.sem["angles_ready"], e.next("angles_ready"))
    r = take_view(m, ANG_AT + 64, 32)
    e.link(e.act(m.rope[:, 1, :, :].rearrange("p t f -> p (t f)"), r, ACT.Sin))
    e.act(m.rope[:, 0, :, :].rearrange("p t f -> p (t f)"), r, ACT.Sin, scale=0.5).then_inc(e.sem["sines_ready"], 1)
    e.q.wait_ge(e.sem["toep_rel"], e.next("toep_rel"))
    e.load(toep[0:8, :], take_view(m, REV_AT, TOEP)[0:8, :]).then_inc(e.sem["toep_stored"], 16)
    e.load(toep[8:16, :], take_view(m, CKOUT_AT, TOEP)[0:8, :]).then_inc(e.sem["toep_stored"], 16)
    e.q.wait_ge(e.sem["toep_stored"], e.next("toep_stored", 32))
    e.load(toep_copies, bass.AP(tensor=toep.tensor, offset=toep.offset, ap=[[0, P], [1, 16 * TOEP]])).then_inc(e.sem["toep_copied"], 16)

    e.ffn(STEPS, peel=2)
    e.norm()
    even_scalar(e, m, toep_copies)
    e.norm()
    e.ffn(STEPS)
    e.norm()
    e.ffn(STEPS)
    e.norm()
    odd_scalar(e, m)
    e.norm()
    e.ffn(STEPS)
    e.q.wait_ge(e.sem["x_ready"], e.following("x_ready"))
    e.load(take_view(m, GAIN_AT, D), broadcast(a["norm_final"], D)).then_inc(e.sem["final_gain"], 16)
    e.norm()
    for layer in range(2):
        e.q.wait_ge(e.sem["x_ready"], e.following("x_ready"))
        if layer == 0:
            e.q.wait_ge(e.sem["ada_stored"], e.next("ada_stored", 16 * 12))
        e.ada_in(layer, 0, 2, MOD)
        e.norm()
        mix_scalar(e, m, a, layer, toep_copies)
        e.q.wait_ge(e.sem["x_ready"], e.following("x_ready"))
        e.ada_in(layer, 3, 2, MOD)
        e.norm()
        if layer == 1:
            e.hi()
            e.q.wait_ge(e.sem["logits_ready"], e.next("logits_ready"))
            r = take_view(m, ROUTE, 512)
            for t in range(NT):
                e.act(r[:, 32 + t * 8:40 + t * 8], r[:, t * 8:t * 8 + 8], ACT.Exp, bias=r[:, 48 + t:49 + t]).then_inc(e.sem["route_exp"], 1)
        e.ada_in(layer, 5, 1, GATE_IN)
        e.ffn(STEPS if layer == 0 else N_EXPERTS * STEPS)


def diagonals(copies, row, n):
    return bass.AP(tensor=copies.tensor, offset=copies.offset + row * TOEP + P - 1,
                   ap=[[16 * TOEP - 1, P], [TOEP, n], [1, S]])


def even_scalar(e, m, toep):
    e.q.wait_ge(e.sem["toep_copied"], e.next("toep_copied", 16))
    e.load(take_view(m, E_BIAS, 8 * S, "p (h s) -> p h s", h=8), diagonals(toep, 0, 8)).then_inc(e.sem["bias_loaded"], 16)
    for _ in range(2):
        e.hi(2)
        for _ in range(2):
            e.gate(ACT.Sigmoid, 1)
    e.hi(3)
    e.attention(8, "sink")
    e.q.wait_ge(e.sem["var_ready"], e.next("var_ready"))
    e.act(take_view(m, E_STD, S), m.banks[6][:, 0:S], ACT.Sqrt, bias=small(m, EPS5), scale=1.0 / 512).then_inc(e.sem["std_ready"], 1)
    conv = take_view(m, E_CONV, 4 * S, "p (c s) -> p c s", c=4)
    for c in range(4):
        e.q.wait_ge(e.sem["ln_ready"], e.next("ln_ready"))
        col = lambda name: m.cols[:, COLS[name] + c:COLS[name] + c + 1]
        e.act(conv[:, c, :], conv[:, c, :], ACT.Silu, bias=col("conv_ln_b"), scale=col("conv_ln_g")).then_inc(e.sem["c_act_ready"], 1)
    e.hi(4)


def odd_scalar(e, m):
    e.hi(4)
    gate = take_view(m, O_GATE, 8 * S)
    for i in range(4):
        e.hi()
        e.q.wait_ge(e.sem["gate_mm_ready"], e.next("gate_mm_ready"))
        e.act(gate[:, i * 512:(i + 1) * 512], m.banks[4 + i % 2][:, :], ACT.Gelu_apprx_tanh).then_inc(e.sem["gate_ready"], 1)
    e.hi()
    r, i_ = take_view(m, O_R, 8 * S, "p (h s) -> p h s", h=8), take_view(m, O_REC, 8 * S, "p (h s) -> p h s", h=8)
    for h in range(8):
        e.q.wait_ge(e.sem["ri_mm_ready"], e.next("ri_mm_ready"))
        bank = m.banks[4 + h % 2]
        e.link(e.act(r[:, h, :], bank[:, 0:S], ACT.Sigmoid, bias=m.cols[:, COLS["gate_a_b"] + h:COLS["gate_a_b"] + h + 1]))
        e.act(i_[:, h, :], bank[:, S:2 * S], ACT.Sigmoid, bias=m.cols[:, COLS["gate_x_b"] + h:COLS["gate_x_b"] + h + 1]).then_inc(e.sem["ri_ready"], 1)
    for h in range(8):
        e.q.wait_ge(e.sem["ix_ready"], e.next("ix_ready"))
        e.link(e.act(i_[:, h, :], r[:, h, :], ACT.Tanh, scale=small(m, LRUC + 8 + h)))
        e.act(r[:, h, :], r[:, h, :], ACT.Exp, scale=small(m, LRUC + h)).then_inc(e.sem["a_ready"], 1)
    for h in range(8):
        e.q.wait_ge(e.sem["b2_ready"], e.next("b2_ready"))
        e.act(i_[:, h, :], i_[:, h, :], ACT.Sqrt).then_inc(e.sem["b_ready"], 1)
    e.hi(4)


def mix_scalar(e, m, a, layer, toep):
    gains = m.qkgain
    e.load(gains[:, 0, :], broadcast(a["mla_q_qknorm_2"][layer:layer + 1, :], 96)).then_inc(e.sem["qk_gain"], 16)
    e.load(gains[:, 1, :], broadcast(a["mla_k_qknorm_2"][layer:layer + 1, :], 96)).then_inc(e.sem["qk_gain"], 16)
    e.hi(2)
    std = take_view(m, M_QKT + 1792, 512)
    e.q.wait_ge(e.sem["var_ready"], e.next("var_ready"))
    e.link(e.act(std[:, 0:S], m.banks[6][:, 0:S], ACT.Sqrt, bias=small(m, EPS6), scale=1.0 / 256))
    e.act(std[:, S:2 * S], m.banks[6][:, S:2 * S], ACT.Sqrt, bias=small(m, EPS6), scale=1.0 / 128).then_inc(e.sem["std_ready"], 1)
    e.hi(2)
    e.q.wait_ge(e.sem["qk_sums"], e.next("qk_sums"))
    e.act(small(m, RSQ, 16), small(m, SSQ, 16), ACT.Sqrt, bias=small(m, EPS6), scale=1.0 / 96).then_inc(e.sem["std_ready"], 1)
    e.q.wait_ge(e.sem["qk_sums"], e.next("qk_sums"))
    e.act(small(m, RSQ, 16), small(m, SSQ, 16), ACT.Sqrt, bias=small(m, EPS6), scale=1.0 / 96).then_inc(e.sem["std_ready"], 1)
    qkt = take_view(m, M_QKT, 8 * 512, "p (h s) -> p h s", h=8)
    for h in range(8):
        e.q.wait_ge(e.sem["qk_turned"], e.next("qk_turned"))
        e.act(qkt[0:96, h, :], m.banks[4 + h % 2][0:96, :], ACT.Copy).then_inc(e.sem["qkT_ready"], 1)
    e.hi(6)
    std = take_view(m, M_OT + 1024, 4 * S)
    for i in range(2):
        e.q.wait_ge(e.sem["var_ready"], e.next("var_ready"))
        e.act(std[:, i * 512:(i + 1) * 512], m.banks[6 + i][:, :], ACT.Sqrt, bias=small(m, EPS6), scale=1.0 / 64).then_inc(e.sem["std_ready"], 1)
    e.load(take_view(m, M_BIAS, 4 * S, "p (h s) -> p h s", h=4), diagonals(toep, 8 + 4 * layer, 4)).then_inc(e.sem["bias_loaded"], 16)
    e.attention(8, "plain")
    e.attention(4, "stick")
    e.attention(4, "plain")
    std = take_view(m, M_QTOK, 3 * S)
    e.q.wait_ge(e.sem["var_ready"], e.next("var_ready"))
    e.link(e.act(std[:, 0:512], m.banks[6][:, :], ACT.Sqrt, bias=small(m, EPS6), scale=1.0 / 256))
    e.q.wait_ge(e.sem["var_ready"], e.next("var_ready"))
    e.act(std[:, 512:768], m.banks[7][:, 0:S], ACT.Sqrt, bias=small(m, EPS6), scale=1.0 / 512).then_inc(e.sem["std_ready"], 1)
    e.ada_in(layer, 2, 1, GATE_IN)
    e.hi(4)



class Vector(Engine):
    def __init__(self, nc, queue, sems, m, arrive):
        super().__init__(queue, sems, "vector")
        self.nc, self.m, self.v = nc, m, nc.vector
        self.split = Split(self, m, arrive)
        self.nv = 0
        self.j = 0
        self.f = 0
        self.y = 0
        self.head = 0
        self.pair = 0

    def lo(self, n=1):
        for _ in range(n):
            self.split.next_lo(self.nc)

    def vb(self):
        self.q.wait_ge(self.sem["vbank_ready"], self.next("vbank_ready"))
        self.nv += 1
        return self.m.banks[(self.nv - 1) % 4]

    def col(self, name, i=0):
        return self.m.cols[:, COLS[name] + i:COLS[name] + i + 1]

    def tt(self, out, a, b, op):
        return self.v.tensor_tensor(out, a, b, op)

    def ts(self, out, a, s1, op, s2=None, op2=None):
        return self.v.tensor_scalar(out, a, s1, s2, op, op2) if op2 is not None else self.v.tensor_scalar(out, a, s1, None, op)

    def stt(self, out, a, s, b, op, op2):
        return self.v.scalar_tensor_tensor(out=out, in0=a, scalar=s, in1=b, op0=op, op1=op2)

    def normed(self, gain=None):
        m = self.m
        self.q.wait_ge(self.sem["std_ready"], self.next("std_ready"))
        self.link(self.v.reciprocal(small(m, RSTD, 2), small(m, STD, 2)))
        for t in range(NT):
            if gain is None:
                self.ts(take_view(m, XN + t * D, D), m.x[:, t, :], small(m, RSTD + t), ALU.mult).then_inc(self.sem["xn_ready"], 1)
            else:
                self.stt(m.x[:, t, :], m.x[:, t, :], small(m, RSTD + t), gain, ALU.mult, ALU.mult).then_inc(self.sem["own_vector"], 1)
        if gain is not None:
            self.q.wait_ge(self.sem["own_vector"], self.next("own_vector", NT))

    def norm(self, gain, shift=None):
        m = self.m
        self.normed()
        if shift is not None:
            self.ada_columns(gain)
            gain = m.small[:, GSC:GSC + 8]
        for kk in range(KT // 2):
            bank = self.vb()
            for i in range(2):
                k = 2 * kk + i
                g, src = gain[:, k:k + 1], bank[:, i * S:(i + 1) * S]
                if shift is None:
                    self.link(self.ts(m.hhi[:, k, :], src, g, ALU.mult))
                    self.stt(m.hlo[:, k, :], src, g, m.hhi[:, k, :].bitcast(F32), ALU.mult, ALU.subtract).then_inc(self.sem["hT_ready"], 1)
                else:
                    tmp = take_view(m, TMP + k % 2 * S, S)
                    self.link(self.ts(tmp, src, g, ALU.mult, small(m, SHC + k), ALU.add))
                    self.halves(m.hhi[:, k, :], m.hlo[:, k, :], tmp).then_inc(self.sem["hT_ready"], 1)
            self.v.tensor_copy(small(m, MX + 3), bank[:, 0:1]).then_inc(self.sem["vbank_free"], 1)
            self.q.wait_ge(self.sem["hT_ready"], self.next("hT_ready", 2))
            self.q.wait_ge(self.sem["vbank_free"], self.nv)

    def halves(self, hi, lo, src):
        self.link(self.v.tensor_copy(hi, src))
        ins = self.tt(lo, src, hi.bitcast(F32), ALU.subtract)
        return ins

    def ada_columns(self, gain):
        m = self.m
        self.q.wait_ge(self.sem["mean_ready"], self.next("mean_ready"))
        self.link(self.v.tensor_copy(m.small[:, SHC:SHC + 8], m.banks[7][:, 0:8]))
        self.link(self.stt(m.small[:, GSC:GSC + 8], m.banks[7][:, 8:16], 1.0, gain, ALU.add, ALU.mult))

    def gain(self, name, layer):
        at = COLS[name] + layer * 8
        return self.m.cols[:, at:at + 8]

    def act(self):
        m, j = self.m, self.j
        self.q.wait_ge(self.sem["gate_act"], self.next("gate_act"))
        prod = take_view(m, PROD + self.f % 2 * S, S)
        if self.f >= 2:
            self.q.wait_ge(self.sem["act_ready"], self.at(self.f - 1, 4))
        self.tt(prod, take_view(m, SIL + j % 2 * S, S), m.banks[j % 4][:, S:2 * S], ALU.mult).then_inc(self.sem["gu_free"], 1)
        self.q.wait_ge(self.sem["gu_free"], self.at(j + 1, 4))
        fa = self.f % 4
        self.link(self.v.tensor_copy(m.ahi[:, fa, :], prod))
        self.tt(m.alo[:, fa, :], prod, m.ahi[:, fa, :].bitcast(F32), ALU.subtract).then_inc(self.sem["act_ready"], 1)
        self.j += 1
        self.f += 1

    def y_in(self, scale, target, last=False):
        m = self.m
        for t in range(NT):
            for half in range(2):
                b = self.y % 4
                self.q.wait_ge(self.sem["y_ready"], self.next("y_ready"))
                if self.y >= 4:
                    self.q.wait_ge(self.sem["y_free"], self.at(self.y - 3, 8))
                dst = target[:, t, half * 512:(half + 1) * 512]
                self.stt(dst, m.banks[4 + b][:, :], scale(t), dst, ALU.mult, ALU.add).then_inc(self.sem["y_free"], 1)
                self.y += 1

    def ffn(self, n, scale, target, peel=0):
        def step(s):
            self.lo()
            self.act()
            self.lo()
            self.act()
            self.lo()
            self.y_in(lambda t: scale(s, t), target)
        self.lo()
        self.act()
        self.lo()
        self.act()
        for i in range(peel):
            step(i)
        turns = (n - 1 - peel) // 2
        n0, j0, f0, y0 = self.split.n, self.j, self.f, self.y
        with self.loop(turns, {"gate_act": 4, "own_vector": 4, "y_ready": 8}) as it:
            step(it * 2 + peel)
            step(it * 2 + (peel + 1))
        self.split.n, self.j, self.y = n0 + 6 * turns, j0 + 4 * turns, y0 + 8 * turns
        self.f = f0 + 4 * turns
        for i in range(peel + 2 * turns, n - 1):
            step(i)
        self.lo()
        self.y_in(lambda t: scale(n - 1, t), target)
        self.q.wait_ge(self.sem["y_free"], self.y)

    def ffn_half(self, peel=0):
        self.ffn(STEPS, lambda s, t: 0.5, self.m.x, peel)
        self.marker().then_inc(self.sem["x_ready"], 1)
        self.q.wait_ge(self.sem["x_ready"], self.next("x_ready"))

    def marker(self):
        return self.v.tensor_copy(small(self.m, MX), small(self.m, EPS6))

    def out_in(self, gain=None):
        m = self.m
        for t in range(NT):
            for half in range(2):
                bank = self.vb()
                dst = m.x[:, t, half * 512:(half + 1) * 512]
                if gain is None:
                    self.tt(dst, bank[:, :], dst, ALU.add).then_inc(self.sem["vbank_free"], 1)
                else:
                    tmp = take_view(m, TMP4 + (2 * t + half) % 2 * 512, 512)
                    self.tt(tmp, bank[:, :], gain[:, half * 512:(half + 1) * 512], ALU.mult).then_inc(self.sem["vbank_free"], 1)
                    self.q.wait_ge(self.sem["vbank_free"], self.nv)
                    self.link(self.tt(dst, tmp, dst, ALU.add))
        self.q.wait_ge(self.sem["vbank_free"], self.nv)
        self.marker().then_inc(self.sem["x_ready"], 1)
        self.q.wait_ge(self.sem["x_ready"], self.next("x_ready"))

    def attention(self, heads, kind, scale, out, filler=lambda: None, bias=None, chunked=False):
        m, v = self.m, self.v
        for i, hd in enumerate(heads):
            h = self.head + i
            p = h % 2
            s = take_view(m, SCORES + p * TOEP, TOEP)
            self.q.wait_ge(self.sem["scores_ready"], self.next("scores_ready"))
            bank = m.banks[p]
            if bias is not None:
                b = bias[:, hd, :]
                self.link(self.stt(s[:, 0:P], bank[:, 0:P], scale, b[:, P:2 * P], ALU.mult, ALU.add))
                self.stt(s[:, P:3 * P], bank[:, P:3 * P], scale, b[:, 0:S], ALU.mult, ALU.add).then_inc(self.sem["scores_taken"], 1)
            else:
                self.ts(s, bank[:, 0:TOEP], scale, ALU.mult).then_inc(self.sem["z_ready" if kind == "stick" else "scores_taken"], 1)
            if kind == "stick":
                self.q.wait_ge(self.sem["z_ready"], self.next("z_ready"))
                v.tensor_copy(small(m, MX + 3), bank[:, 0:1]).then_inc(self.sem["scores_taken"], 1)
                self.q.wait_ge(self.sem["scores_taken"], h + 1)
                self.stick(s)
                self.q.wait_ge(self.sem["exp_ready"], self.next("exp_ready"))
                for at in (0, 2 * P):
                    w = s[:, at:at + P]
                    ins = self.tt(w, w, m.strict[:, :], ALU.mult)
                    ins.then_inc(self.sem["probs_ready"], 1) if at else self.link(ins)
            else:
                self.q.wait_ge(self.sem["scores_taken"], h + 1)
                if chunked:
                    self.link(v.memset(s[0:64, 64:P], NEG))
                    self.link(v.memset(s[0:64, 2 * P + 64:3 * P], NEG))
                mx, nm = small(m, MX, 2), small(m, NM + 2 * p, 2)
                self.link(v.reduce_max(mx[:, 0:1], s[:, 0:P], AX.X))
                self.link(v.reduce_max(mx[:, 1:2], s[:, P:3 * P], AX.X))
                if kind == "sink":
                    self.ts(nm, mx, small(m, SINK + hd), ALU.max, -1.0, ALU.mult).then_inc(self.sem["max_ready"], 1)
                else:
                    self.ts(nm, mx, -1.0, ALU.mult).then_inc(self.sem["max_ready"], 1)
                filler()
                self.q.wait_ge(self.sem["exp_ready"], self.next("exp_ready"))
                den, rden = small(m, DEN + 2 * p, 2), small(m, RDEN + 2 * p, 2)
                if kind == "sink":
                    self.link(self.tt(den, den, small(m, ES + 2 * p, 2), ALU.add))
                self.link(v.reciprocal(rden, den))
                self.link(self.ts(s[:, 0:P], s[:, 0:P], rden[:, 0:1], ALU.mult))
                self.ts(s[:, P:3 * P], s[:, P:3 * P], rden[:, 1:2], ALU.mult).then_inc(self.sem["probs_ready"], 1)
                filler()
            if i % 2 == 1 and i > 1:
                self.q.wait_ge(self.sem["outs_ready"], self.next("outs_ready"))
                out(m.banks[4 + (self.pair) % 2][:, 0:S], i // 2 - 1)
                self.pair += 1
        self.q.wait_ge(self.sem["outs_ready"], self.next("outs_ready"))
        out(m.banks[4 + (self.pair) % 2][:, 0:S], len(heads) // 2 - 1)
        self.pair += 1
        self.head += len(heads)

    def stick(self, s):
        m, v = self.m, self.v
        t = take_view(m, STICK, 2 * TOEP)
        self.q.wait_ge(self.sem["log1p_ready"], self.next("log1p_ready"))
        sp = t[:, 0:TOEP]
        self.link(self.stt(sp, s, 0.0, t[:, TOEP:2 * TOEP], ALU.max, ALU.add))
        for at in (0, 2 * P):
            self.link(self.tt(sp[:, at:at + P], sp[:, at:at + P], m.strict[:, :], ALU.mult))
        c = t[:, TOEP:2 * TOEP]
        for lo, hi in ((0, P), (P, 3 * P)):
            x = sp[:, lo:hi][:, ::-1]
            self.link(v.tensor_tensor_scan(c[:, lo:hi][:, ::-1], x, x, 0.0, ALU.add, ALU.bypass))
        self.link(self.tt(s, s, c, ALU.subtract))
        for at in (0, 2 * P):
            ins = self.tt(s[:, at:at + P], s[:, at:at + P], m.strict[:, :], ALU.mult)
            ins.then_inc(self.sem["logw_ready"], 1) if at else self.link(ins)


def vector_program(nc, e, consts):
    m, v = e.m, e.v
    e.lo(AHEAD)
    e.q.wait_ge(e.sem["rel_loaded"], e.next("rel_loaded", 32))
    rel = take_view(m, REL_AT, 8)
    v.memset(rel[32:33, :], NEG).then_inc(e.sem["relbias_ready"], 1)
    e.q.wait_ge(e.sem["ck_loaded"], e.next("ck_loaded", 16))
    ck, rows = take_view(m, CKROW_AT, 257), take_view(m, CKOUT_AT, TOEP)
    e.link(v.tensor_copy(rows[0:8, 0:P - 1], ck[0:8, 256:257].to_broadcast([8, P - 1])))
    e.link(v.tensor_copy(rows[0:8, TOEP - 1:TOEP], ck[0:8, 0:1]))
    e.link(v.tensor_copy(rows[0:8, P - 1:TOEP - 1], ck[0:8, 1:257][:, ::-1]))
    at = 0
    for i, names in enumerate(ROW_TILES):
        n = sum(n for name, n in COLUMN_SIZES if name in names)
        v.tensor_copy(m.cols[:, at:at + n], e.vb()[:, 0:n]).then_inc(e.sem["vbank_free"], 1)
        at += n
    e.q.wait_ge(e.sem["vbank_free"], e.nv)
    e.marker().then_inc(e.sem["cols_ready"], 1)
    e.q.wait_ge(e.sem["cols_ready"], e.next("cols_ready"))
    v.tensor_copy(take_view(m, REV_AT, TOEP)[0:8, :], e.vb()[0:8, 0:TOEP]).then_inc(e.sem["vbank_free"], 1)
    e.q.wait_ge(e.sem["vbank_free"], e.nv)
    e.q.wait_ge(e.sem["misc_loaded"], e.next("misc_loaded", 48))
    ang = take_view(m, ANG_AT, 32, "p (t f) -> p t f", t=NT)
    turns, r, posf = (take_view(m, ANG_AT + 32 * i, 32) for i in (1, 2, 3))
    e.link(v.tensor_copy(posf[:, 0:NT], m.pos[:, :]))
    for t in range(NT):
        e.link(e.ts(ang[:, t, :], take_view(m, INVF_AT, 16), posf[:, t:t + 1], ALU.mult))
    flat = take_view(m, ANG_AT, 32)
    e.link(e.ts(turns, flat, float(1 / (2 * np.pi)), ALU.mult))
    e.link(e.ts(turns, turns, 12582912.0, ALU.add))
    e.link(e.ts(turns, turns, -12582912.0, ALU.add))
    c1 = 6.28125
    c2 = 2029 / 2**20
    c3 = float(2 * np.pi - c1 - c2)
    e.link(e.stt(r, turns, -c1, flat, ALU.mult, ALU.add))
    e.link(e.stt(r, turns, -c2, r, ALU.mult, ALU.add))
    e.link(e.stt(r, turns, -c3, r, ALU.mult, ALU.add))
    e.ts(r, r, 3.1415925, ALU.min, -3.1415925, ALU.max).then_inc(e.sem["angles_ready"], 1)
    e.q.wait_ge(e.sem["lam_exp"], e.next("lam_exp"))
    y, z, z2, acc = (take_view(m, LAM_AT + 8 * i, 8) for i in range(4))
    e.link(e.ts(z, y, 2.0, ALU.add))
    e.link(v.reciprocal(z, z))
    e.link(e.tt(z, z, y, ALU.mult))
    e.link(e.tt(z2, z, z, ALU.mult))
    e.link(v.memset(acc, 1.0 / 15))
    for k in (13, 11, 9, 7, 5, 3, 1):
        e.link(e.tt(acc, acc, z2, ALU.mult))
        e.link(e.ts(acc, acc, 1.0 / k, ALU.add))
    e.link(e.tt(acc, acc, z, ALU.mult))
    lam = m.cols[:, COLS["lru_lambda"]:COLS["lru_lambda"] + 8]
    e.link(e.ts(z, lam, 0.0, ALU.min, 8.0, ALU.mult))
    e.link(e.stt(small(m, LRUC, 8), acc, -16.0, z, ALU.mult, ALU.add))
    e.link(e.ts(small(m, LRUC + 8, 8), small(m, LRUC, 8), -1.0, ALU.mult))
    e.q.wait_ge(e.sem["sines_ready"], e.next("sines_ready"))
    cos = m.rope[:, 0, :, :].rearrange("p t f -> p (t f)")
    e.link(e.tt(cos, cos, cos, ALU.mult))
    e.link(e.ts(cos, cos, -2.0, ALU.mult, 1.0, ALU.add))
    e.marker().then_inc(e.sem["toep_rel"], 1)
    e.q.wait_ge(e.sem["toep_rel"], e.next("toep_rel"))

    e.norm(e.gain("norm_ffn1", 0))
    e.ffn_half(peel=2)
    e.norm(e.gain("norm_mix", 0))
    even_vector(e, m)
    e.norm(e.gain("norm_ffn2", 0))
    e.ffn_half()
    e.norm(e.gain("norm_ffn1", 1))
    e.ffn_half()
    e.norm(e.gain("norm_mix", 1))
    odd_vector(e, m)
    e.norm(e.gain("norm_ffn2", 1))
    e.ffn_half()
    e.q.wait_ge(e.sem["final_gain"], e.next("final_gain", 16))
    e.normed(take_view(m, GAIN_AT, D))
    e.marker().then_inc(e.sem["x_ready"], 1)
    e.q.wait_ge(e.sem["x_ready"], e.next("x_ready"))
    for layer in range(2):
        e.norm(e.gain("norm_mix_2", layer), True)
        mix_vector(e, m, layer)
        e.norm(e.gain("norm_ffn_2", layer), True)
        yacc = take_view(m, YACC, NT * D, "p (t d) -> p t d", t=NT)
        e.link(v.memset(yacc, 0.0))
        if layer == 0:
            e.ffn(STEPS, lambda s, t: 1.0, yacc)
        else:
            route(e, m)
            n = N_EXPERTS * STEPS
            gates = take_view(m, GATES, NT * n, "p (t s) -> p t s", t=NT)
            e.ffn(n, lambda s, t: gates[:, t, s:s + 1] if isinstance(s, int) else gates[:, t, bass.ds(s, 1)], yacc)
        gain = ada_gain(e, m)
        for t in range(NT):
            e.link(e.tt(yacc[:, t, :], yacc[:, t, :], gain, ALU.mult))
            e.link(e.tt(m.x[:, t, :], m.x[:, t, :], yacc[:, t, :], ALU.add))
        e.marker().then_inc(e.sem["x_ready" if layer == 0 else "x_ready_out"], 1)
        e.q.wait_ge(e.sem["x_ready" if layer == 0 else "x_ready_out"], e.next("x_ready" if layer == 0 else "x_ready_out"))


def ada_gain(e, m):
    gain = take_view(m, GAIN_AT, D)
    for half in range(2):
        e.v.tensor_copy(gain[:, half * 512:(half + 1) * 512], e.vb()[:, :]).then_inc(e.sem["vbank_free"], 1)
    e.q.wait_ge(e.sem["vbank_free"], e.nv)
    return gain


def route(e, m):
    v = e.v
    r = take_view(m, ROUTE, 512)
    logits = r[:, 0:16]
    e.lo()
    v.tensor_copy(logits, e.vb()[:, 0:16]).then_inc(e.sem["vbank_free"], 1)
    e.q.wait_ge(e.sem["vbank_free"], e.nv)
    for t in range(NT):
        e.link(v.reduce_max(r[:, 48 + t:49 + t], r[:, t * 8:t * 8 + 8], AX.X))
    e.link(e.ts(r[:, 48:50], r[:, 48:50], -1.0, ALU.mult))
    e.marker().then_inc(e.sem["logits_ready"], 1)
    e.q.wait_ge(e.sem["logits_ready"], e.next("logits_ready"))
    gates = take_view(m, GATES, NT * N_EXPERTS * STEPS, "p (t x s) -> p t x s", t=NT, x=N_EXPERTS)
    above, equal = (r[:, 64 + 64 * i:128 + 64 * i].rearrange("p (x j) -> p x j", x=8) for i in range(2))
    tri = m.small[:, TRI:TRI + 64].rearrange("p (x j) -> p x j", x=8)
    e.q.wait_ge(e.sem["route_exp"], e.next("route_exp", NT))
    for t in range(NT):
        l = r[:, t * 8:t * 8 + 8]
        lj = l.unsqueeze(1).to_broadcast([P, 8, 8])
        lx = l.unsqueeze(2).to_broadcast([P, 8, 8])
        e.link(e.tt(above, lj, lx, ALU.is_gt))
        e.link(e.tt(equal, lj, lx, ALU.is_equal))
        e.link(e.tt(equal, equal, tri, ALU.mult))
        e.link(e.tt(above, above, equal, ALU.add))
        rank = r[:, 192:200]
        e.link(v.reduce_sum(rank, above, AX.X))
        e.link(e.ts(rank, rank, 2.0, ALU.is_lt))
        ex = r[:, 32 + t * 8:40 + t * 8]
        e.link(e.tt(ex, ex, rank, ALU.mult))
        e.link(v.reduce_sum(r[:, 200:201], ex, AX.X))
        e.link(v.reciprocal(r[:, 200:201], r[:, 200:201]))
        e.link(e.ts(ex, ex, r[:, 200:201], ALU.mult))
        e.link(v.tensor_copy(gates[:, t, :, :], ex.unsqueeze(2).to_broadcast([P, N_EXPERTS, STEPS])))


def even_vector(e, m):
    v = e.v
    pad = 30
    gp = take_view(m, E_GP, 4 * (pad + S), "p (c s) -> p c s", c=4)
    conv = take_view(m, E_CONV, 4 * S, "p (c s) -> p c s", c=4)
    sq = take_view(m, E_SQ, 4 * S, "p (c s) -> p c s", c=4)
    e.link(v.memset(gp[:, :, 0:pad], 0.0))
    for i in range(4):
        if i % 2 == 0:
            e.lo(2)
        e.q.wait_ge(e.sem["gate_act"], e.next("gate_act"))
        e.tt(gp[:, i, pad:], take_view(m, SIL + e.j % 2 * S, S), m.banks[e.j % 4][:, 0:S], ALU.mult).then_inc(e.sem["gu_free"], 1)
        e.q.wait_ge(e.sem["gu_free"], e.j + 1)
        e.j += 1
    e.lo()
    v.tensor_copy(take_view(m, E_KV, 512), e.vb()[:, :]).then_inc(e.sem["vbank_free"], 1)
    for i in range(2):
        e.lo()
        v.tensor_copy(take_view(m, E_QT + 512 * i, 512), e.vb()[:, :]).then_inc(e.sem["vbank_free"], 1)
    e.q.wait_ge(e.sem["vbank_free"], e.nv)
    e.q.wait_ge(e.sem["bias_loaded"], e.next("bias_loaded", 16))

    taps = [(j, c) for j in range(31) for c in range(4)]
    at = [0]

    def some_taps(n=8):
        for _ in range(n):
            if at[0] == len(taps):
                return
            j, c = taps[at[0]]
            if at[0] >= 4:
                e.q.wait_ge(e.sem["conv_tap"], at[0] - 3)
            w = e.col("conv_b_w", j * 4 + c)
            if j == 0:
                ins = e.ts(conv[:, c, :], gp[:, c, 0:S], w, ALU.mult, e.col("conv_b_b", c), ALU.add)
            else:
                ins = e.stt(conv[:, c, :], gp[:, c, j:j + S], w, conv[:, c, :], ALU.mult, ALU.add)
            ins.then_inc(e.sem["conv_tap"], 1)
            at[0] += 1

    def outs(bank, pair):
        k = pair
        e.link(v.tensor_copy(m.hhi[:, k, :], bank))
        e.tt(m.hlo[:, k, :], bank, m.hhi[:, k, :].bitcast(F32), ALU.subtract).then_inc(e.sem["outs_taken"], 1)
        e.q.wait_ge(e.sem["outs_taken"], e.pair + 1)

    bias = take_view(m, E_BIAS, 8 * S, "p (h s) -> p h s", h=8)
    e.attention([i + 4 * b for i in range(4) for b in range(2)], "sink", 0.125, outs, some_taps, bias)
    some_taps(len(taps))
    e.q.wait_ge(e.sem["conv_tap"], len(taps))
    e.marker().then_inc(e.sem["conv_ready"], 1)
    e.q.wait_ge(e.sem["conv_ready"], e.next("conv_ready"))
    e.q.wait_ge(e.sem["mean_ready"], e.next("mean_ready"))
    for c in range(4):
        e.link(e.stt(conv[:, c, :], m.banks[7][:, 0:S], -1.0 / 512, conv[:, c, :], ALU.mult, ALU.add))
        e.link(e.tt(sq[:, c, :], conv[:, c, :], conv[:, c, :], ALU.mult))
    e.marker().then_inc(e.sem["squares_ready"], 1)
    e.q.wait_ge(e.sem["squares_ready"], e.next("squares_ready"))
    e.q.wait_ge(e.sem["std_ready"], e.next("std_ready"))
    rstd = take_view(m, E_SQ, S)
    e.link(v.reciprocal(rstd, take_view(m, E_STD, S)))
    for c in range(4):
        e.tt(conv[:, c, :], conv[:, c, :], rstd, ALU.mult).then_inc(e.sem["ln_ready"], 1)
    for c in range(4):
        e.q.wait_ge(e.sem["c_act_ready"], e.next("c_act_ready"))
        e.halves(m.hhi[:, 4 + c, :], m.hlo[:, 4 + c, :], conv[:, c, :]).then_inc(e.sem["cat_ready"], 1)
    e.lo(4)
    e.out_in()


def odd_vector(e, m):
    v = e.v
    pad = 3
    w = pad + S
    rec = take_view(m, O_REC, 8 * w, "p (h s) -> p h s", h=8)
    xc = take_view(m, O_XC, 8 * S, "p (h s) -> p h s", h=8)
    e.link(v.memset(rec[:, :, 0:pad], 0.0))
    for i in range(4):
        e.lo()
        v.tensor_copy(rec[:, 2 * i:2 * i + 2, pad:], e.vb()[:, :].rearrange("p (i s) -> p i s", i=2)).then_inc(e.sem["vbank_free"], 1)
    e.q.wait_ge(e.sem["vbank_free"], e.nv)
    n0 = e.seen.get("lru_tap", 0)
    for j in range(4):
        for h in range(8):
            wc = e.col("lru_conv_w", j * 8 + h)
            if j == 0:
                ins = e.ts(xc[:, h, :], rec[:, h, 0:S], wc, ALU.mult, e.col("lru_conv_b", h), ALU.add)
            else:
                e.q.wait_ge(e.sem["lru_tap"], j * 8 + h - 7)
                ins = e.stt(xc[:, h, :], rec[:, h, j:j + S], wc, xc[:, h, :], ALU.mult, ALU.add)
            ins.then_inc(e.sem["lru_tap"], 1)
    e.q.wait_ge(e.sem["lru_tap"], 32)
    for _ in range(4):
        e.lo()
        e.q.wait_ge(e.sem["gate_ready"], e.next("gate_ready"))
    for h in range(8):
        e.halves(m.hhi[:, h, :], m.hlo[:, h, :], xc[:, h, :]).then_inc(e.sem["xc_ready"], 1)
    e.lo()
    r = take_view(m, O_R, 8 * S, "p (h s) -> p h s", h=8)
    i_ = take_view(m, O_REC, 8 * S, "p (h s) -> p h s", h=8)
    gate = take_view(m, O_GATE, 8 * S, "p (h s) -> p h s", h=8)
    e.q.wait_ge(e.sem["ri_ready"], e.next("ri_ready", 8))
    for h in range(8):
        e.tt(xc[:, h, :], xc[:, h, :], i_[:, h, :], ALU.mult).then_inc(e.sem["ix_ready"], 1)
    e.q.wait_ge(e.sem["ix_ready"], e.next("ix_ready", 8))
    for h in range(8):
        e.q.wait_ge(e.sem["a_ready"], e.next("a_ready"))
        tmp = take_view(m, TMP2, S)
        e.link(e.tt(tmp, r[:, h, :], r[:, h, :], ALU.mult))
        e.stt(i_[:, h, :], tmp, 1.0, i_[:, h, :], ALU.add, ALU.mult).then_inc(e.sem["b2_ready"], 1)
        e.q.wait_ge(e.sem["b2_ready"], e.next("b2_ready"))
    for h in range(8):
        e.q.wait_ge(e.sem["b_ready"], e.next("b_ready"))
        e.link(e.tt(xc[:, h, :], xc[:, h, :], i_[:, h, :], ALU.mult))
        e.link(v.tensor_tensor_scan(i_[:, h, :], r[:, h, :], xc[:, h, :], 0.0, ALU.mult, ALU.add))
        e.link(e.tt(gate[:, h, :], gate[:, h, :], i_[:, h, :], ALU.mult))
        e.halves(m.hhi[:, h, :], m.hlo[:, h, :], gate[:, h, :]).then_inc(e.sem["cat_ready"], 1)
    e.lo(4)
    e.out_in()


def mix_vector(e, m, layer):
    v = e.v
    lat = take_view(m, M_QKT, 1024)
    sq = take_view(m, M_QKT + 1024, 3 * S)
    e.lo()
    v.tensor_copy(lat[:, 0:512], e.vb()[:, :]).then_inc(e.sem["vbank_free"], 1)
    e.q.wait_ge(e.sem["vbank_free"], e.nv)
    e.lo()
    v.tensor_copy(lat[:, 512:832], e.vb()[:, 0:320]).then_inc(e.sem["vbank_free"], 1)
    e.q.wait_ge(e.sem["vbank_free"], e.nv)
    e.tt(sq, lat[:, 0:768], lat[:, 0:768], ALU.mult).then_inc(e.sem["squares_ready"], 1)
    kpe = lat[:, 768:832].rearrange("p (t f) -> p t f", t=NT)
    cos, sin = m.rope[:, 0, :, :], m.rope[:, 1, :, :]
    tmp = [take_view(m, M_OT + 256 * i, 256) for i in range(4)]
    small_tmp = [t[:, 0:32].rearrange("p (t f) -> p t f", t=NT) for t in tmp]
    rope(e, kpe[:, :, 0:16], kpe[:, :, 16:32], cos, sin, small_tmp)
    e.q.wait_ge(e.sem["std_ready"], e.next("std_ready"))
    std = take_view(m, M_QKT + 1792, 512)
    e.link(v.reciprocal(std, std))
    for i in range(3):
        t = lat[:, i * S:(i + 1) * S]
        gain = e.col("mla_q_norm_2", 2 * layer + i) if i < 2 else e.col("mla_kv_norm_2", layer)
        e.link(e.stt(t, t, gain, std[:, (i // 2) * S:(i // 2 + 1) * S], ALU.mult, ALU.mult))
        e.link(e.halves(m.ahi[:, i, :], m.alo[:, i, :], t))
    e.marker().then_inc(e.sem["latents_ready"], 1)
    e.q.wait_ge(e.sem["latents_ready"], e.next("latents_ready"))
    q_tok = take_view(m, M_QTOK, NT * 768, "p (t h d) -> p t h d", t=NT, h=8)
    k_tok = take_view(m, M_KTOK, NT * 768, "p (t h d) -> p t h d", t=NT, h=8)
    v_tok = take_view(m, M_VTOK, NT * 512, "p (t h d) -> p t h d", t=NT, h=8)
    e.lo()
    for t in range(NT):
        for half in range(2):
            v.tensor_copy(q_tok[:, t, 4 * half:4 * half + 4, :],
                                 e.vb()[:, 0:384].rearrange("p (h d) -> p h d", h=4)).then_inc(e.sem["vbank_free"], 1)
    e.q.wait_ge(e.sem["vbank_free"], e.nv)
    e.lo()
    for t in range(NT):
        e.link(v.tensor_copy(k_tok[:, t, :, 64:96], kpe[:, t:t + 1, :].to_broadcast([P, 8, 32])))
    for t in range(NT):
        for half in range(2):
            kv = e.vb()[:, :].rearrange("p (h d) -> p h d", h=4)
            hs = slice(4 * half, 4 * half + 4)
            e.link(v.tensor_copy(k_tok[:, t, hs, 0:64], kv[:, :, 0:64]))
            v.tensor_copy(v_tok[:, t, hs, :], kv[:, :, 64:128]).then_inc(e.sem["vbank_free"], 1)
    e.q.wait_ge(e.sem["vbank_free"], e.nv)
    e.q.wait_ge(e.sem["qk_gain"], e.next("qk_gain", 32))
    for t in range(NT):
        tmp8 = [x[:, 0:128].rearrange("p (h f) -> p h f", h=8) for x in tmp]
        wide = [x[:, t:t + 1, :].to_broadcast([P, 8, 16]) for x in (cos, sin)]
        rope(e, q_tok[:, t, :, 64:80], q_tok[:, t, :, 80:96], *wide, tmp8)
    scratch = take_view(m, M_QKT + 1024, 1536)
    for i, at in enumerate((M_QTOK, M_KTOK)):
        flat = take_view(m, at, 1536)
        heads = flat.rearrange("p (h d) -> p h d", d=96)
        e.link(e.tt(scratch, flat, flat, ALU.mult))
        v.reduce_sum(small(m, SSQ, 16), scratch.rearrange("p (h d) -> p h d", d=96), AX.X).then_inc(e.sem["qk_sums"], 1)
        e.link(e.tt(heads, heads, m.qkgain[:, i:i + 1, :].to_broadcast([P, 16, 96]), ALU.mult))
        e.q.wait_ge(e.sem["std_ready"], e.next("std_ready"))
        e.link(v.reciprocal(small(m, RSQ, 16), small(m, RSQ, 16)))
        e.link(e.tt(heads, heads, small(m, RSQ, 16).unsqueeze(2).to_broadcast([P, 16, 96]), ALU.mult))
    e.marker().then_inc(e.sem["normed_qk"], 1)
    e.q.wait_ge(e.sem["normed_qk"], e.next("normed_qk"))
    for i in range(6):
        e.lo()
        v.tensor_copy(take_view(m, M_SB + 512 * i, 512), e.vb()[:, :]).then_inc(e.sem["vbank_free"], 1)
    e.q.wait_ge(e.sem["vbank_free"], e.nv)
    ck = take_view(m, M_CK, 1024)
    sq = take_view(m, M_OT, 1024)
    e.tt(sq, ck, ck, ALU.mult).then_inc(e.sem["squares_ready"], 1)
    std = take_view(m, M_OT + 1024, 1024)
    for i, name in enumerate(("ck_q_qknorm_2", "ck_k_qknorm_2")):
        s, t = std[:, i * 512:(i + 1) * 512], ck[:, i * 512:(i + 1) * 512]
        e.q.wait_ge(e.sem["std_ready"], e.next("std_ready"))
        e.link(v.reciprocal(s, s))
        e.link(e.stt(t, t, e.col(name, layer), s, ALU.mult, ALU.mult))
    e.marker().then_inc(e.sem["band_ready"], 1)
    e.q.wait_ge(e.sem["band_ready"], e.next("band_ready"))

    def outs(base):
        def copy(bank, pair):
            v.tensor_copy(take_view(m, M_OT + (base + pair) * S, S), bank).then_inc(e.sem["outs_taken"], 1)
            e.q.wait_ge(e.sem["outs_taken"], e.pair + 1)
        return copy

    e.attention(range(8), "plain", float(96 ** -0.5), outs(2), chunked=True)
    e.attention(range(4), "stick", 0.125, outs(0))
    e.q.wait_ge(e.sem["bias_loaded"], e.next("bias_loaded", 16))
    bias = take_view(m, M_BIAS, 4 * S, "p (h s) -> p h s", h=4)
    e.attention(range(4), "plain", 0.125, outs(6), bias=bias, chunked=True)
    ot = take_view(m, M_OT, 8 * S, "p (k s) -> p k s", k=8)
    e.tt(take_view(m, M_QKT, 8 * S), take_view(m, M_OT, 8 * S), take_view(m, M_OT, 8 * S), ALU.mult).then_inc(e.sem["squares_ready"], 1)
    e.q.wait_ge(e.sem["std_ready"], e.next("std_ready"))
    std = take_view(m, M_QTOK, 3 * S)
    e.link(v.reciprocal(std, std))
    gain = ada_gain(e, m)
    for k in range(8):
        g = 0 if k < 2 else 2 if k < 6 else 1
        e.link(e.stt(ot[:, k, :], ot[:, k, :], e.col("group_out_norm_2", 8 * layer + k), std[:, g * S:(g + 1) * S],
                     ALU.mult, ALU.mult))
        e.halves(m.hhi[:, k, :], m.hlo[:, k, :], ot[:, k, :]).then_inc(e.sem["cat_ready"], 1)
    e.lo(4)
    e.out_in(gain)


def rope(e, x1, x2, cos, sin, tmp):
    e.link(e.tt(tmp[0], x1, cos, ALU.mult))
    e.link(e.tt(tmp[1], x2, sin, ALU.mult))
    e.link(e.tt(tmp[2], x2, cos, ALU.mult))
    e.link(e.tt(tmp[3], x1, sin, ALU.mult))
    e.link(e.tt(x1, tmp[0], tmp[1], ALU.subtract))
    e.link(e.tt(x2, tmp[2], tmp[3], ALU.add))



NAMES = ['x', 'norm_ffn1', 'ffn1_wg', 'ffn1_wu', 'ffn1_wd', 'norm_mix', 'norm_ffn2', 'ffn2_wg', 'ffn2_wu', 'ffn2_wd',
         'rel_bias', 'even_w_in', 'attn_sinks', 'conv_b_w', 'conv_b_b', 'conv_ln_g', 'conv_ln_b', 'even_w_out',
         'odd_w_in', 'lru_conv_w', 'lru_conv_b', 'gate_a_w', 'gate_a_b', 'gate_x_w', 'gate_x_b', 'lru_lambda',
         'odd_w_out', 'norm_final', 'c_2', 'positions_2', 'ada_w_2', 'ada_b_2', 'norm_mix_2', 'norm_ffn_2', 'w_in_2',
         'mla_q_norm_2', 'w_q_up_2', 'mla_kv_norm_2', 'w_kv_up_2', 'mla_q_qknorm_2', 'mla_k_qknorm_2',
         'ck_q_qknorm_2', 'ck_k_qknorm_2', 'ck_rel_bias_2', 'group_out_norm_2', 'w_out_2', 'ffn_w_gate_2',
         'ffn_w_up_2', 'ffn_w_down_2', 'moe_router_2', 'moe_w_gate_2', 'moe_w_up_2', 'moe_w_down_2']


def shape_constants():
    distance = LOOK - np.arange(TOEP)
    n = np.maximum(distance, 0)
    nf = np.maximum(n, 16).astype(np.float32)
    large = 16 + (np.log(nf / np.float32(16)) / np.float32(np.log(128 / 16)) * np.float32(16)).astype(np.int32)
    bucket = np.where(n < 16, n, np.minimum(large, 31))
    bucket = np.where((distance >= 0) & (distance < 128), bucket, 32)
    onehot = (np.arange(33)[:, None] == bucket[None, :]).astype(np.float32)
    inv_freq = np.float32(10000.0) ** (-np.arange(0, 32, 2, dtype=np.float32) / np.float32(32))
    return {"bucket_onehot": onehot, "inv_freq": inv_freq.astype(np.float32)[None, :]}


def kernel(**inputs):
    import concourse.bacc as bacc
    from concourse.bass_utils import run_bass_kernel_spmd

    nc = bacc.Bacc("TRN2", target_bir_lowering=False, num_devices=1)
    arrays, aps = {}, {}
    given = {name: np.ascontiguousarray(inputs[name]) for name in NAMES}
    constants = shape_constants()
    for name, array in [*given.items(), *constants.items()]:
        arrays[name + "_dram"] = array
        aps[name] = nc.dram_tensor(name + "_dram", array.shape, mybir.dt.from_np(array.dtype),
                                   kind="ExternalInput").ap()
    out = nc.dram_tensor("out_dram", (1, S, D), F32, kind="ExternalOutput").ap()
    build(nc, aps, out, {name: aps[name] for name in constants})
    result = run_bass_kernel_spmd(nc, [arrays], core_ids=[0])
    return result.results[0]["out_dram"]
```

```python
from contextlib import ExitStack, contextmanager

import numpy as np
import concourse.bass as bass
from concourse import mybir

F32 = mybir.dt.float32
F32R = mybir.dt.float32r
I32 = mybir.dt.int32
ALU = mybir.AluOpType
ACT = mybir.ActivationFunctionType
AX = mybir.AxisListType

P = 128
S = 256
NT = S // P
D = 1024
KT = D // P
FF = 2816
FC = 256
STEPS = FF // FC
N_EXPERTS = 8
NEG = -1e30
PIECE = 2048
N_RAW = 3
N_HL = 6
AHEAD = 3
LOOK = 255
TOEP = 384

XN = 4096
SIL, PROD, YACC, GATES = 6144, 6656, 7168, 9216
TMP4 = 6144
MOD, GATE_IN, GAIN_AT, TMP = 8192, 10240, 11264, 12288
ROUTE = 11264
SCORES, PROBT = 11264, 12032
ROWS_AT, REL_AT, ONEHOT_AT, CKROW_AT, REV_AT, CKOUT_AT = 8192, 8576, 8704, 9088, 9472, 9856
INVF_AT, ANG_AT, LAM_AT = 10240, 10304, 10496
E_GP, E_KV, E_SQ, E_STD, E_CONV, E_QT, E_BIAS = 4096, 5240, 6144, 6400, 7168, 8192, 9216
O_REC, O_GATE, O_XC, O_R, TMP2 = 4096, 6168, 8216, 10264, 12312
M_QTOK, M_KTOK, M_VTOK, M_QKT, M_OT, M_BIAS = 0, 1536, 3072, 4096, 8192, 10240
M_SB = M_OT + 2 * S
M_CK = M_QTOK
STICK_Z, STICK_L = M_QKT + 1024, M_QKT + 2560
M_SQ = M_OT + 2 * S

COLUMN_SIZES = (("norm_ffn1", 16), ("norm_mix", 16), ("norm_ffn2", 16), ("conv_b_b", 4), ("conv_ln_g", 4),
                    ("conv_ln_b", 4), ("lru_conv_b", 8), ("gate_a_b", 8), ("gate_x_b", 8), ("lru_lambda", 8),
                    ("lru_conv_w", 32), ("conv_b_w", 124), ("norm_mix_2", 16), ("norm_ffn_2", 16),
                    ("mla_q_norm_2", 4), ("mla_kv_norm_2", 2), ("group_out_norm_2", 16),
                    ("ck_q_qknorm_2", 2), ("ck_k_qknorm_2", 2), ("c_2", 8))
COLS = {name: sum(n for _, n in COLUMN_SIZES[:i]) for i, (name, _) in enumerate(COLUMN_SIZES)}
N_COLS = sum(n for _, n in COLUMN_SIZES)
ROW_TILES = (("norm_ffn1", "norm_mix", "norm_ffn2", "conv_b_b", "conv_ln_g", "conv_ln_b", "lru_conv_b",
              "gate_a_b", "gate_x_b", "lru_lambda", "lru_conv_w"),
             ("conv_b_w",),
             ("norm_mix_2", "norm_ffn_2", "mla_q_norm_2", "mla_kv_norm_2", "group_out_norm_2",
              "ck_q_qknorm_2", "ck_k_qknorm_2", "c_2"))


class Semaphores:

    def __init__(self, nc, ctx):
        self.nc, self.ctx, self.by_name = nc, ctx, {}

    def __getitem__(self, name):
        if name not in self.by_name:
            self.by_name[name] = self.ctx.enter_context(self.nc.semaphore(name))
        return self.by_name[name]


class Engine:

    def __init__(self, queue, sem, name):
        self.q, self.sem, self.own = queue, sem, "own_" + name
        self.seen = {}
        self.it, self.per = None, {}

    def next(self, name, n=1):
        self.seen[name] = self.seen.get(name, 0) + n
        per = self.per.get(name, 0)
        assert self.it is None or per, name
        return self.at(self.seen[name], per)

    def following(self, name):
        return self.seen.get(name, 0) + 1

    def at(self, value, per):
        assert value > 0
        return value if self.it is None or not per else self.it * per + value

    def link(self, instruction):
        instruction.then_inc(self.sem[self.own], 1)
        self.q.wait_ge(self.sem[self.own], self.next(self.own))

    @contextmanager
    def loop(self, iterations, per):
        before = dict(self.seen)
        with self.q.Fori(0, iterations) as it:
            self.it, self.per = it, per
            yield it
        self.it, self.per = None, {}
        for name, n in per.items():
            assert self.seen.get(name, 0) - before.get(name, 0) == n, name
            self.seen[name] += n * (iterations - 1)


def layout(nc, ctx):
    class M:
        pass
    m = M()

    def sb(name, free, dt=F32):
        t = ctx.enter_context(nc.sbuf_tensor(name, [P, free], dt))
        return t

    m.raw = sb("w_raw", N_RAW * PIECE)
    m.whi = sb("w_hi", N_HL * PIECE, F32R)
    m.wlo = sb("w_lo", N_HL * PIECE, F32R)
    m.x = sb("x_resid", NT * D)[:, :].rearrange("p (t d) -> p t d", t=NT)
    m.hhi = sb("h_hi", KT * S, F32R)[:, :].rearrange("p (k s) -> p k s", k=KT)
    m.hlo = sb("h_lo", KT * S, F32R)[:, :].rearrange("p (k s) -> p k s", k=KT)
    m.ahi = sb("act_hi", 4 * S, F32R)[:, :].rearrange("p (f s) -> p f s", f=4)
    m.alo = sb("act_lo", 4 * S, F32R)[:, :].rearrange("p (f s) -> p f s", f=4)
    m.ident = sb("ident", P)
    m.ones = sb("ones", P)
    m.cols = sb("cols", N_COLS)
    m.strict = sb("strict", P)
    m.blocks = sb("blocks", P)
    m.small = sb("small", 208)
    m.pos = sb("positions", NT, I32)
    m.rope = sb("rope_cs", 2 * NT * 16)[:, :].rearrange("p (c t f) -> p c t f", c=2, t=NT)
    m.qkgain = sb("qk_gain", 2 * 96)[:, :].rearrange("p (c f) -> p c f", c=2)
    m.arena = sb("arena", ARENA)
    m.banks = [ctx.enter_context(nc.psum_tensor(f"bank{i}", [P, 512], F32)) for i in range(8)]
    return m


ARENA = 12800


def take_view(m, at, n, pattern=None, **sizes):
    v = m.arena[:, at:at + n]
    return v if pattern is None else v.rearrange(pattern, **sizes)


def small(m, at, n=1):
    return m.small[:, at:at + n]


SS, STD, RSTD, EPS6, EPS5, CACT, SINK, HALF_PI = 0, 2, 4, 6, 7, 8, 16, 24
NM, DEN, ES, RDEN, MX = 26, 30, 34, 38, 42
SHC, GSC, LRUC = 48, 56, 64
SSQ, RSQ, TRI = 80, 112, 144
POOL_CONSTS = 8
ROWS_LOADS = len(COLUMN_SIZES) + 2



def ffn_order(n):
    out = [("gate", 0), ("up", 0)]
    for s in range(n - 1):
        out += [("gate", s + 1), ("up", s + 1), ("down", s)]
    return out + [("down", n - 1)]


def stream(a):
    pieces = []

    def columns(w, c, n=FC, at=0):
        kt = w.shape[0] // P
        src = w.rearrange("(k p) n -> p k n", p=P)[:, :, c:c + n]
        return lambda raw: raw[:, at:at + kt * n].rearrange("p (k n) -> p k n", k=kt), src

    def rows(w, r):
        src = w[r:r + 2 * P, :].rearrange("(k p) n -> p k n", p=P)
        return lambda raw: raw.rearrange("p (k n) -> p k n", k=2), src

    def head_columns(w, h, j):
        src = w.rearrange("(k p) n -> p k n", p=P)[:, :, 64 * h:64 * h + 64]
        return lambda raw: raw.rearrange("p (k n) -> p k n", k=KT)[:, :, 64 * j:64 * j + 64], src

    def head_rows(w, h, kt, half):
        return lambda raw: raw[64 * half:64 * half + 64, kt * D:(kt + 1) * D], w[64 * h:64 * h + 64, :]

    def gates(w, at):
        return lambda raw: raw[:, at:at + D].rearrange("p (h j) -> p h j", h=8), w.rearrange("h i j -> i h j")

    def ffn(tag, n):
        for kind, s in ffn_order(n):
            pieces.append((tag, kind, s))

    def plain(*loads):
        pieces.append(("plain", list(loads), None))

    ffn("ffn1_0", STEPS)
    w = a["even_w_in"][0]
    for i in range(2):
        plain(columns(w, 768 + FC * i))
        plain(columns(w, 1280 + FC * i))
    plain(columns(w, 512))
    for i in range(2):
        plain(*[head_columns(w, h, j) for j, h in enumerate((2 * i, 2 * i + 4, 2 * i + 1, 2 * i + 5))])
    w = a["even_w_out"][0]
    for i in range(2):
        plain(*[head_rows(w, 2 * i + kt + 4 * half, kt, half) for kt in range(2) for half in range(2)])
    for i in range(2):
        plain(rows(w, 512 + 256 * i))
    ffn("ffn2_0", STEPS)
    ffn("ffn1_1", STEPS)
    w = a["odd_w_in"][0]
    for i in range(4):
        plain(columns(w, D + FC * i))
    for i in range(4):
        plain(columns(w, FC * i))
    plain(gates(a["gate_a_w"][0], 0), gates(a["gate_x_w"][0], D))
    for i in range(4):
        plain(rows(a["odd_w_out"][0], 256 * i))
    ffn("ffn2_1", STEPS)
    for layer in range(2):
        w = a["w_in_2"][layer]
        plain(columns(w, 768))
        plain(columns(w, 1024, 160))
        for c in (0, 256, 512):
            plain(columns(w, c))
        plain(columns(a["w_q_up_2"][layer], 0, 768))
        plain(columns(a["w_kv_up_2"][layer], 0, D))
        for c in (1184, 1440, 1696):
            plain(columns(w, c))
        for i in range(4):
            plain(rows(a["w_out_2"][layer], 256 * i))
        if layer == 0:
            ffn("dense", STEPS)
        else:
            plain(columns(a["moe_router_2"][0], 0, N_EXPERTS))
            ffn("moe", N_EXPERTS * STEPS)
    return pieces


def arrivals(pieces):
    at, out = [0] * N_RAW, []
    for n, piece in enumerate(pieces):
        at[n % N_RAW] += 16 * (len(piece[1]) if piece[0] == "plain" else 1)
        out.append(at[n % N_RAW])
    return out



class Split:

    def __init__(self, eng, m, arrive):
        self.e, self.m, self.arrive, self.n = eng, m, arrive, 0

    def next_hi(self, nc):
        n, m, e = self.n, self.m, self.e
        if n >= len(self.arrive):
            return
        e.q.wait_ge(e.sem[f"raw_filled{n % N_RAW}"], e.at(self.arrive[n], 16 * (6 // N_RAW)))
        if n >= N_HL:
            e.q.wait_ge(e.sem["piece_used"], e.at(n - N_HL + 1, 6))
        raw = m.raw[:, n % N_RAW * PIECE:(n % N_RAW + 1) * PIECE]
        hi = m.whi[:, n % N_HL * PIECE:(n % N_HL + 1) * PIECE]
        nc.scalar.activation(hi, raw, ACT.Copy).then_inc(e.sem["piece_hi"], 1)
        self.n += 1

    def next_lo(self, nc):
        n, m, e = self.n, self.m, self.e
        if n >= len(self.arrive):
            return
        e.q.wait_ge(e.sem["piece_hi"], e.at(n + 1, 6))
        raw = m.raw[:, n % N_RAW * PIECE:(n % N_RAW + 1) * PIECE]
        hi = m.whi[:, n % N_HL * PIECE:(n % N_HL + 1) * PIECE]
        lo = m.wlo[:, n % N_HL * PIECE:(n % N_HL + 1) * PIECE]
        nc.vector.tensor_tensor(lo, raw, hi.bitcast(F32), ALU.subtract).then_inc(e.sem["piece_lo"], 1)
        self.n += 1


def build(nc, a, out, consts):
    x_in = a["x"][0].rearrange("(t p) d -> p t d", p=P)
    out_v = out[0].rearrange("(t p) d -> p t d", p=P)
    ada_sums = nc.dram_tensor("ada_sums", (12, P, D), F32, kind="Internal").ap()
    toep_rows = nc.dram_tensor("toeplitz_rows", (16, TOEP), F32, kind="Internal").ap()
    toep_copies = nc.dram_tensor("toeplitz_copies", (P, 16 * TOEP), F32, kind="Internal").ap()
    pieces = stream(a)
    arrive = arrivals(pieces)
    ffn_w = {
        "ffn1_0": (a["ffn1_wg"][0], a["ffn1_wu"][0], a["ffn1_wd"][0]),
        "ffn2_0": (a["ffn2_wg"][0], a["ffn2_wu"][0], a["ffn2_wd"][0]),
        "ffn1_1": (a["ffn1_wg"][1], a["ffn1_wu"][1], a["ffn1_wd"][1]),
        "ffn2_1": (a["ffn2_wg"][1], a["ffn2_wu"][1], a["ffn2_wd"][1]),
        "dense": (a["ffn_w_gate_2"][0], a["ffn_w_up_2"][0], a["ffn_w_down_2"][0]),
    }

    ctx = ExitStack()
    with ctx:
        sems = Semaphores(nc, ctx)
        m = layout(nc, ctx)
        block = ctx.enter_context(nc.Block())

        @block.sync
        def _(queue):
            load_program(nc, Engine(queue, sems, "sync"), m, a, x_in, out_v, consts, pieces, ffn_w)

        @block.gpsimd
        def _(queue):
            pool_program(nc, Engine(queue, sems, "gpsimd"), m, a, ada_sums)

        @block.scalar
        def _(queue):
            scalar_program(nc, Scalar(nc, queue, sems, m, arrive), a, consts, ada_sums, toep_rows, toep_copies)

        @block.vector
        def _(queue):
            vector_program(nc, Vector(nc, queue, sems, m, arrive), consts)

        @block.tensor
        def _(queue):
            tensor_program(nc, Tensor(nc, queue, sems, m), m)


def pool_program(nc, e, m, a, ada_sums):
    g = nc.gpsimd
    e.link(g.memset(m.ident[:, :], 0.0))
    g.memset(m.ones[:, :], 1.0).then_inc(e.sem["pool_const"], 1)
    e.link(g.memset(m.strict[:, :], 1.0))
    e.link(g.memset(m.blocks[:, :], 0.0))
    tri = small(m, TRI, 64)
    e.link(g.memset(tri, 1.0))
    g.memset(small(m, EPS6), 1e-6).then_inc(e.sem["pool_const"], 1)
    g.memset(small(m, EPS5), 1e-5).then_inc(e.sem["pool_const"], 1)
    g.affine_select(out=m.ident[:, :], in_=m.ident[:, :], compare_op=ALU.not_equal, fill=1.0, base=0,
                          pattern=[[-1, P]], channel_multiplier=1).then_inc(e.sem["pool_const"], 1)
    g.affine_select(out=m.strict[:, :], in_=m.strict[:, :], compare_op=ALU.is_gt, fill=0.0, base=0,
                          pattern=[[-1, P]], channel_multiplier=1).then_inc(e.sem["pool_const"], 1)
    t3 = tri.rearrange("p (e j) -> p e j", e=8)
    g.affine_select(out=t3, in_=t3, compare_op=ALU.is_gt, fill=0.0, base=0,
                          pattern=[[1, 8], [-1, 8]], channel_multiplier=0).then_inc(e.sem["pool_const"], 1)
    e.q.wait_ge(e.sem["pool_const"], e.next("pool_const", POOL_CONSTS - 2))
    for b in range(2):
        g.memset(m.blocks[64 * b:64 * b + 64, 64 * b:64 * b + 64], 1.0).then_inc(e.sem["pool_const"], 1)
        e.q.wait_ge(e.sem["pool_const"], e.next("pool_const"))

    ring = [take_view(m, b * D, D) for b in range(2)]
    acc, tmp = take_view(m, 2 * D, D), take_view(m, 3 * D, D)
    e.q.wait_ge(e.sem["c_ready"], e.next("c_ready"))
    for layer in range(2):
        w = a["ada_w_2"][layer].rearrange("(k p) n -> p k n", p=P)
        bias = a["ada_b_2"][layer:layer + 1, :]
        for v in range(6):
            for k in range(2):
                g.dma_start(ring[k], w[:, k, v * D:(v + 1) * D]).then_inc(e.sem[f"ada_w_loaded{k}"], 16)
            if layer or v:
                e.q.wait_ge(e.sem["ada_stored"], e.next("ada_stored", 16))
            e.link(g.memset(acc, 0.0))
            g.dma_start(acc[0:1, :], bias[:, v * D:(v + 1) * D]).then_inc(e.sem["ada_b_loaded"], 16)
            e.q.wait_ge(e.sem["ada_b_loaded"], e.next("ada_b_loaded", 16))
            for k in range(KT):
                e.q.wait_ge(e.sem[f"ada_w_loaded{k % 2}"], e.next(f"ada_w_loaded{k % 2}", 16))
                e.link(g.tensor_scalar(tmp, ring[k % 2], small(m, CACT + k), None, ALU.mult))
                if k + 2 < KT:
                    g.dma_start(ring[k % 2], w[:, k + 2, v * D:(v + 1) * D]).then_inc(e.sem[f"ada_w_loaded{k % 2}"], 16)
                e.link(g.tensor_tensor(acc, acc, tmp, ALU.add))
            g.dma_start(ada_sums[layer * 6 + v], acc).then_inc(e.sem["ada_stored"], 16)
    e.q.wait_ge(e.sem["ada_stored"], e.next("ada_stored", 16))



def load_program(nc, e, m, a, x_in, out_v, consts, pieces, ffn_w):
    nc.sync.dma_start(m.x, x_in).then_inc(e.sem["x_loaded"], 16)
    n = 0

    def slot():
        nonlocal n
        if n >= N_RAW:
            e.q.wait_ge(e.sem["piece_lo"], e.at(n - N_RAW + 1, PER[0]))
        raw = m.raw[:, n % N_RAW * PIECE:(n % N_RAW + 1) * PIECE]
        name = f"raw_filled{n % N_RAW}"
        n += 1
        return raw, name

    PER = [0]

    def ffn_columns(w, k0, c):
        raw, name = slot()
        nc.sync.dma_start(raw.rearrange("p (k n) -> p k n", k=KT), w[:, k0, c]).then_inc(e.sem[name], 16)

    def ffn_rows(w, k0):
        raw, name = slot()
        nc.sync.dma_start(raw.rearrange("p (k n) -> p k n", k=2), w[:, k0, :]).then_inc(e.sem[name], 16)

    def ffn(wg, wu, wd):
        nonlocal n
        wg, wu, wd = (w.rearrange("(k p) n -> p k n", p=P) for w in (wg, wu, wd))
        every = slice(0, KT)
        for w in (wg, wu):
            ffn_columns(w, every, slice(0, FC))

        def step(s, at):
            for w in (wg, wu):
                ffn_columns(w, every, bass.ds(s * FC + at * FC + FC, FC))
            ffn_rows(wd, bass.ds(s * 2 + at * 2, 2))
        step(0, 0)
        step(1, 0)
        PER[0] = 6
        with e.loop((STEPS - 3) // 2, {}) as it:
            for i in range(2):
                step(it * 2, 2 + i)
        PER[0] = 0
        n += 6 * ((STEPS - 3) // 2 - 1)
        ffn_rows(wd, slice(2 * STEPS - 2, 2 * STEPS))

    def moe(wg, wu, wd):
        nonlocal n
        wg, wu, wd = (w.rearrange("e (k p) n -> p (e k) n", p=P) for w in (wg, wu, wd))
        for w in (wg, wu):
            ffn_columns(w, slice(0, KT), slice(0, FC))

        def step(pair, s, last=False):
            if not last:
                x, c = divmod(s + 1, STEPS)
                for w in (wg, wu):
                    ffn_columns(w, bass.ds(pair * (2 * KT) + x * KT, KT), slice(c * FC, (c + 1) * FC))
            x, c = divmod(s, STEPS)
            kf = FF // P
            ffn_rows(wd, bass.ds(pair * (2 * kf) + (x * kf + 2 * c), 2))
        pairs = N_EXPERTS // 2
        PER[0] = 3 * 2 * STEPS
        with e.loop(pairs - 1, {}) as it:
            for s in range(2 * STEPS):
                step(it, s)
        PER[0] = 0
        n += 3 * 2 * STEPS * (pairs - 2)
        for s in range(2 * STEPS):
            step(pairs - 1, s, last=s == 2 * STEPS - 1)

    done = set()
    for piece in pieces:
        if piece[0] == "plain":
            raw, name = slot()
            for dst, src in piece[1]:
                nc.sync.dma_start(dst(raw), src).then_inc(e.sem[name], 16)
        elif piece[0] not in done:
            done.add(piece[0])
            if piece[0] == "moe":
                moe(a["moe_w_gate_2"][0], a["moe_w_up_2"][0], a["moe_w_down_2"][0])
            else:
                ffn(*ffn_w[piece[0]])
    e.q.wait_ge(e.sem["x_ready_out"], e.next("x_ready_out"))
    nc.sync.dma_start(out_v, m.x).then_inc(e.sem["out_stored"], 16)
    e.q.wait_ge(e.sem["out_stored"], e.next("out_stored", 16))



class Tensor(Engine):

    def __init__(self, nc, queue, sem, m):
        super().__init__(queue, sem, "tensor")
        self.nc, self.m = nc, m
        self.n = 0
        self.unsaid = 0
        self.j = 0
        self.y = 0
        self.v = 0
        self.exps = 0
        self.taken = 0
        self.outs = 0
        self.pair = 0

    def mm(self, out, l, r, start=True, stop=True):
        return self.nc.tensor.matmul(out, l, r, start=start, stop=stop)

    def mm3(self, out, l, r, start, stop):
        first = self.mm(out, l[0], r[0], start, False)
        if self.unsaid:
            first.then_inc(self.sem["piece_used"], 1)
            self.unsaid -= 1
        self.mm(out, l[0], r[1], False, False)
        return self.mm(out, l[1], r[0], False, stop)

    def transpose(self, out, in_):
        rows = in_.shape[0]
        return self.nc.tensor.transpose(out, in_, self.m.ident[0:rows, 0:rows])

    def piece(self):
        n, m = self.n, self.m
        self.q.wait_ge(self.sem["piece_lo"], self.at(n + 1, 6))
        self.n += 1
        at = n % N_HL * PIECE
        return m.whi[:, at:at + PIECE], m.wlo[:, at:at + PIECE]

    def used(self):
        self.unsaid += 1

    def vbank(self):
        if self.v >= 4:
            self.q.wait_ge(self.sem["vbank_free"], self.v - 3)
        self.v += 1
        return self.m.banks[(self.v - 1) % 4]

    def emptied(self):
        self.q.wait_ge(self.sem["vbank_free"], self.v)

    def gate_up(self, first=False):
        m = self.m
        w0, w1 = self.piece(), self.piece()
        for f in range(2):
            if self.j >= 4:
                self.q.wait_ge(self.sem["gu_free"], self.at(self.j - 3, 4))
            bank = m.banks[self.j % 4]
            self.j += 1
            for i, w in enumerate((w0, w1)):
                for k in range(KT):
                    if first and f == 0 and i == 0:
                        self.q.wait_ge(self.sem["hT_ready"], self.next("hT_ready"))
                    at = k * FC + f * P
                    last = self.mm3(bank[:, i * S:(i + 1) * S], tuple(h[:, at:at + P] for h in w),
                                    (m.hhi[:, k, :], m.hlo[:, k, :]), k == 0, k == KT - 1)
                if i == 0 and f == 1:
                    self.used()
            last.then_inc(self.sem["gu_ready"], 1)
        self.used()

    def down(self):
        m = self.m
        w = self.piece()
        step = self.y // 4
        self.q.wait_ge(self.sem["act_ready"], self.next("act_ready", 2))
        for t in range(NT):
            for half in range(2):
                b = self.y % 4
                if self.y >= 4:
                    self.q.wait_ge(self.sem["y_free"], self.at(self.y - 3, 8))
                self.y += 1
                for f in range(2):
                    fa = step % 2 * 2 + f
                    at = f * D + half * 512
                    last = self.mm3(m.banks[4 + b][:, :],
                                    (m.ahi[:, fa, t * P:(t + 1) * P], m.alo[:, fa, t * P:(t + 1) * P]),
                                    tuple(h[:, at:at + 512] for h in w), f == 0, f == 1)
                last.then_inc(self.sem["y_ready"], 1)
        self.used()

    def ffn(self, n, peel=0, first=True):
        self.emptied()
        self.gate_up(first)
        for _ in range(peel):
            self.gate_up()
            self.down()
        turns = (n - 1 - peel) // 2
        n0, j0, y0 = self.n, self.j, self.y
        with self.loop(turns, {"act_ready": 4}):
            for _ in range(2):
                self.gate_up()
                self.down()
        self.n, self.j, self.y = n0 + 6 * turns, j0 + 4 * turns, y0 + 8 * turns
        for _ in range((n - 1 - peel) % 2):
            self.gate_up()
            self.down()
        self.down()

    def norm(self):
        m = self.m
        xn = take_view(m, XN, NT * D, "p (t d) -> p t d", t=NT)
        self.q.wait_ge(self.sem["xn_ready"], self.next("xn_ready", NT))
        for kk in range(KT // 2):
            bank = self.vbank()
            for k in range(2):
                for t in range(NT):
                    at = (2 * k + t) * P
                    last = self.transpose(bank[:, at:at + P], xn[:, t, (2 * kk + k) * P:(2 * kk + k + 1) * P])
            last.then_inc(self.sem["vbank_ready"], 1)

    def features(self, w, tiles, bank, n=FC):
        m = self.m
        for i, (c, width) in enumerate(tiles):
            for k in range(KT):
                last = self.mm3(bank[0:width, i * S:(i + 1) * S], tuple(h[:, k * n + c:k * n + c + width] for h in w),
                                (m.hhi[:, k, :], m.hlo[:, k, :]), k == 0, k == KT - 1)
        return last

    def tokens(self, w, t, c, width, out, n=FC, hT=None, kt=KT):
        m = self.m
        hT = hT or (m.hhi, m.hlo)
        for k in range(kt):
            last = self.mm3(out, tuple(h[:, k, t * P:(t + 1) * P] for h in hT),
                            tuple(h[:, k * n + c:k * n + c + width] for h in w), k == 0, k == kt - 1)
        return last

    def out_projection(self, i, banks):
        m = self.m
        w = self.piece()
        for kt in range(2):
            k = 2 * i + kt
            for t in range(NT):
                for half in range(2):
                    at = kt * D + half * 512
                    last = self.mm3(banks[2 * t + half][:, :],
                                    (m.hhi[:, k, t * P:(t + 1) * P], m.hlo[:, k, t * P:(t + 1) * P]),
                                    tuple(h[:, at:at + 512] for h in w), k == 0, k == KT - 1)
                    if k == KT - 1:
                        last.then_inc(self.sem["vbank_ready"], 1)
        self.used()

    def turn(self, s, bank):
        self.transpose(bank[:, 0:P], s[:, 0:P])
        self.transpose(bank[:, P:2 * P], s[:, P:2 * P])
        self.transpose(bank[:, 2 * P:3 * P], s[:, 2 * P:3 * P]).then_inc(self.sem["probs_turned"], 1)

    def output(self, value, half, bank):
        m = self.m
        pt = take_view(m, PROBT + self.outs % 2 * TOEP, TOEP)
        self.outs += 1
        if half == 0 and self.pair >= 2:
            self.q.wait_ge(self.sem["outs_taken"], self.pair - 1)
        self.q.wait_ge(self.sem["probT_ready"], self.next("probT_ready"))
        o = bank[64 * half:64 * half + 64, :]
        self.mm(o[:, 0:P], value(0), pt[:, 0:P])
        self.mm(o[:, P:2 * P], value(0), pt[:, P:2 * P], True, False)
        last = self.mm(o[:, P:2 * P], value(1), pt[:, 2 * P:3 * P], False, True)
        if half:
            last.then_inc(self.sem["outs_ready"], 1)
            self.pair += 1

    def scores(self, q, k, bank):
        self.mm(bank[:, 0:P], q[:, 0:P], k[:, 0:P])
        self.mm(bank[:, P:3 * P], q[:, P:2 * P], k[:, :]).then_inc(self.sem["scores_ready"], 1)

    def attention(self, heads):
        m = self.m
        pair0 = self.pair

        def scores(i):
            q, k, _, _, kind = heads[i]
            if i >= 2:
                if heads[i - 2][4] == "direct":
                    self.q.wait_ge(self.sem["exp_ready"], self.exps + i - 1)
                else:
                    self.taken += 1
                    self.q.wait_ge(self.sem["scores_taken"], self.taken)
            if kind == "band" and heads[i - 1][4] != "band":
                self.q.wait_ge(self.sem["band_ready"], self.next("band_ready"))
            self.scores(q, k, m.banks[i % 2])

        def output(i):
            _, _, value, half, _ = heads[i]
            self.output(value, half, m.banks[4 + (self.pair - pair0) % 2])

        scores(0)
        scores(1)
        for i in range(len(heads)):
            if i + 2 < len(heads):
                scores(i + 2)
            self.q.wait_ge(self.sem["probs_ready"], self.next("probs_ready"))
            self.turn(take_view(m, SCORES + i % 2 * TOEP, TOEP), m.banks[2 + i % 2])
            if i:
                output(i - 1)
        output(len(heads) - 1)
        self.exps += len(heads)
        self.taken += sum(h[4] != "direct" for h in heads[-2:])

    def sums(self, out, operands):
        for i, op in enumerate(operands):
            last = self.mm(out, self.m.ones[:, :], op, i == 0, i == len(operands) - 1)
        return last

    def ada_columns(self):
        m = self.m
        self.q.wait_ge(self.sem["ada_in"], self.next("ada_in", 32))
        for v in range(2):
            for k in range(KT):
                last = self.mm(m.banks[7][:, v * KT + k:v * KT + k + 1], take_view(m, MOD + v * D + k * P, P),
                               m.ones[:, 0:1])
        last.then_inc(self.sem["mean_ready"], 1)

    def ada_gain(self):
        m = self.m
        self.q.wait_ge(self.sem["ada_gate_in"], self.next("ada_gate_in", 16))
        for half in range(2):
            bank = self.vbank()
            self.mm(bank[:, :], m.ones[:, :], take_view(m, GATE_IN + half * 512, 512)).then_inc(
                self.sem["vbank_ready"], 1)


def tensor_program(nc, e, m):
    sem = e.sem
    e.q.wait_ge(sem["pool_const"], e.next("pool_const", POOL_CONSTS))
    e.q.wait_ge(sem["rows_loaded"], ROWS_LOADS * 16)
    for i, names in enumerate(ROW_TILES):
        rows = sum(n for name, n in COLUMN_SIZES if name in names)
        e.transpose(e.vbank()[:, 0:rows], take_view(m, ROWS_AT + i * P, P)[0:rows, :]).then_inc(sem["vbank_ready"], 1)
    e.q.wait_ge(sem["relbias_ready"], e.next("relbias_ready"))
    e.mm(e.vbank()[0:8, 0:TOEP], take_view(m, REL_AT, 8)[0:33, :],
         take_view(m, ONEHOT_AT, TOEP)[0:33, :]).then_inc(sem["vbank_ready"], 1)

    e.norm()
    e.ffn(STEPS, peel=2)
    e.norm()
    even_tensor(e, m)
    e.norm()
    e.ffn(STEPS)
    e.norm()
    e.ffn(STEPS)
    e.norm()
    odd_tensor(e, m)
    e.norm()
    e.ffn(STEPS)
    for layer in range(2):
        e.ada_columns()
        e.norm()
        mix_tensor(e, m, layer)
        e.ada_columns()
        e.norm()
        if layer == 0:
            e.ffn(STEPS)
        else:
            w, bank = e.piece(), e.vbank()
            e.q.wait_ge(sem["hT_ready"], e.next("hT_ready", KT))
            for t in range(NT):
                last = e.tokens(w, t, 0, N_EXPERTS, bank[:, t * 8:t * 8 + 8], n=N_EXPERTS)
            last.then_inc(sem["vbank_ready"], 1)
            e.used()
            e.ffn(N_EXPERTS * STEPS, first=False)
        e.ada_gain()


def even_tensor(e, m):
    sem = e.sem
    e.emptied()
    e.gate_up(True)
    e.gate_up()
    e.q.wait_ge(sem["gu_free"], e.j)
    w, bank = e.piece(), e.vbank()
    e.features(w, [(0, P)], bank)
    for t in range(NT):
        last = e.tokens(w, t, P, P, bank[:, S + t * P:S + (t + 1) * P])
    last.then_inc(sem["vbank_ready"], 1)
    e.used()
    for _ in range(2):
        e.features(e.piece(), [(0, P), (P, P)], e.vbank()).then_inc(sem["vbank_ready"], 1)
        e.used()
    e.emptied()
    qt = take_view(m, E_QT, 4 * S, "p (i s) -> p i s", i=4)
    kt = take_view(m, E_KV, S)
    v = take_view(m, E_KV + S, S, "p (t d) -> p t d", t=NT)
    heads = []
    for i in range(4):
        for b in range(2):
            rows = slice(64 * b, 64 * b + 64)
            heads.append((qt[rows, i, :], kt[rows, :], lambda t, b=b: v[:, t, 64 * b:64 * b + 64], b, "sink"))
    e.attention(heads)
    conv = take_view(m, E_CONV, 4 * S, "p (c s) -> p c s", c=4)
    sq = take_view(m, E_SQ, 4 * S, "p (c s) -> p c s", c=4)
    e.q.wait_ge(sem["conv_ready"], e.next("conv_ready"))
    e.sums(m.banks[7][:, 0:S], [conv[:, c, :] for c in range(4)]).then_inc(sem["mean_ready"], 1)
    e.q.wait_ge(sem["squares_ready"], e.next("squares_ready"))
    e.sums(m.banks[6][:, 0:S], [sq[:, c, :] for c in range(4)]).then_inc(sem["var_ready"], 1)
    banks = [e.vbank() for _ in range(4)]
    e.q.wait_ge(sem["outs_taken"], e.pair)
    for i in range(4):
        if i >= 2:
            e.q.wait_ge(sem["cat_ready"], e.next("cat_ready", 2))
        e.out_projection(i, banks)


def odd_tensor(e, m):
    sem = e.sem
    e.q.wait_ge(sem["hT_ready"], e.next("hT_ready", KT))
    for _ in range(4):
        e.features(e.piece(), [(0, P), (P, P)], e.vbank()).then_inc(sem["vbank_ready"], 1)
        e.used()
    for i in range(4):
        w = e.piece()
        if i >= 2:
            e.q.wait_ge(sem["gate_ready"], i - 1)
        e.features(w, [(0, P), (P, P)], m.banks[4 + i % 2]).then_inc(sem["gate_mm_ready"], 1)
        e.used()
    w = e.piece()
    for h in range(KT):
        e.q.wait_ge(sem["xc_ready"], e.next("xc_ready"))
        if h >= 2:
            e.q.wait_ge(sem["ri_ready"], h - 1)
        for i in range(2):
            at = i * D + h * P
            last = e.mm3(m.banks[4 + h % 2][:, i * S:(i + 1) * S], tuple(x[:, at:at + P] for x in w),
                         (m.hhi[:, h, :], m.hlo[:, h, :]), True, True)
        last.then_inc(sem["ri_mm_ready"], 1)
    e.used()
    banks = [e.vbank() for _ in range(4)]
    for i in range(4):
        e.q.wait_ge(sem["cat_ready"], e.next("cat_ready", 2))
        e.out_projection(i, banks)


def mix_tensor(e, m, layer):
    sem = e.sem
    e.q.wait_ge(sem["hT_ready"], e.next("hT_ready", KT))
    e.features(e.piece(), [(0, P), (P, P)], e.vbank()).then_inc(sem["vbank_ready"], 1)
    e.used()
    w, bank = e.piece(), e.vbank()
    e.features(w, [(0, P)], bank, n=160)
    for t in range(NT):
        last = e.tokens(w, t, P, 32, bank[:, S + 32 * t:S + 32 * t + 32], n=160)
    last.then_inc(sem["vbank_ready"], 1)
    e.used()
    for i in range(3):
        w, bank = e.piece(), e.vbank()
        if i < 2:
            last = e.features(w, [(0, P), (P, P)], bank)
        else:
            for t in range(NT):
                last = e.tokens(w, t, 0, FC, bank[:, t * FC:(t + 1) * FC])
        last.then_inc(sem["vbank_ready"], 1)
        e.used()
    sq = take_view(m, SCORES, 3 * S, "p (c s) -> p c s", c=3)
    e.q.wait_ge(sem["squares_ready"], e.next("squares_ready"))
    e.sums(m.banks[6][:, 0:S], [sq[:, 0, :], sq[:, 1, :]])
    e.sums(m.banks[6][:, S:2 * S], [sq[:, 2, :]]).then_inc(sem["var_ready"], 1)
    qt, kt, vals = (take_view(m, M_SB + 512 * i, 512, "p (i s) -> p i s", i=2) for i in range(3))
    e.q.wait_ge(sem["stick_in"], e.next("stick_in"))
    for h in range(3):
        rows = slice(64 * (h % 2), 64 * (h % 2) + 64)
        e.scores(qt[rows, h // 2, :], kt[rows, h // 2, :], m.banks[(4, 5, 7)[h]])
    w = e.piece()
    e.q.wait_ge(sem["latents_ready"], e.next("latents_ready"))
    e.scores(qt[64:128, 1, :], kt[64:128, 1, :], m.banks[6])
    for t in range(NT):
        for half in range(2):
            e.tokens(w, t, 384 * half, 384, e.vbank()[:, 0:384], n=768, hT=(m.ahi[:, 0:2, :], m.alo[:, 0:2, :]),
                     kt=2).then_inc(sem["vbank_ready"], 1)
    e.used()
    w = e.piece()
    for t in range(NT):
        for half in range(2):
            e.tokens(w, t, 512 * half, 512, e.vbank()[:, :], n=D, hT=(m.ahi[:, 2:3, :], m.alo[:, 2:3, :]),
                     kt=1).then_inc(sem["vbank_ready"], 1)
    e.used()
    for i in range(2):
        e.features(e.piece(), [(0, P), (P, P)], e.vbank()).then_inc(sem["vbank_ready"], 1)
        e.used()
    e.q.wait_ge(sem["probs_ready"], e.next("probs_ready"))
    for h in range(5):
        if h < 4:
            e.turn(take_view(m, STICK_Z + h * TOEP, TOEP), m.banks[4 + h % 2])
        if h:
            e.output(lambda t: vals[:, t, 64 * (h - 1):64 * h], (h - 1) % 2, m.banks[6 + (h - 1) // 2])
    e.exps += 1
    w, bank = e.piece(), e.vbank()
    for t in range(NT):
        last = e.tokens(w, t, 0, FC, bank[:, t * FC:(t + 1) * FC])
    last.then_inc(sem["vbank_ready"], 1)
    e.used()
    sq = take_view(m, SCORES, 2 * S, "p (k s) -> p k s", k=2)
    e.q.wait_ge(sem["squares_ready"], e.next("squares_ready"))
    e.sums(m.banks[6][:, 0:S], [sq[:, 0, :], sq[:, 1, :]]).then_inc(sem["var_ready"], 1)
    for i, at in enumerate((M_QTOK, M_KTOK)):
        tok = take_view(m, at, NT * 768, "p (t h d) -> p t h d", t=NT, h=8)
        e.q.wait_ge(sem["normed_qk"], e.next("normed_qk"))
        for j in range(4):
            bank = m.banks[4 + j % 2]
            if 4 * i + j >= 2:
                e.q.wait_ge(sem["qkT_ready"], 8 * layer + 4 * i + j - 1)
            for b in range(2):
                for t in range(NT):
                    last = e.transpose(bank[0:96, b * S + t * P:b * S + (t + 1) * P], tok[:, t, 2 * j + b, :])
            last.then_inc(sem["qk_turned"], 1)
    sq = take_view(m, M_SQ, 4 * S)
    e.q.wait_ge(sem["squares_ready"], e.next("squares_ready"))
    for i in range(2):
        e.mm(m.banks[6 + i][:, :], m.blocks[:, :], sq[:, i * 512:(i + 1) * 512]).then_inc(sem["var_ready"], 1)
    e.emptied()
    e.q.wait_ge(sem["qkT_ready"], e.next("qkT_ready", 8))
    e.q.wait_ge(sem["chunk_rows"], e.next("chunk_rows", 16))
    qkt = take_view(m, M_QKT, 8 * 512, "p (h c s) -> p h c s", h=8, c=2)
    v_tok = take_view(m, M_VTOK, NT * 512, "p (t h d) -> p t h d", t=NT, h=8)
    heads = [(qkt[0:98, h, 0, :], qkt[0:98, h, 1, :], lambda t, h=h: v_tok[:, t, h, :], h % 2, "direct")
             for h in range(8)]
    qt, kt, v = (take_view(m, M_CK + 512 * i, 512, "p (i s) -> p i s", i=2) for i in range(3))
    for h in range(4):
        rows = slice(64 * (h % 2), 64 * (h % 2) + 64)
        heads.append((qt[rows, h // 2, :], kt[rows, h // 2, :], lambda t, h=h: v[:, t, 64 * h:64 * h + 64],
                      h % 2, "band"))
    e.attention(heads)
    banks = [e.vbank() for _ in range(4)]
    e.q.wait_ge(sem["cat_ready"], e.next("cat_ready", 2))
    e.out_projection(0, banks)
    sq = take_view(m, M_QKT, 6 * S, "p (k s) -> p k s", k=6)
    e.q.wait_ge(sem["squares_ready"], e.next("squares_ready"))
    e.sums(m.banks[6][:, 0:S], [sq[:, k, :] for k in range(4)])
    e.sums(m.banks[6][:, S:2 * S], [sq[:, k, :] for k in (4, 5)]).then_inc(sem["var_ready"], 1)
    e.q.wait_ge(sem["ada_gate_in"], e.next("ada_gate_in", 16))
    e.q.wait_ge(sem["outs_taken"], e.pair)
    for half in range(2):
        e.mm(m.banks[4 + half][:, :], m.ones[:, :], take_view(m, GATE_IN + half * 512, 512)).then_inc(
            sem["gain_mm_ready"], 1)
    for i in range(1, 4):
        e.q.wait_ge(sem["cat_ready"], e.next("cat_ready", 2))
        e.out_projection(i, banks)



class Scalar(Engine):
    def __init__(self, nc, queue, sems, m, arrive):
        super().__init__(queue, sems, "scalar")
        self.nc, self.m = nc, m
        self.split = Split(self, m, arrive)
        self.j = 0
        self.turned = 0

    def hi(self, n=1):
        for _ in range(n):
            self.split.next_hi(self.nc)

    def act(self, out, in_, f, bias=0.0, scale=1.0, accum=None):
        return self.nc.scalar.activation(out, in_, f, bias=bias, scale=scale, accum_out=accum)

    def load(self, dst, src):
        return self.nc.scalar.dma_start(dst, src)

    def norm(self, first=False):
        m = self.m
        self.q.wait_ge(self.sem["x_loaded"], self.next("x_loaded", 16)) if first else self.q.wait_ge(self.sem["x_ready"], self.next("x_ready"))
        for t in range(NT):
            self.link(self.act(take_view(m, XN + t * D, D), m.x[:, t, :], ACT.Square, accum=small(m, SS + t)))
        self.act(small(m, STD, 2), small(m, SS, 2), ACT.Sqrt, bias=small(m, EPS6), scale=1.0 / D).then_inc(self.sem["std_ready"], 1)

    def gate(self, f, half):
        m = self.m
        self.q.wait_ge(self.sem["gu_ready"], self.next("gu_ready"))
        if self.j >= 2:
            self.q.wait_ge(self.sem["gu_free"], self.at(self.j - 1, 4))
        self.act(take_view(m, SIL + self.j % 2 * S, S), m.banks[self.j % 4][:, half * S:(half + 1) * S], f).then_inc(self.sem["gate_act"], 1)
        self.j += 1

    def step(self):
        self.hi()
        self.gate(ACT.Silu, 0)
        self.hi()
        self.gate(ACT.Silu, 0)
        self.hi()

    def ffn(self, n, peel=0):
        self.hi()
        self.gate(ACT.Silu, 0)
        self.hi()
        self.gate(ACT.Silu, 0)
        for _ in range(peel):
            self.step()
        turns = (n - 1 - peel) // 2
        n0, j0 = self.split.n, self.j
        with self.loop(turns, {"gu_ready": 4}):
            self.step()
            self.step()
        self.split.n, self.j = n0 + 6 * turns, j0 + 4 * turns
        for _ in range((n - 1 - peel) % 2):
            self.step()
        self.hi()

    def copy_turned(self, bank):
        self.q.wait_ge(self.sem["probs_turned"], self.next("probs_turned"))
        self.act(take_view(self.m, PROBT + self.turned % 2 * TOEP, TOEP), bank[:, 0:TOEP], ACT.Copy).then_inc(self.sem["probT_ready"], 1)
        self.turned += 1

    def attention(self, kinds, scale=1.0):
        m = self.m
        for i, kind in enumerate(kinds):
            p = i % 2
            s = take_view(m, SCORES + p * TOEP, TOEP)
            src = m.banks[p] if kind == "direct" else s
            by = scale if kind == "direct" else 1.0
            self.q.wait_ge(self.sem["max_ready"], self.next("max_ready"))
            nm, den = small(m, NM + 2 * p, 2), small(m, DEN + 2 * p, 2)
            if kind == "sink":
                hd = i // 2 + 4 * p
                self.link(self.act(small(m, ES + 2 * p, 2), nm, ACT.Exp, bias=small(m, SINK + hd)))
            self.link(self.act(s[:, 0:P], src[:, 0:P], ACT.Exp, bias=nm[:, 0:1], scale=by, accum=den[:, 0:1]))
            self.act(s[:, P:3 * P], src[:, P:3 * P], ACT.Exp, bias=nm[:, 1:2], scale=by, accum=den[:, 1:2]).then_inc(self.sem["exp_ready"], 1)
            if i:
                self.copy_turned(m.banks[2 + (i - 1) % 2])
        self.copy_turned(m.banks[2 + (len(kinds) - 1) % 2])

    def ada_in(self, layer, v, n, at):
        for i in range(n):
            self.load(take_view(self.m, at + i * D, D), self.sums[layer * 6 + v + i]).then_inc(self.sem["ada_gate_in" if n == 1 else "ada_in"], 16)


def broadcast(ap, n):
    return bass.AP(tensor=ap.tensor, offset=ap.offset, ap=[[0, P], [1, n]])


def scalar_program(nc, e, a, consts, ada_sums, toep, toep_copies):
    m = e.m
    e.sums = ada_sums
    for i, names in enumerate(ROW_TILES):
        at = 0
        for name, n in COLUMN_SIZES:
            if name not in names:
                continue
            dst = take_view(m, ROWS_AT + i * P, P)[at:at + n, :]
            src = a[name]
            if "qknorm" in name:
                e.load(dst[:, 0:64], src).then_inc(e.sem["rows_loaded"], 16)
                e.load(dst[:, 64:128], src).then_inc(e.sem["rows_loaded"], 16)
            else:
                while len(src.shape) > 2:
                    src = src.rearrange("a b c -> (a b) c")
                e.load(dst, src.rearrange("a (k f) -> (a k) f", f=P)).then_inc(e.sem["rows_loaded"], 16)
            at += n
    e.load(take_view(m, REL_AT, 8)[0:32, :], a["rel_bias"]).then_inc(e.sem["rel_loaded"], 16)
    e.load(take_view(m, ONEHOT_AT, TOEP)[0:33, :], consts["bucket_onehot"]).then_inc(e.sem["rel_loaded"], 16)
    e.load(take_view(m, CKROW_AT, 257)[0:8, :], a["ck_rel_bias_2"].rearrange("l h r -> (l h) r")).then_inc(e.sem["ck_loaded"], 16)
    e.load(small(m, SINK, 8), broadcast(a["attn_sinks"], 8)).then_inc(e.sem["misc_loaded"], 16)
    pos = a["positions_2"]
    with nc.allow_non_contiguous_dma(reason="one position for each token"):
        e.load(m.pos[:, :], bass.AP(tensor=pos.tensor, offset=pos.offset, ap=[[1, P], [P, NT]])).then_inc(e.sem["misc_loaded"], 16)
    e.load(take_view(m, INVF_AT, 16), broadcast(consts["inv_freq"], 16)).then_inc(e.sem["misc_loaded"], 16)

    e.hi(AHEAD)
    e.q.wait_ge(e.sem["pool_const"], e.next("pool_const", POOL_CONSTS))
    e.norm(first=True)
    e.q.wait_ge(e.sem["cols_ready"], e.next("cols_ready"))
    e.act(small(m, CACT, 8), m.cols[:, COLS["c_2"]:COLS["c_2"] + 8], ACT.Silu).then_inc(e.sem["c_ready"], 1)
    t = take_view(m, LAM_AT, 8)
    e.link(e.act(t, m.cols[:, COLS["lru_lambda"]:COLS["lru_lambda"] + 8], ACT.Abs))
    e.act(t, t, ACT.Exp, scale=-1.0).then_inc(e.sem["lam_exp"], 1)
    e.q.wait_ge(e.sem["angles_ready"], e.next("angles_ready"))
    r = take_view(m, ANG_AT + 64, 32)
    e.link(e.act(m.rope[:, 1, :, :].rearrange("p t f -> p (t f)"), r, ACT.Sin))
    e.act(m.rope[:, 0, :, :].rearrange("p t f -> p (t f)"), r, ACT.Sin, scale=0.5).then_inc(e.sem["sines_ready"], 1)
    e.q.wait_ge(e.sem["toep_rel"], e.next("toep_rel"))
    e.load(toep[0:8, :], take_view(m, REV_AT, TOEP)[0:8, :]).then_inc(e.sem["toep_stored"], 16)
    e.load(toep[8:16, :], take_view(m, CKOUT_AT, TOEP)[0:8, :]).then_inc(e.sem["toep_stored"], 16)
    e.q.wait_ge(e.sem["toep_stored"], e.next("toep_stored", 32))
    e.load(toep_copies, bass.AP(tensor=toep.tensor, offset=toep.offset, ap=[[0, P], [1, 16 * TOEP]])).then_inc(e.sem["toep_copied"], 16)

    e.ffn(STEPS, peel=2)
    e.norm()
    even_scalar(e, m, toep_copies)
    e.norm()
    e.ffn(STEPS)
    e.norm()
    e.ffn(STEPS)
    e.norm()
    odd_scalar(e, m)
    e.norm()
    e.ffn(STEPS)
    e.q.wait_ge(e.sem["x_ready"], e.following("x_ready"))
    e.load(take_view(m, GAIN_AT, D), broadcast(a["norm_final"], D)).then_inc(e.sem["final_gain"], 16)
    e.norm()
    for layer in range(2):
        e.q.wait_ge(e.sem["x_ready"], e.following("x_ready"))
        if layer == 0:
            e.q.wait_ge(e.sem["ada_stored"], e.next("ada_stored", 16 * 12))
        e.ada_in(layer, 0, 2, MOD)
        e.norm()
        mix_scalar(e, m, a, layer, toep_copies, bass.AP(tensor=consts["chunk_rows"].tensor, offset=consts["chunk_rows"].offset,
                                                        ap=[[2 * S, 2], [0, 8], [1, 2 * S]]))
        e.q.wait_ge(e.sem["x_ready"], e.following("x_ready"))
        e.ada_in(layer, 3, 2, MOD)
        e.norm()
        if layer == 1:
            e.hi()
            e.q.wait_ge(e.sem["logits_ready"], e.next("logits_ready"))
            r = take_view(m, ROUTE, 512)
            for t in range(NT):
                e.act(r[:, 32 + t * 8:40 + t * 8], r[:, t * 8:t * 8 + 8], ACT.Exp, bias=r[:, 48 + t:49 + t]).then_inc(e.sem["route_exp"], 1)
        e.ada_in(layer, 5, 1, GATE_IN)
        e.ffn(STEPS if layer == 0 else N_EXPERTS * STEPS)


def diagonals(copies, row, n):
    return bass.AP(tensor=copies.tensor, offset=copies.offset + row * TOEP + P - 1,
                   ap=[[16 * TOEP - 1, P], [TOEP, n], [1, S]])


def even_scalar(e, m, toep):
    e.q.wait_ge(e.sem["toep_copied"], e.next("toep_copied", 16))
    e.load(take_view(m, E_BIAS, 8 * S, "p (h s) -> p h s", h=8), diagonals(toep, 0, 8)).then_inc(e.sem["bias_loaded"], 16)
    for _ in range(2):
        e.hi(2)
        for _ in range(2):
            e.gate(ACT.Sigmoid, 1)
    e.hi(3)
    e.attention(["sink"] * 8)
    e.q.wait_ge(e.sem["var_ready"], e.next("var_ready"))
    e.act(take_view(m, E_STD, S), m.banks[6][:, 0:S], ACT.Sqrt, bias=small(m, EPS5), scale=1.0 / 512).then_inc(e.sem["std_ready"], 1)
    conv = take_view(m, E_CONV, 4 * S, "p (c s) -> p c s", c=4)
    for c in range(4):
        e.q.wait_ge(e.sem["ln_ready"], e.next("ln_ready"))
        col = lambda name: m.cols[:, COLS[name] + c:COLS[name] + c + 1]
        e.act(conv[:, c, :], conv[:, c, :], ACT.Silu, bias=col("conv_ln_b"), scale=col("conv_ln_g")).then_inc(e.sem["c_act_ready"], 1)
    e.hi(4)


def odd_scalar(e, m):
    e.hi(4)
    gate = take_view(m, O_GATE, 8 * S)
    for i in range(4):
        e.hi()
        e.q.wait_ge(e.sem["gate_mm_ready"], e.next("gate_mm_ready"))
        e.act(gate[:, i * 512:(i + 1) * 512], m.banks[4 + i % 2][:, :], ACT.Gelu_apprx_tanh).then_inc(e.sem["gate_ready"], 1)
    e.hi()
    r, i_ = take_view(m, O_R, 8 * S, "p (h s) -> p h s", h=8), take_view(m, O_REC, 8 * S, "p (h s) -> p h s", h=8)
    for h in range(8):
        e.q.wait_ge(e.sem["ri_mm_ready"], e.next("ri_mm_ready"))
        bank = m.banks[4 + h % 2]
        e.link(e.act(r[:, h, :], bank[:, 0:S], ACT.Sigmoid, bias=m.cols[:, COLS["gate_a_b"] + h:COLS["gate_a_b"] + h + 1]))
        e.act(i_[:, h, :], bank[:, S:2 * S], ACT.Sigmoid, bias=m.cols[:, COLS["gate_x_b"] + h:COLS["gate_x_b"] + h + 1]).then_inc(e.sem["ri_ready"], 1)
    for h in range(8):
        e.q.wait_ge(e.sem["ix_ready"], e.next("ix_ready"))
        e.link(e.act(i_[:, h, :], r[:, h, :], ACT.Tanh, scale=small(m, LRUC + 8 + h)))
        e.act(r[:, h, :], r[:, h, :], ACT.Exp, scale=small(m, LRUC + h)).then_inc(e.sem["a_ready"], 1)
    for h in range(8):
        e.q.wait_ge(e.sem["b2_ready"], e.next("b2_ready"))
        e.act(i_[:, h, :], i_[:, h, :], ACT.Sqrt).then_inc(e.sem["b_ready"], 1)
    e.hi(4)


def mix_scalar(e, m, a, layer, toep, chunk_rows):
    gains = m.qkgain
    e.load(gains[:, 0, :], broadcast(a["mla_q_qknorm_2"][layer:layer + 1, :], 96)).then_inc(e.sem["qk_gain"], 16)
    e.load(gains[:, 1, :], broadcast(a["mla_k_qknorm_2"][layer:layer + 1, :], 96)).then_inc(e.sem["qk_gain"], 16)
    e.hi(4)
    std = take_view(m, PROBT, 512)
    e.q.wait_ge(e.sem["var_ready"], e.next("var_ready"))
    e.link(e.act(std[:, 0:S], m.banks[6][:, 0:S], ACT.Sqrt, bias=small(m, EPS6), scale=1.0 / 256))
    e.act(std[:, S:2 * S], m.banks[6][:, S:2 * S], ACT.Sqrt, bias=small(m, EPS6), scale=1.0 / 128).then_inc(e.sem["std_ready"], 1)
    e.load(take_view(m, M_BIAS, 4 * S, "p (h s) -> p h s", h=4), diagonals(toep, 8 + 4 * layer, 4)).then_inc(e.sem["bias_loaded"], 16)
    z, l = take_view(m, STICK_Z, 4 * TOEP), take_view(m, STICK_L, 4 * TOEP)
    for h in range(4):
        at = slice(h * TOEP, (h + 1) * TOEP)
        e.q.wait_ge(e.sem["z_ready"], e.next("z_ready"))
        e.link(e.act(l[:, at], z[:, at], ACT.Abs))
    e.link(e.act(l, l, ACT.Exp, scale=-1.0))
    e.act(l, l, ACT.Ln, bias=1.0).then_inc(e.sem["log1p_ready"], 1)
    e.hi(3)
    e.q.wait_ge(e.sem["logw_ready"], e.next("logw_ready"))
    e.act(z, z, ACT.Exp).then_inc(e.sem["exp_ready"], 1)
    for h in range(4):
        e.copy_turned(m.banks[4 + h % 2])
    e.q.wait_ge(e.sem["qk_sums"], e.next("qk_sums"))
    e.act(small(m, RSQ, 32), small(m, SSQ, 32), ACT.Sqrt, bias=small(m, EPS6), scale=1.0 / 96).then_inc(e.sem["std_ready"], 1)
    e.q.wait_ge(e.sem["var_ready"], e.next("var_ready"))
    e.act(take_view(m, SCORES + 2 * S, S), m.banks[6][:, 0:S], ACT.Sqrt, bias=small(m, EPS6), scale=1.0 / 256).then_inc(e.sem["std_ready"], 1)
    qkt = take_view(m, M_QKT, 8 * 512, "p (h c s) -> p h c s", h=8, c=2)
    e.load(qkt[96:98, :, :, :].rearrange("p h c s -> p h (c s)"), chunk_rows).then_inc(e.sem["chunk_rows"], 16)
    for c in range(2):
        for j in range(4):
            e.q.wait_ge(e.sem["qk_turned"], e.next("qk_turned"))
            e.act(qkt[0:96, 2 * j:2 * j + 2, c, :], m.banks[4 + j % 2][0:96, :].rearrange("p (h s) -> p h s", h=2), ACT.Copy).then_inc(e.sem["qkT_ready"], 1)
    std = take_view(m, M_SQ, 4 * S)
    for i in range(2):
        e.q.wait_ge(e.sem["var_ready"], e.next("var_ready"))
        e.act(std[:, i * 512:(i + 1) * 512], m.banks[6 + i][:, :], ACT.Sqrt, bias=small(m, EPS6), scale=1.0 / 64).then_inc(e.sem["std_ready"], 1)
    e.hi(3)
    e.attention(["direct"] * 8 + ["band"] * 4, float(96 ** -0.5))
    e.ada_in(layer, 2, 1, GATE_IN)
    std = take_view(m, M_QTOK, 2 * S)
    e.q.wait_ge(e.sem["var_ready"], e.next("var_ready"))
    e.link(e.act(std[:, 0:S], m.banks[6][:, 0:S], ACT.Sqrt, bias=small(m, EPS6), scale=1.0 / 512))
    e.act(std[:, S:2 * S], m.banks[6][:, S:2 * S], ACT.Sqrt, bias=small(m, EPS6), scale=1.0 / 256).then_inc(e.sem["std_ready"], 1)
    for half in range(2):
        e.q.wait_ge(e.sem["gain_mm_ready"], e.next("gain_mm_ready"))
        e.act(take_view(m, GAIN_AT + half * 512, 512), m.banks[4 + half][:, :], ACT.Copy).then_inc(e.sem["gain_ready"], 1)
    e.hi(4)



class Vector(Engine):
    def __init__(self, nc, queue, sems, m, arrive):
        super().__init__(queue, sems, "vector")
        self.nc, self.m, self.v = nc, m, nc.vector
        self.split = Split(self, m, arrive)
        self.nv = 0
        self.j = 0
        self.f = 0
        self.y = 0
        self.turned = 0
        self.pair = 0

    def lo(self, n=1):
        for _ in range(n):
            self.split.next_lo(self.nc)

    def vb(self):
        self.q.wait_ge(self.sem["vbank_ready"], self.next("vbank_ready"))
        self.nv += 1
        return self.m.banks[(self.nv - 1) % 4]

    def col(self, name, i=0):
        return self.m.cols[:, COLS[name] + i:COLS[name] + i + 1]

    def tt(self, out, a, b, op):
        return self.v.tensor_tensor(out, a, b, op)

    def ts(self, out, a, s1, op, s2=None, op2=None):
        return self.v.tensor_scalar(out, a, s1, s2, op, op2) if op2 is not None else self.v.tensor_scalar(out, a, s1, None, op)

    def stt(self, out, a, s, b, op, op2):
        return self.v.scalar_tensor_tensor(out=out, in0=a, scalar=s, in1=b, op0=op, op1=op2)

    def normed(self, gain=None):
        m = self.m
        self.q.wait_ge(self.sem["std_ready"], self.next("std_ready"))
        self.link(self.v.reciprocal(small(m, RSTD, 2), small(m, STD, 2)))
        for t in range(NT):
            if gain is None:
                self.ts(take_view(m, XN + t * D, D), m.x[:, t, :], small(m, RSTD + t), ALU.mult).then_inc(self.sem["xn_ready"], 1)
            else:
                self.stt(m.x[:, t, :], m.x[:, t, :], small(m, RSTD + t), gain, ALU.mult, ALU.mult).then_inc(self.sem["own_vector"], 1)
        if gain is not None:
            self.q.wait_ge(self.sem["own_vector"], self.next("own_vector", NT))

    def norm(self, gain, shift=None):
        m = self.m
        self.normed()
        if shift is not None:
            self.ada_columns(gain)
            gain = m.small[:, GSC:GSC + 8]
        for kk in range(KT // 2):
            bank = self.vb()
            for i in range(2):
                k = 2 * kk + i
                g, src = gain[:, k:k + 1], bank[:, i * S:(i + 1) * S]
                if shift is None:
                    self.link(self.ts(m.hhi[:, k, :], src, g, ALU.mult))
                    self.stt(m.hlo[:, k, :], src, g, m.hhi[:, k, :].bitcast(F32), ALU.mult, ALU.subtract).then_inc(self.sem["hT_ready"], 1)
                else:
                    tmp = take_view(m, TMP + k % 2 * S, S)
                    self.link(self.ts(tmp, src, g, ALU.mult, small(m, SHC + k), ALU.add))
                    self.halves(m.hhi[:, k, :], m.hlo[:, k, :], tmp).then_inc(self.sem["hT_ready"], 1)
            self.v.tensor_copy(small(m, MX + 5), bank[:, 0:1]).then_inc(self.sem["vbank_free"], 1)
            self.q.wait_ge(self.sem["hT_ready"], self.next("hT_ready", 2))
            self.q.wait_ge(self.sem["vbank_free"], self.nv)

    def halves(self, hi, lo, src):
        self.link(self.v.tensor_copy(hi, src))
        ins = self.tt(lo, src, hi.bitcast(F32), ALU.subtract)
        return ins

    def ada_columns(self, gain):
        m = self.m
        self.q.wait_ge(self.sem["mean_ready"], self.next("mean_ready"))
        self.link(self.v.tensor_copy(m.small[:, SHC:SHC + 8], m.banks[7][:, 0:8]))
        self.link(self.stt(m.small[:, GSC:GSC + 8], m.banks[7][:, 8:16], 1.0, gain, ALU.add, ALU.mult))

    def gain(self, name, layer):
        at = COLS[name] + layer * 8
        return self.m.cols[:, at:at + 8]

    def act(self):
        m, j = self.m, self.j
        self.q.wait_ge(self.sem["gate_act"], self.next("gate_act"))
        prod = take_view(m, PROD + self.f % 2 * S, S)
        if self.f >= 2:
            self.q.wait_ge(self.sem["act_ready"], self.at(self.f - 1, 4))
        self.tt(prod, take_view(m, SIL + j % 2 * S, S), m.banks[j % 4][:, S:2 * S], ALU.mult).then_inc(self.sem["gu_free"], 1)
        self.q.wait_ge(self.sem["gu_free"], self.at(j + 1, 4))
        fa = self.f % 4
        self.link(self.v.tensor_copy(m.ahi[:, fa, :], prod))
        self.tt(m.alo[:, fa, :], prod, m.ahi[:, fa, :].bitcast(F32), ALU.subtract).then_inc(self.sem["act_ready"], 1)
        self.j += 1
        self.f += 1

    def y_in(self, scale, target, last=False):
        m = self.m
        for t in range(NT):
            for half in range(2):
                b = self.y % 4
                self.q.wait_ge(self.sem["y_ready"], self.next("y_ready"))
                if self.y >= 4:
                    self.q.wait_ge(self.sem["y_free"], self.at(self.y - 3, 8))
                dst = target[:, t, half * 512:(half + 1) * 512]
                self.stt(dst, m.banks[4 + b][:, :], scale(t), dst, ALU.mult, ALU.add).then_inc(self.sem["y_free"], 1)
                self.y += 1

    def ffn(self, n, scale, target, peel=0):
        def step(s):
            self.lo()
            self.act()
            self.lo()
            self.act()
            self.lo()
            self.y_in(lambda t: scale(s, t), target)
        self.lo()
        self.act()
        self.lo()
        self.act()
        for i in range(peel):
            step(i)
        turns = (n - 1 - peel) // 2
        n0, j0, f0, y0 = self.split.n, self.j, self.f, self.y
        with self.loop(turns, {"gate_act": 4, "own_vector": 4, "y_ready": 8}) as it:
            step(it * 2 + peel)
            step(it * 2 + (peel + 1))
        self.split.n, self.j, self.y = n0 + 6 * turns, j0 + 4 * turns, y0 + 8 * turns
        self.f = f0 + 4 * turns
        for i in range(peel + 2 * turns, n - 1):
            step(i)
        self.lo()
        self.y_in(lambda t: scale(n - 1, t), target)
        self.q.wait_ge(self.sem["y_free"], self.y)

    def ffn_half(self, peel=0):
        self.ffn(STEPS, lambda s, t: 0.5, self.m.x, peel)
        self.marker().then_inc(self.sem["x_ready"], 1)
        self.q.wait_ge(self.sem["x_ready"], self.next("x_ready"))

    def marker(self):
        return self.v.tensor_copy(small(self.m, MX + 4), small(self.m, EPS6))

    def out_in(self, gain=None):
        m = self.m
        for t in range(NT):
            for half in range(2):
                bank = self.vb()
                dst = m.x[:, t, half * 512:(half + 1) * 512]
                if gain is None:
                    self.tt(dst, bank[:, :], dst, ALU.add).then_inc(self.sem["vbank_free"], 1)
                else:
                    tmp = take_view(m, TMP4 + (2 * t + half) % 2 * 512, 512)
                    self.tt(tmp, bank[:, :], gain[:, half * 512:(half + 1) * 512], ALU.mult).then_inc(self.sem["vbank_free"], 1)
                    self.q.wait_ge(self.sem["vbank_free"], self.nv)
                    self.link(self.tt(dst, tmp, dst, ALU.add))
        self.q.wait_ge(self.sem["vbank_free"], self.nv)
        self.marker().then_inc(self.sem["x_ready"], 1)
        self.q.wait_ge(self.sem["x_ready"], self.next("x_ready"))

    def attention(self, heads, out, fill=lambda i: None):
        m, v = self.m, self.v
        pair0 = self.pair
        turned0 = self.turned

        def maxima(i):
            kind, scale, bias, sink = heads[i]
            p = i % 2
            s = take_view(m, SCORES + p * TOEP, TOEP)
            src = m.banks[p] if kind == "direct" else s
            self.q.wait_ge(self.sem["scores_ready"], self.next("scores_ready"))
            if kind != "direct":
                if i >= 2:
                    self.q.wait_ge(self.sem["probs_turned"], turned0 + i - 1)
                self.link(self.stt(s[:, 0:P], m.banks[p][:, 0:P], scale, bias[:, P:2 * P], ALU.mult, ALU.add))
                self.stt(s[:, P:3 * P], m.banks[p][:, P:3 * P], scale, bias[:, 0:S], ALU.mult, ALU.add).then_inc(self.sem["scores_taken"], 1)
                self.q.wait_ge(self.sem["scores_taken"], self.next("scores_taken"))
            mx, nm = small(m, MX + 2 * p, 2), small(m, NM + 2 * p, 2)
            v.reduce_max(mx[:, 0:1], src[:, 0:P], AX.X).then_inc(self.sem[self.own], 1)
            self.link(v.reduce_max(mx[:, 1:2], src[:, P:3 * P], AX.X))
            self.q.wait_ge(self.sem[self.own], self.next(self.own))
            if kind == "sink":
                self.ts(nm, mx, sink, ALU.max, -1.0, ALU.mult).then_inc(self.sem["max_ready"], 1)
            else:
                self.ts(nm, mx, -scale if kind == "direct" else -1.0, ALU.mult).then_inc(self.sem["max_ready"], 1)

        def normalise(i):
            p = i % 2
            s = take_view(m, SCORES + p * TOEP, TOEP)
            self.q.wait_ge(self.sem["exp_ready"], self.next("exp_ready"))
            den, rden = small(m, DEN + 2 * p, 2), small(m, RDEN + 2 * p, 2)
            if heads[i][0] == "sink":
                self.link(self.tt(den, den, small(m, ES + 2 * p, 2), ALU.add))
            self.link(v.reciprocal(rden, den))
            self.link(self.ts(s[:, 0:P], s[:, 0:P], rden[:, 0:1], ALU.mult))
            self.ts(s[:, P:3 * P], s[:, P:3 * P], rden[:, 1:2], ALU.mult).then_inc(self.sem["probs_ready"], 1)

        def outputs():
            self.q.wait_ge(self.sem["outs_ready"], self.next("outs_ready"))
            pair = self.pair - pair0
            self.pair += 1
            out(m.banks[4 + pair % 2][:, 0:S], pair)

        maxima(0)
        for i in range(len(heads)):
            if i + 1 < len(heads):
                maxima(i + 1)
            fill(i)
            normalise(i)
            fill(i)
            if i % 2 == 1 and i > 1:
                outputs()
        outputs()
        self.turned += len(heads)

    def stick(self):
        m, v = self.m, self.v
        z = take_view(m, STICK_Z, 4 * TOEP, "p (h s) -> p h s", h=4)
        l = take_view(m, STICK_L, 4 * TOEP, "p (h s) -> p h s", h=4)
        own = m.strict[:, :].unsqueeze(1).to_broadcast([P, 4, P])
        self.q.wait_ge(self.sem["log1p_ready"], self.next("log1p_ready"))
        self.link(self.stt(l, z, 0.0, l, ALU.max, ALU.add))
        for at in (0, 2 * P):
            self.tt(l[:, :, at:at + P], l[:, :, at:at + P], own, ALU.mult).then_inc(self.sem[self.own], 1)
        self.q.wait_ge(self.sem[self.own], self.next(self.own, 2))
        for h in range(4):
            for lo, hi in ((0, P), (P, 3 * P)):
                x = l[:, h, lo:hi][:, ::-1]
                v.tensor_tensor_scan(x, x, x, 0.0, ALU.add, ALU.bypass).then_inc(self.sem[self.own], 1)
        self.q.wait_ge(self.sem[self.own], self.next(self.own, 8))
        self.link(self.tt(z, z, l, ALU.subtract))
        for at in (0, 2 * P):
            self.tt(z[:, :, at:at + P], z[:, :, at:at + P], own, ALU.mult).then_inc(self.sem["logw_part"], 1)
        self.q.wait_ge(self.sem["logw_part"], self.next("logw_part", 2))
        self.marker().then_inc(self.sem["logw_ready"], 1)
        self.q.wait_ge(self.sem["logw_ready"], self.next("logw_ready"))

    def stick_masked(self):
        m = self.m
        z = take_view(m, STICK_Z, 4 * TOEP, "p (h s) -> p h s", h=4)
        own = m.strict[:, :].unsqueeze(1).to_broadcast([P, 4, P])
        self.q.wait_ge(self.sem["exp_ready"], self.next("exp_ready"))
        for at in (0, 2 * P):
            self.tt(z[:, :, at:at + P], z[:, :, at:at + P], own, ALU.mult).then_inc(self.sem[self.own], 1)
        self.q.wait_ge(self.sem[self.own], self.next(self.own, 2))
        self.marker().then_inc(self.sem["probs_ready"], 1)


def vector_program(nc, e, consts):
    m, v = e.m, e.v
    e.lo(AHEAD)
    e.q.wait_ge(e.sem["rel_loaded"], e.next("rel_loaded", 32))
    rel = take_view(m, REL_AT, 8)
    v.memset(rel[32:33, :], NEG).then_inc(e.sem["relbias_ready"], 1)
    e.q.wait_ge(e.sem["ck_loaded"], e.next("ck_loaded", 16))
    ck, rows = take_view(m, CKROW_AT, 257), take_view(m, CKOUT_AT, TOEP)
    e.link(v.tensor_copy(rows[0:8, 0:P - 1], ck[0:8, 256:257].to_broadcast([8, P - 1])))
    e.link(v.tensor_copy(rows[0:8, TOEP - 1:TOEP], ck[0:8, 0:1]))
    e.link(v.tensor_copy(rows[0:8, P - 1:TOEP - 1], ck[0:8, 1:257][:, ::-1]))
    at = 0
    for i, names in enumerate(ROW_TILES):
        n = sum(n for name, n in COLUMN_SIZES if name in names)
        v.tensor_copy(m.cols[:, at:at + n], e.vb()[:, 0:n]).then_inc(e.sem["vbank_free"], 1)
        at += n
    e.q.wait_ge(e.sem["vbank_free"], e.nv)
    e.marker().then_inc(e.sem["cols_ready"], 1)
    e.q.wait_ge(e.sem["cols_ready"], e.next("cols_ready"))
    v.tensor_copy(take_view(m, REV_AT, TOEP)[0:8, :], e.vb()[0:8, 0:TOEP]).then_inc(e.sem["vbank_free"], 1)
    e.q.wait_ge(e.sem["vbank_free"], e.nv)
    e.q.wait_ge(e.sem["misc_loaded"], e.next("misc_loaded", 48))
    ang = take_view(m, ANG_AT, 32, "p (t f) -> p t f", t=NT)
    turns, r, posf = (take_view(m, ANG_AT + 32 * i, 32) for i in (1, 2, 3))
    e.link(v.tensor_copy(posf[:, 0:NT], m.pos[:, :]))
    for t in range(NT):
        e.link(e.ts(ang[:, t, :], take_view(m, INVF_AT, 16), posf[:, t:t + 1], ALU.mult))
    flat = take_view(m, ANG_AT, 32)
    e.link(e.ts(turns, flat, float(1 / (2 * np.pi)), ALU.mult))
    e.link(e.ts(turns, turns, 12582912.0, ALU.add))
    e.link(e.ts(turns, turns, -12582912.0, ALU.add))
    c1 = 6.28125
    c2 = 2029 / 2**20
    c3 = float(2 * np.pi - c1 - c2)
    e.link(e.stt(r, turns, -c1, flat, ALU.mult, ALU.add))
    e.link(e.stt(r, turns, -c2, r, ALU.mult, ALU.add))
    e.link(e.stt(r, turns, -c3, r, ALU.mult, ALU.add))
    e.ts(r, r, 3.1415925, ALU.min, -3.1415925, ALU.max).then_inc(e.sem["angles_ready"], 1)
    e.q.wait_ge(e.sem["lam_exp"], e.next("lam_exp"))
    y, z, z2, acc = (take_view(m, LAM_AT + 8 * i, 8) for i in range(4))
    e.link(e.ts(z, y, 2.0, ALU.add))
    e.link(v.reciprocal(z, z))
    e.link(e.tt(z, z, y, ALU.mult))
    e.link(e.tt(z2, z, z, ALU.mult))
    e.link(v.memset(acc, 1.0 / 15))
    for k in (13, 11, 9, 7, 5, 3, 1):
        e.link(e.tt(acc, acc, z2, ALU.mult))
        e.link(e.ts(acc, acc, 1.0 / k, ALU.add))
    e.link(e.tt(acc, acc, z, ALU.mult))
    lam = m.cols[:, COLS["lru_lambda"]:COLS["lru_lambda"] + 8]
    e.link(e.ts(z, lam, 0.0, ALU.min, 8.0, ALU.mult))
    e.link(e.stt(small(m, LRUC, 8), acc, -16.0, z, ALU.mult, ALU.add))
    e.link(e.ts(small(m, LRUC + 8, 8), small(m, LRUC, 8), -1.0, ALU.mult))
    e.q.wait_ge(e.sem["sines_ready"], e.next("sines_ready"))
    cos = m.rope[:, 0, :, :].rearrange("p t f -> p (t f)")
    e.link(e.tt(cos, cos, cos, ALU.mult))
    e.link(e.ts(cos, cos, -2.0, ALU.mult, 1.0, ALU.add))
    e.marker().then_inc(e.sem["toep_rel"], 1)
    e.q.wait_ge(e.sem["toep_rel"], e.next("toep_rel"))

    e.norm(e.gain("norm_ffn1", 0))
    e.ffn_half(peel=2)
    e.norm(e.gain("norm_mix", 0))
    even_vector(e, m)
    e.norm(e.gain("norm_ffn2", 0))
    e.ffn_half()
    e.norm(e.gain("norm_ffn1", 1))
    e.ffn_half()
    e.norm(e.gain("norm_mix", 1))
    odd_vector(e, m)
    e.norm(e.gain("norm_ffn2", 1))
    e.ffn_half()
    e.q.wait_ge(e.sem["final_gain"], e.next("final_gain", 16))
    e.normed(take_view(m, GAIN_AT, D))
    e.marker().then_inc(e.sem["x_ready"], 1)
    e.q.wait_ge(e.sem["x_ready"], e.next("x_ready"))
    for layer in range(2):
        e.norm(e.gain("norm_mix_2", layer), True)
        mix_vector(e, m, layer)
        e.norm(e.gain("norm_ffn_2", layer), True)
        yacc = take_view(m, YACC, NT * D, "p (t d) -> p t d", t=NT)
        e.link(v.memset(yacc, 0.0))
        if layer == 0:
            e.ffn(STEPS, lambda s, t: 1.0, yacc)
        else:
            route(e, m)
            n = N_EXPERTS * STEPS
            gates = take_view(m, GATES, NT * n, "p (t s) -> p t s", t=NT)
            e.ffn(n, lambda s, t: gates[:, t, s:s + 1] if isinstance(s, int) else gates[:, t, bass.ds(s, 1)], yacc)
        gain = ada_gain(e, m)
        for t in range(NT):
            e.link(e.tt(yacc[:, t, :], yacc[:, t, :], gain, ALU.mult))
            e.link(e.tt(m.x[:, t, :], m.x[:, t, :], yacc[:, t, :], ALU.add))
        e.marker().then_inc(e.sem["x_ready" if layer == 0 else "x_ready_out"], 1)
        e.q.wait_ge(e.sem["x_ready" if layer == 0 else "x_ready_out"], e.next("x_ready" if layer == 0 else "x_ready_out"))


def ada_gain(e, m):
    gain = take_view(m, GAIN_AT, D)
    for half in range(2):
        e.v.tensor_copy(gain[:, half * 512:(half + 1) * 512], e.vb()[:, :]).then_inc(e.sem["vbank_free"], 1)
    e.q.wait_ge(e.sem["vbank_free"], e.nv)
    return gain


def route(e, m):
    v = e.v
    r = take_view(m, ROUTE, 512)
    logits = r[:, 0:16]
    e.lo()
    v.tensor_copy(logits, e.vb()[:, 0:16]).then_inc(e.sem["vbank_free"], 1)
    e.q.wait_ge(e.sem["vbank_free"], e.nv)
    for t in range(NT):
        e.link(v.reduce_max(r[:, 48 + t:49 + t], r[:, t * 8:t * 8 + 8], AX.X))
    e.link(e.ts(r[:, 48:50], r[:, 48:50], -1.0, ALU.mult))
    e.marker().then_inc(e.sem["logits_ready"], 1)
    e.q.wait_ge(e.sem["logits_ready"], e.next("logits_ready"))
    gates = take_view(m, GATES, NT * N_EXPERTS * STEPS, "p (t x s) -> p t x s", t=NT, x=N_EXPERTS)
    above, equal = (r[:, 64 + 64 * i:128 + 64 * i].rearrange("p (x j) -> p x j", x=8) for i in range(2))
    tri = m.small[:, TRI:TRI + 64].rearrange("p (x j) -> p x j", x=8)
    e.q.wait_ge(e.sem["route_exp"], e.next("route_exp", NT))
    for t in range(NT):
        l = r[:, t * 8:t * 8 + 8]
        lj = l.unsqueeze(1).to_broadcast([P, 8, 8])
        lx = l.unsqueeze(2).to_broadcast([P, 8, 8])
        e.link(e.tt(above, lj, lx, ALU.is_gt))
        e.link(e.tt(equal, lj, lx, ALU.is_equal))
        e.link(e.tt(equal, equal, tri, ALU.mult))
        e.link(e.tt(above, above, equal, ALU.add))
        rank = r[:, 192:200]
        e.link(v.reduce_sum(rank, above, AX.X))
        e.link(e.ts(rank, rank, 2.0, ALU.is_lt))
        ex = r[:, 32 + t * 8:40 + t * 8]
        e.link(e.tt(ex, ex, rank, ALU.mult))
        e.link(v.reduce_sum(r[:, 200:201], ex, AX.X))
        e.link(v.reciprocal(r[:, 200:201], r[:, 200:201]))
        e.link(e.ts(ex, ex, r[:, 200:201], ALU.mult))
        e.link(v.tensor_copy(gates[:, t, :, :], ex.unsqueeze(2).to_broadcast([P, N_EXPERTS, STEPS])))


def even_vector(e, m):
    v = e.v
    pad = 30
    gp = take_view(m, E_GP, 4 * (pad + S), "p (c s) -> p c s", c=4)
    conv = take_view(m, E_CONV, 4 * S, "p (c s) -> p c s", c=4)
    sq = take_view(m, E_SQ, 4 * S, "p (c s) -> p c s", c=4)
    e.link(v.memset(gp[:, :, 0:pad], 0.0))
    for i in range(4):
        if i % 2 == 0:
            e.lo(2)
        e.q.wait_ge(e.sem["gate_act"], e.next("gate_act"))
        e.tt(gp[:, i, pad:], take_view(m, SIL + e.j % 2 * S, S), m.banks[e.j % 4][:, 0:S], ALU.mult).then_inc(e.sem["gu_free"], 1)
        e.q.wait_ge(e.sem["gu_free"], e.j + 1)
        e.j += 1
    e.lo()
    v.tensor_copy(take_view(m, E_KV, 512), e.vb()[:, :]).then_inc(e.sem["vbank_free"], 1)
    for i in range(2):
        e.lo()
        v.tensor_copy(take_view(m, E_QT + 512 * i, 512), e.vb()[:, :]).then_inc(e.sem["vbank_free"], 1)
    e.q.wait_ge(e.sem["vbank_free"], e.nv)
    e.q.wait_ge(e.sem["bias_loaded"], e.next("bias_loaded", 16))

    taps = [(j, c) for j in range(31) for c in range(4)]
    at = [0]

    def some_taps(n=8):
        for _ in range(n):
            if at[0] == len(taps):
                return
            j, c = taps[at[0]]
            if at[0] >= 4:
                e.q.wait_ge(e.sem["conv_tap"], at[0] - 3)
            w = e.col("conv_b_w", j * 4 + c)
            if j == 0:
                ins = e.ts(conv[:, c, :], gp[:, c, 0:S], w, ALU.mult, e.col("conv_b_b", c), ALU.add)
            else:
                ins = e.stt(conv[:, c, :], gp[:, c, j:j + S], w, conv[:, c, :], ALU.mult, ALU.add)
            ins.then_inc(e.sem["conv_tap"], 1)
            at[0] += 1

    def outs(bank, pair):
        k = pair
        e.link(v.tensor_copy(m.hhi[:, k, :], bank))
        e.tt(m.hlo[:, k, :], bank, m.hhi[:, k, :].bitcast(F32), ALU.subtract).then_inc(e.sem["outs_taken"], 1)
        e.q.wait_ge(e.sem["outs_taken"], e.pair)

    bias = take_view(m, E_BIAS, 8 * S, "p (h s) -> p h s", h=8)
    e.attention([("sink", 0.125, bias[:, h, :], small(m, SINK + h)) for h in (0, 4, 1, 5, 2, 6, 3, 7)], outs,
                lambda i: some_taps())
    some_taps(len(taps))
    e.q.wait_ge(e.sem["conv_tap"], len(taps))
    e.marker().then_inc(e.sem["conv_ready"], 1)
    e.q.wait_ge(e.sem["conv_ready"], e.next("conv_ready"))
    e.q.wait_ge(e.sem["mean_ready"], e.next("mean_ready"))
    for c in range(4):
        e.link(e.stt(conv[:, c, :], m.banks[7][:, 0:S], -1.0 / 512, conv[:, c, :], ALU.mult, ALU.add))
        e.link(e.tt(sq[:, c, :], conv[:, c, :], conv[:, c, :], ALU.mult))
    e.marker().then_inc(e.sem["squares_ready"], 1)
    e.q.wait_ge(e.sem["squares_ready"], e.next("squares_ready"))
    e.q.wait_ge(e.sem["std_ready"], e.next("std_ready"))
    rstd = take_view(m, E_SQ, S)
    e.link(v.reciprocal(rstd, take_view(m, E_STD, S)))
    for c in range(4):
        e.tt(conv[:, c, :], conv[:, c, :], rstd, ALU.mult).then_inc(e.sem["ln_ready"], 1)
    for c in range(4):
        e.q.wait_ge(e.sem["c_act_ready"], e.next("c_act_ready"))
        e.halves(m.hhi[:, 4 + c, :], m.hlo[:, 4 + c, :], conv[:, c, :]).then_inc(e.sem["cat_ready"], 1)
    e.lo(4)
    e.out_in()


def odd_vector(e, m):
    v = e.v
    pad = 3
    w = pad + S
    rec = take_view(m, O_REC, 8 * w, "p (h s) -> p h s", h=8)
    xc = take_view(m, O_XC, 8 * S, "p (h s) -> p h s", h=8)
    e.link(v.memset(rec[:, :, 0:pad], 0.0))
    for i in range(4):
        e.lo()
        v.tensor_copy(rec[:, 2 * i:2 * i + 2, pad:], e.vb()[:, :].rearrange("p (i s) -> p i s", i=2)).then_inc(e.sem["vbank_free"], 1)
    e.q.wait_ge(e.sem["vbank_free"], e.nv)
    n0 = e.seen.get("lru_tap", 0)
    for j in range(4):
        for h in range(8):
            wc = e.col("lru_conv_w", j * 8 + h)
            if j == 0:
                ins = e.ts(xc[:, h, :], rec[:, h, 0:S], wc, ALU.mult, e.col("lru_conv_b", h), ALU.add)
            else:
                e.q.wait_ge(e.sem["lru_tap"], j * 8 + h - 7)
                ins = e.stt(xc[:, h, :], rec[:, h, j:j + S], wc, xc[:, h, :], ALU.mult, ALU.add)
            ins.then_inc(e.sem["lru_tap"], 1)
    e.q.wait_ge(e.sem["lru_tap"], 32)
    for _ in range(4):
        e.lo()
        e.q.wait_ge(e.sem["gate_ready"], e.next("gate_ready"))
    for h in range(8):
        e.halves(m.hhi[:, h, :], m.hlo[:, h, :], xc[:, h, :]).then_inc(e.sem["xc_ready"], 1)
    e.lo()
    r = take_view(m, O_R, 8 * S, "p (h s) -> p h s", h=8)
    i_ = take_view(m, O_REC, 8 * S, "p (h s) -> p h s", h=8)
    gate = take_view(m, O_GATE, 8 * S, "p (h s) -> p h s", h=8)
    e.q.wait_ge(e.sem["ri_ready"], e.next("ri_ready", 8))
    for h in range(8):
        e.tt(xc[:, h, :], xc[:, h, :], i_[:, h, :], ALU.mult).then_inc(e.sem["ix_ready"], 1)
    e.q.wait_ge(e.sem["ix_ready"], e.next("ix_ready", 8))
    for h in range(8):
        e.q.wait_ge(e.sem["a_ready"], e.next("a_ready"))
        tmp = take_view(m, TMP2, S)
        e.link(e.tt(tmp, r[:, h, :], r[:, h, :], ALU.mult))
        e.stt(i_[:, h, :], tmp, 1.0, i_[:, h, :], ALU.add, ALU.mult).then_inc(e.sem["b2_ready"], 1)
        e.q.wait_ge(e.sem["b2_ready"], e.next("b2_ready"))
    for h in range(8):
        e.q.wait_ge(e.sem["b_ready"], e.next("b_ready"))
        e.link(e.tt(xc[:, h, :], xc[:, h, :], i_[:, h, :], ALU.mult))
        e.link(v.tensor_tensor_scan(i_[:, h, :], r[:, h, :], xc[:, h, :], 0.0, ALU.mult, ALU.add))
        e.link(e.tt(gate[:, h, :], gate[:, h, :], i_[:, h, :], ALU.mult))
        e.halves(m.hhi[:, h, :], m.hlo[:, h, :], gate[:, h, :]).then_inc(e.sem["cat_ready"], 1)
    e.lo(4)
    e.out_in()


def mix_vector(e, m, layer):
    v = e.v
    lat = take_view(m, M_QKT, 1024)
    sq = take_view(m, SCORES, 3 * S)
    e.lo()
    v.tensor_copy(lat[:, 0:512], e.vb()[:, :]).then_inc(e.sem["vbank_free"], 1)
    e.lo()
    v.tensor_copy(lat[:, 512:832], e.vb()[:, 0:320]).then_inc(e.sem["vbank_free"], 1)
    e.q.wait_ge(e.sem["vbank_free"], e.nv)
    e.tt(sq, lat[:, 0:768], lat[:, 0:768], ALU.mult).then_inc(e.sem["squares_ready"], 1)
    kpe = lat[:, 768:832].rearrange("p (t f) -> p t f", t=NT)
    cos, sin = m.rope[:, 0, :, :], m.rope[:, 1, :, :]
    tmp = [take_view(m, M_OT + 128 * i, 128) for i in range(4)]
    small_tmp = [t[:, 0:32].rearrange("p (t f) -> p t f", t=NT) for t in tmp]
    rope(e, kpe[:, :, 0:16], kpe[:, :, 16:32], cos, sin, small_tmp)
    for i in range(3):
        if i == 1:
            e.lo(2)
        v.tensor_copy(take_view(m, M_SB + 512 * i, 512), e.vb()[:, :]).then_inc(e.sem["vbank_free"], 1)
    e.q.wait_ge(e.sem["vbank_free"], e.nv)
    e.marker().then_inc(e.sem["stick_in"], 1)
    e.q.wait_ge(e.sem["stick_in"], e.next("stick_in"))
    e.q.wait_ge(e.sem["std_ready"], e.next("std_ready"))
    std = take_view(m, PROBT, 512)
    e.link(v.reciprocal(std, std))
    for i in range(3):
        t = lat[:, i * S:(i + 1) * S]
        gain = e.col("mla_q_norm_2", 2 * layer + i) if i < 2 else e.col("mla_kv_norm_2", layer)
        e.stt(t, t, gain, std[:, (i // 2) * S:(i // 2 + 1) * S], ALU.mult, ALU.mult).then_inc(e.sem["own_vector"], 1)
    e.q.wait_ge(e.sem["own_vector"], e.next("own_vector", 3))
    for i in range(3):
        v.tensor_copy(m.ahi[:, i, :], lat[:, i * S:(i + 1) * S]).then_inc(e.sem["own_vector"], 1)
    e.q.wait_ge(e.sem["own_vector"], e.next("own_vector", 3))
    for i in range(3):
        e.tt(m.alo[:, i, :], lat[:, i * S:(i + 1) * S], m.ahi[:, i, :].bitcast(F32), ALU.subtract).then_inc(e.sem["own_vector"], 1)
    e.q.wait_ge(e.sem["own_vector"], e.next("own_vector", 3))
    e.marker().then_inc(e.sem["latents_ready"], 1)
    e.q.wait_ge(e.sem["latents_ready"], e.next("latents_ready"))
    for h in range(4):
        e.q.wait_ge(e.sem["scores_ready"], e.next("scores_ready"))
        e.ts(take_view(m, STICK_Z + h * TOEP, TOEP), m.banks[(4, 5, 7, 6)[h]][:, 0:TOEP], 0.125, ALU.mult).then_inc(e.sem["z_ready"], 1)
    e.q.wait_ge(e.sem["z_ready"], e.next("z_ready", 4))
    q_tok = take_view(m, M_QTOK, NT * 768, "p (t h d) -> p t h d", t=NT, h=8)
    k_tok = take_view(m, M_KTOK, NT * 768, "p (t h d) -> p t h d", t=NT, h=8)
    v_tok = take_view(m, M_VTOK, NT * 512, "p (t h d) -> p t h d", t=NT, h=8)
    for t in range(NT):
        for half in range(2):
            v.tensor_copy(q_tok[:, t, 4 * half:4 * half + 4, :],
                          e.vb()[:, 0:384].rearrange("p (h d) -> p h d", h=4)).then_inc(e.sem["vbank_free"], 1)
    e.lo(2)
    for t in range(NT):
        for half in range(2):
            kv = e.vb()[:, :].rearrange("p (h d) -> p h d", h=4)
            hs = slice(4 * half, 4 * half + 4)
            v.tensor_copy(k_tok[:, t, hs, 0:64], kv[:, :, 0:64]).then_inc(e.sem["own_vector"], 1)
            v.tensor_copy(v_tok[:, t, hs, :], kv[:, :, 64:128]).then_inc(e.sem["vbank_free"], 1)
    for t in range(NT):
        v.tensor_copy(k_tok[:, t, :, 64:96], kpe[:, t:t + 1, :].to_broadcast([P, 8, 32])).then_inc(e.sem["own_vector"], 1)
    e.q.wait_ge(e.sem["own_vector"], e.next("own_vector", 6))
    e.q.wait_ge(e.sem["vbank_free"], e.nv)
    e.stick()
    e.lo()
    for t in range(NT):
        tmp8 = [x[:, 0:128].rearrange("p (h f) -> p h f", h=8) for x in tmp]
        wide = [x[:, t:t + 1, :].to_broadcast([P, 8, 16]) for x in (cos, sin)]
        rope(e, q_tok[:, t, :, 64:80], q_tok[:, t, :, 80:96], *wide, tmp8)
    e.stick_masked()
    e.q.wait_ge(e.sem["qk_gain"], e.next("qk_gain", 32))
    heads = [take_view(m, at, 1536, "p (h d) -> p h d", d=96) for at in (M_QTOK, M_KTOK)]
    for pair in range(2):
        e.q.wait_ge(e.sem["outs_ready"], e.next("outs_ready"))
        v.tensor_copy(take_view(m, M_OT + pair * S, S), m.banks[6 + pair][:, 0:S]).then_inc(e.sem["outs_taken"], 1)
    e.pair += 2
    e.turned += 4
    e.q.wait_ge(e.sem["outs_taken"], e.pair)
    sb = take_view(m, M_OT, 2 * S)
    e.tt(take_view(m, SCORES, 2 * S), sb, sb, ALU.mult).then_inc(e.sem["squares_ready"], 1)
    for i, at in enumerate((M_QTOK, M_KTOK)):
        flat, scratch = take_view(m, at, 1536), take_view(m, M_SQ, 1536)
        e.link(e.tt(scratch, flat, flat, ALU.mult))
        e.link(v.reduce_sum(small(m, SSQ + 16 * i, 16), scratch.rearrange("p (h d) -> p h d", d=96), AX.X))
    e.marker().then_inc(e.sem["qk_sums"], 1)
    e.q.wait_ge(e.sem["qk_sums"], e.next("qk_sums"))
    for i in range(2):
        e.link(e.tt(heads[i], heads[i], m.qkgain[:, i:i + 1, :].to_broadcast([P, 16, 96]), ALU.mult))
    e.q.wait_ge(e.sem["std_ready"], e.next("std_ready"))
    e.link(v.reciprocal(small(m, RSQ, 32), small(m, RSQ, 32)))
    for i in range(2):
        e.tt(heads[i], heads[i], small(m, RSQ + 16 * i, 16).unsqueeze(2).to_broadcast([P, 16, 96]), ALU.mult).then_inc(e.sem["normed_qk"], 1)
    e.q.wait_ge(e.sem["normed_qk"], e.next("normed_qk", 2))
    e.q.wait_ge(e.sem["std_ready"], e.next("std_ready"))
    std = take_view(m, SCORES + 2 * S, S)
    e.link(v.reciprocal(std, std))
    for k in range(2):
        t = take_view(m, M_OT + k * S, S)
        e.stt(t, t, e.col("group_out_norm_2", 8 * layer + k), std, ALU.mult, ALU.mult).then_inc(e.sem["own_vector"], 1)
    e.q.wait_ge(e.sem["own_vector"], e.next("own_vector", 2))
    e.q.wait_ge(e.sem["qk_turned"], e.next("qk_turned", 4))
    for i in range(3):
        v.tensor_copy(take_view(m, M_CK + 512 * i, 512), e.vb()[:, :]).then_inc(e.sem["vbank_free"], 1)
    e.q.wait_ge(e.sem["vbank_free"], e.nv)
    e.seen["qk_turned"] += 4
    ck = take_view(m, M_CK, 1024)
    e.tt(take_view(m, M_SQ, 1024), ck, ck, ALU.mult).then_inc(e.sem["squares_ready"], 1)
    e.q.wait_ge(e.sem["bias_loaded"], e.next("bias_loaded", 16))
    bias = take_view(m, M_BIAS, 4 * S, "p (h s) -> p h s", h=4)
    e.link(v.memset(bias[0:64, :, P + 64:2 * P], NEG))
    for k in range(2):
        e.halves(m.hhi[:, k, :], m.hlo[:, k, :], take_view(m, M_OT + k * S, S)).then_inc(e.sem["cat_ready"], 1)

    def band():
        for i, name in enumerate(("ck_q_qknorm_2", "ck_k_qknorm_2")):
            s, t = take_view(m, M_SQ + i * 512, 512), ck[:, i * 512:(i + 1) * 512]
            e.q.wait_ge(e.sem["std_ready"], e.next("std_ready"))
            e.link(v.reciprocal(s, s))
            e.link(e.stt(t, t, e.col(name, layer), s, ALU.mult, ALU.mult))
        e.marker().then_inc(e.sem["band_ready"], 1)
        e.q.wait_ge(e.sem["band_ready"], e.next("band_ready"))

    done = set()

    def fill(i):
        if i == 0 and not done:
            done.add("band")
            band()
        elif i >= 3 and len(e.ahead) and i % 2:
            e.lo(e.ahead.pop())

    def outs(bank, pair):
        v.tensor_copy(take_view(m, M_OT + (2 + pair) * S, S), bank).then_inc(e.sem["outs_taken"], 1)
        e.q.wait_ge(e.sem["outs_taken"], e.pair)

    e.ahead = [1, 1, 1]
    e.attention([("direct", float(96 ** -0.5), None, None)] * 8 +
                [("band", 0.125, bias[:, h, :], None) for h in range(4)], outs, fill)
    ot = take_view(m, M_OT, 8 * S, "p (k s) -> p k s", k=8)
    others = take_view(m, M_OT + 2 * S, 6 * S)
    e.tt(take_view(m, M_QKT, 6 * S), others, others, ALU.mult).then_inc(e.sem["squares_ready"], 1)
    e.q.wait_ge(e.sem["std_ready"], e.next("std_ready"))
    std = take_view(m, M_QTOK, 2 * S)
    e.link(v.reciprocal(std, std))
    for k in range(2, 8):
        g = 0 if k < 6 else 1
        e.link(e.stt(ot[:, k, :], ot[:, k, :], e.col("group_out_norm_2", 8 * layer + k), std[:, g * S:(g + 1) * S],
                     ALU.mult, ALU.mult))
        e.halves(m.hhi[:, k, :], m.hlo[:, k, :], ot[:, k, :]).then_inc(e.sem["cat_ready"], 1)
    e.lo(4)
    e.q.wait_ge(e.sem["gain_ready"], e.next("gain_ready", 2))
    e.out_in(take_view(m, GAIN_AT, D))


def rope(e, x1, x2, cos, sin, tmp):
    e.link(e.tt(tmp[0], x1, cos, ALU.mult))
    e.link(e.tt(tmp[1], x2, sin, ALU.mult))
    e.link(e.tt(tmp[2], x2, cos, ALU.mult))
    e.link(e.tt(tmp[3], x1, sin, ALU.mult))
    e.link(e.tt(x1, tmp[0], tmp[1], ALU.subtract))
    e.link(e.tt(x2, tmp[2], tmp[3], ALU.add))



NAMES = ['x', 'norm_ffn1', 'ffn1_wg', 'ffn1_wu', 'ffn1_wd', 'norm_mix', 'norm_ffn2', 'ffn2_wg', 'ffn2_wu', 'ffn2_wd',
         'rel_bias', 'even_w_in', 'attn_sinks', 'conv_b_w', 'conv_b_b', 'conv_ln_g', 'conv_ln_b', 'even_w_out',
         'odd_w_in', 'lru_conv_w', 'lru_conv_b', 'gate_a_w', 'gate_a_b', 'gate_x_w', 'gate_x_b', 'lru_lambda',
         'odd_w_out', 'norm_final', 'c_2', 'positions_2', 'ada_w_2', 'ada_b_2', 'norm_mix_2', 'norm_ffn_2', 'w_in_2',
         'mla_q_norm_2', 'w_q_up_2', 'mla_kv_norm_2', 'w_kv_up_2', 'mla_q_qknorm_2', 'mla_k_qknorm_2',
         'ck_q_qknorm_2', 'ck_k_qknorm_2', 'ck_rel_bias_2', 'group_out_norm_2', 'w_out_2', 'ffn_w_gate_2',
         'ffn_w_up_2', 'ffn_w_down_2', 'moe_router_2', 'moe_w_gate_2', 'moe_w_up_2', 'moe_w_down_2']


def shape_constants():
    distance = LOOK - np.arange(TOEP)
    n = np.maximum(distance, 0)
    nf = np.maximum(n, 16).astype(np.float32)
    large = 16 + (np.log(nf / np.float32(16)) / np.float32(np.log(128 / 16)) * np.float32(16)).astype(np.int32)
    bucket = np.where(n < 16, n, np.minimum(large, 31))
    bucket = np.where((distance >= 0) & (distance < 128), bucket, 32)
    onehot = (np.arange(33)[:, None] == bucket[None, :]).astype(np.float32)
    inv_freq = np.float32(10000.0) ** (-np.arange(0, 32, 2, dtype=np.float32) / np.float32(32))
    chunk_rows = np.zeros((2, 2, S // 64, 64), np.float32)
    for i in range(2):
        chunk_rows[i, 0, 2 * i] = 1.0
        chunk_rows[i, 1, 2 * i + 1] = NEG
    return {"chunk_rows": chunk_rows.reshape(2, 2 * S), "bucket_onehot": onehot, "inv_freq": inv_freq.astype(np.float32)[None, :]}


def kernel(**inputs):
    import concourse.bacc as bacc
    from concourse.bass_utils import run_bass_kernel_spmd

    nc = bacc.Bacc("TRN2", target_bir_lowering=False, num_devices=1)
    arrays, aps = {}, {}
    given = {name: np.ascontiguousarray(inputs[name]) for name in NAMES}
    constants = shape_constants()
    for name, array in [*given.items(), *constants.items()]:
        arrays[name + "_dram"] = array
        aps[name] = nc.dram_tensor(name + "_dram", array.shape, mybir.dt.from_np(array.dtype),
                                   kind="ExternalInput").ap()
    out = nc.dram_tensor("out_dram", (1, S, D), F32, kind="ExternalOutput").ap()
    build(nc, aps, out, {name: aps[name] for name in constants})
    result = run_bass_kernel_spmd(nc, [arrays], core_ids=[0])
    return result.results[0]["out_dram"]
```
